# Optimizing a Trainium2 kernel written in Bass

```python
import jax, jax.numpy as jnp
from jax import lax
import numpy as np

D_MODEL = 1024
BATCH = 1
SEQ = 512
DEPTH = 1
DEC_BATCH = 1
DEC_SEQ = 32
PAST_LEN = 512

CHUNK = 64
EPS = 1e-6
GLA_HEADS = 4
GLA_DK = 128
GLA_DV = 256
GLA_RANK = 16
GLA_TAU = 16.0
SWA_HEADS = 16
SWA_KV_HEADS = 2
SWA_HD = 64
SWA_GROUP = SWA_HEADS // SWA_KV_HEADS
WINDOW = 128
WIN_CHUNKS = WINDOW // CHUNK
D_FF = 2816

GLA_QK_W = GLA_HEADS * GLA_DK
GLA_V_W = GLA_HEADS * GLA_DV
SWA_Q_W = SWA_HEADS * SWA_HD
SWA_KV_W = SWA_KV_HEADS * SWA_HD
SPLITS = (GLA_QK_W, GLA_QK_W, GLA_V_W, GLA_V_W, GLA_RANK,
          SWA_Q_W, SWA_KV_W, SWA_KV_W, D_MODEL, D_MODEL)
IN_W = sum(SPLITS)

kernel_name = "hybrid_gla_swa_macaron_stream_step"

def rmsnorm(x, g):
    xf = x.astype(jnp.float32)
    y = xf * lax.rsqrt(jnp.mean(xf * xf, axis=-1, keepdims=True) + EPS)
    return (y * g.astype(jnp.float32)).astype(x.dtype)

def half_swiglu(x, norm_g, w_in, w_out):
    h = rmsnorm(x, norm_g)
    gate, up = jnp.split(h @ w_in, 2, axis=-1)
    return x + 0.5 * ((jax.nn.silu(gate) * up) @ w_out)

def in_projection(h, w_in):
    idx, off = [], 0
    for s in SPLITS[:-1]:
        off += s
        idx.append(off)
    return jnp.split(h @ w_in, idx, axis=-1)

def gla_features(q, k, v, glr, w_gate_up, b_gate):
    B, T, _ = q.shape
    def heads(a, d):
        return a.reshape(B, T, GLA_HEADS, d).transpose(0, 2, 1, 3)
    q = heads(q, GLA_DK) * (GLA_DK ** -0.5)
    k = heads(k, GLA_DK)
    v = heads(v, GLA_DV)
    logit = (glr @ w_gate_up + b_gate).astype(jnp.float32)
    log_alpha = heads(jax.nn.log_sigmoid(logit) / GLA_TAU, GLA_DK)
    return q, k, v, log_alpha

def gla_block(S, q, k, v, la):
    q, k, v = (a.astype(jnp.float32) for a in (q, k, v))
    L = q.shape[2]
    b = jnp.cumsum(la, axis=2)
    causal = jnp.arange(L)[:, None] >= jnp.arange(L)[None, :]
    diff = b[:, :, :, None, :] - b[:, :, None, :, :]
    decay = jnp.exp(jnp.where(causal[None, None, :, :, None], diff, -jnp.inf))
    A = jnp.einsum('bhtd,bhsd,bhtsd->bhts', q, k, decay)
    o = A @ v + jnp.einsum('bhtd,bhde->bhte', q * jnp.exp(b), S)
    bL = b[:, :, -1:, :]
    S_new = jnp.exp(bL[:, :, 0, :])[..., None] * S + \
        jnp.einsum('bhsd,bhse->bhde', k * jnp.exp(bL - b), v)
    return S_new, o

def gla_prompt(q, k, v, la):
    B, H, S, _ = q.shape
    nc = S // CHUNK
    def blocks(a):
        return a.reshape(B, H, nc, CHUNK, a.shape[-1]).transpose(2, 0, 1, 3, 4)
    S0 = jnp.zeros((B, H, GLA_DK, GLA_DV), jnp.float32)
    S_fin, o = lax.scan(lambda s, c: gla_block(s, *c), S0,
                        (blocks(q), blocks(k), blocks(v), blocks(la)))
    o = o.transpose(1, 2, 0, 3, 4).reshape(B, H, S, GLA_DV)
    return o, S_fin

def sink_softmax(s, sinks):
    sk = sinks.astype(jnp.float32).reshape(SWA_KV_HEADS, SWA_GROUP)[:, :, None, None]
    m = jnp.maximum(jnp.max(s, axis=-1, keepdims=True), sk)
    p = jnp.exp(s - m)
    return p / (jnp.sum(p, axis=-1, keepdims=True) + jnp.exp(sk - m))

def swa_prompt(q, k, v, sinks):
    B, S, _ = q.shape
    nc = S // CHUNK
    nk = (WIN_CHUNKS + 1) * CHUNK
    pad = WIN_CHUNKS * CHUNK
    q = q.reshape(B, nc, CHUNK, SWA_KV_HEADS, SWA_GROUP, SWA_HD)
    k = k.reshape(B, S, SWA_KV_HEADS, SWA_HD)
    v = v.reshape(B, S, SWA_KV_HEADS, SWA_HD)
    def band(a):
        ap = jnp.pad(a, ((0, 0), (pad, 0), (0, 0), (0, 0)))
        ap = ap.reshape(B, nc + WIN_CHUNKS, CHUNK, SWA_KV_HEADS, SWA_HD)
        return jnp.concatenate([ap[:, i:i + nc] for i in range(WIN_CHUNKS + 1)], axis=2)
    kb, vb = band(k), band(v)
    key_pos = (jnp.arange(nc) * CHUNK)[:, None] - pad + jnp.arange(nk)[None, :]
    valid = key_pos >= 0
    s = jnp.einsum('bcqkgd,bcjkd->bckgqj', q, kb).astype(jnp.float32) * (SWA_HD ** -0.5)
    s = jnp.where(valid[None, :, None, None, None, :], s, -jnp.inf)
    p = sink_softmax(s, sinks)
    o = jnp.einsum('bckgqj,bcjkd->bcqkgd', p.astype(vb.dtype), vb).reshape(B, S, SWA_Q_W)
    return o, k[:, -WINDOW:], v[:, -WINDOW:]

def swa_sample(q, k, v, sinks, cache_k, cache_v):
    B, T, _ = q.shape
    q = q.reshape(B, T, SWA_KV_HEADS, SWA_GROUP, SWA_HD)
    k_all = jnp.concatenate([cache_k.astype(k.dtype), k.reshape(B, T, SWA_KV_HEADS, SWA_HD)], axis=1)
    v_all = jnp.concatenate([cache_v.astype(v.dtype), v.reshape(B, T, SWA_KV_HEADS, SWA_HD)], axis=1)
    s = jnp.einsum('bqkgd,bjkd->bkgqj', q, k_all).astype(jnp.float32) * (SWA_HD ** -0.5)
    p = sink_softmax(s, sinks)
    o = jnp.einsum('bkgqj,bjkd->bqkgd', p.astype(v_all.dtype), v_all).reshape(B, T, SWA_Q_W)
    n = cache_k.shape[1]
    return o, k_all[:, -n:], v_all[:, -n:]

def token_mixing(x, norm_g, w_in, w_gate_up, b_gate, gla_norm_g, sinks,
                 w_br_gla, w_br_swa, w_out, state_gla=None, cache_k=None, cache_v=None):
    B, T, _ = x.shape
    h = rmsnorm(x, norm_g)
    gq, gk, gv, gr, glr, sq, sk, sv, gate_gla, gate_swa = in_projection(h, w_in)
    q, k, v, la = gla_features(gq, gk, gv, glr, w_gate_up, b_gate)
    if state_gla is None:
        o_gla, s_gla = gla_prompt(q, k, v, la)
    else:
        s_gla, o_gla = gla_block(state_gla.astype(jnp.float32), q, k, v, la)
    o_gla = rmsnorm(o_gla, gla_norm_g).astype(h.dtype)
    o_gla = o_gla.transpose(0, 2, 1, 3).reshape(B, T, GLA_V_W) * jax.nn.silu(gr)
    if cache_k is None:
        o_swa, k_keep, v_keep = swa_prompt(sq, sk, sv, sinks)
    else:
        o_swa, k_keep, v_keep = swa_sample(sq, sk, sv, sinks, cache_k, cache_v)
    merged = jax.nn.sigmoid(gate_gla) * (o_gla @ w_br_gla) + jax.nn.sigmoid(gate_swa) * (o_swa @ w_br_swa)
    return x + merged @ w_out, s_gla, k_keep, v_keep

def macaron_layer(x, ffn1, mix, ffn2, state_gla=None, cache_k=None, cache_v=None):
    x = half_swiglu(x, *ffn1)
    x, s_gla, k_keep, v_keep = token_mixing(x, *mix, state_gla=state_gla, cache_k=cache_k, cache_v=cache_v)
    x = half_swiglu(x, *ffn2)
    return x, s_gla, k_keep, v_keep

def setup_inputs(seed: int = 0) -> dict:
    key = jax.random.key(seed)
    ks = jax.random.split(key, 24)
    f32 = jnp.float32
    def nrm(k, shape, scale):
        return jax.random.normal(k, shape, f32) * scale
    L = DEPTH
    return {
        "x_prompt": nrm(ks[0], (BATCH, SEQ, D_MODEL), 1.0),
        "x_sample": nrm(ks[1], (DEC_BATCH, DEC_SEQ, D_MODEL), 1.0),
        "state_gla": nrm(ks[2], (L, DEC_BATCH, GLA_HEADS, GLA_DK, GLA_DV), 1.0),
        "cache_swa_k": nrm(ks[3], (L, DEC_BATCH, WINDOW, SWA_KV_HEADS, SWA_HD), 1.0),
        "cache_swa_v": nrm(ks[4], (L, DEC_BATCH, WINDOW, SWA_KV_HEADS, SWA_HD), 1.0),
        "norm_ffn1": 1.0 + nrm(ks[5], (L, D_MODEL), 0.02),
        "w_ffn1_in": nrm(ks[6], (L, D_MODEL, 2 * D_FF), D_MODEL ** -0.5),
        "w_ffn1_out": nrm(ks[7], (L, D_FF, D_MODEL), D_FF ** -0.5),
        "norm_mix": 1.0 + nrm(ks[8], (L, D_MODEL), 0.02),
        "w_in": nrm(ks[9], (L, D_MODEL, IN_W), D_MODEL ** -0.5),
        "w_gla_gate_up": nrm(ks[10], (L, GLA_RANK, GLA_QK_W), GLA_RANK ** -0.5),
        "b_gla_gate": nrm(ks[11], (L, GLA_QK_W), 0.1),
        "gla_norm": 1.0 + nrm(ks[12], (L, GLA_DV), 0.02),
        "swa_sinks": nrm(ks[13], (L, SWA_HEADS), 0.5),
        "w_branch_gla": nrm(ks[14], (L, GLA_V_W, D_MODEL), GLA_V_W ** -0.5),
        "w_branch_swa": nrm(ks[15], (L, SWA_Q_W, D_MODEL), SWA_Q_W ** -0.5),
        "w_out": nrm(ks[16], (L, D_MODEL, D_MODEL), D_MODEL ** -0.5),
        "norm_ffn2": 1.0 + nrm(ks[17], (L, D_MODEL), 0.02),
        "w_ffn2_in": nrm(ks[18], (L, D_MODEL, 2 * D_FF), D_MODEL ** -0.5),
        "w_ffn2_out": nrm(ks[19], (L, D_FF, D_MODEL), D_FF ** -0.5),
        "norm_final": 1.0 + nrm(ks[20], (D_MODEL,), 0.02),
    }

def reference(x_prompt, x_sample, state_gla, cache_swa_k, cache_swa_v,
              norm_ffn1, w_ffn1_in, w_ffn1_out, norm_mix, w_in, w_gla_gate_up, b_gla_gate,
              gla_norm, swa_sinks, w_branch_gla, w_branch_swa, w_out,
              norm_ffn2, w_ffn2_in, w_ffn2_out, norm_final):
    yp, ys = x_prompt, x_sample
    sg_p, sk_p, sv_p, sg_s, sk_s, sv_s = [], [], [], [], [], []
    for l in range(DEPTH):
        ffn1 = (norm_ffn1[l], w_ffn1_in[l], w_ffn1_out[l])
        mix = (norm_mix[l], w_in[l], w_gla_gate_up[l], b_gla_gate[l], gla_norm[l], swa_sinks[l],
               w_branch_gla[l], w_branch_swa[l], w_out[l])
        ffn2 = (norm_ffn2[l], w_ffn2_in[l], w_ffn2_out[l])
        yp, g_p, k_p, v_p = macaron_layer(yp, ffn1, mix, ffn2)
        ys, g_s, k_s, v_s = macaron_layer(ys, ffn1, mix, ffn2, state_gla[l], cache_swa_k[l], cache_swa_v[l])
        sg_p.append(g_p); sk_p.append(k_p); sv_p.append(v_p)
        sg_s.append(g_s); sk_s.append(k_s); sv_s.append(v_s)
    y_prompt = rmsnorm(yp, norm_final)
    y_sample = rmsnorm(ys, norm_final)
    return (y_prompt, y_sample,
            jnp.stack(sg_p), jnp.stack(sk_p), jnp.stack(sv_p),
            jnp.stack(sg_s), jnp.stack(sk_s), jnp.stack(sv_s))


_drawn_inputs = setup_inputs


def setup_inputs(seed=0):
    import zlib

    import numpy as np

    out = dict(_drawn_inputs(seed))
    spreads = {}
    factors = {'norm_ffn1': 4.602,
     'gla_norm': 53.244,
     'swa_sinks': 200.0,
     'norm_ffn2': 20.745,
     'norm_final': 25.809,
     'w_branch_swa': 20.127}
    for name, (base, spread) in spreads.items():
        noise = np.random.default_rng([zlib.crc32(name.encode()), seed]).standard_normal(out[name].shape)
        drawn = base * np.exp(spread * noise) if base else spread * noise
        out[name] = __import__('jax').numpy.asarray(drawn.astype(out[name].dtype))
    for name, factor in factors.items():
        out[name] = (out[name] * factor).astype(out[name].dtype)
    return out
```

```python
from contextlib import ExitStack

import concourse.bass as bass
from concourse import mybir
import numpy as np

ALU = mybir.AluOpType
ACT = mybir.ActivationFunctionType
F32 = mybir.dt.float32
F32R = mybir.dt.float32r
U32 = mybir.dt.uint32
AX_X = mybir.AxisListType.X

P = 128
D = 1024
NP, NS = 512, 32
T = NP + NS
TH = T // 2
KD = D // P
DFF = 2816
KF = DFF // P
TB = NP // P
EPS = 1e-6

GH, GDK, GDV, GRANK = 4, 128, 256, 16
GTAU = 16.0
SH, SKV, SHD, WIN, CHUNK = 16, 2, 64, 128, 64
SG = SH // SKV
NLV = 7

C_GQ, C_GK, C_GV, C_GR, C_GLR = 0, 512, 1024, 2048, 3072
C_SQ, C_SK, C_SV, C_GA, C_GB = 3088, 4112, 4240, 4368, 5392

UW = KD * P
FO_SPLIT = ((0, 6), (6, 6), (12, 5), (17, 5))

G_FFN1, G_MIX, G_FFN2, G_FIN, G_BG, G_GLA = 0, 8, 16, 24, 32, 36
NG = 38

K_ID, K_ONE, K_LM = 0, P, 2 * P
K_BAND = K_LM + NLV * 64
K_RST = K_BAND + 2 * P
K_EPS = K_RST + T
NK = K_EPS + 2
MASKED = -1e30
N_TRD = 2 * KD + 2
N_HT = 3 * KD


def constants():
    c = np.zeros((P, NK), np.float32)
    s = np.arange(P)[:, None]
    c[:, K_ID:K_ID + P] = np.eye(P)
    c[:, K_ONE:K_ONE + P] = 1.0
    for lv in range(NLV):
        span = P >> lv
        half = span // 2
        col = np.arange(64)[None, :]
        c[:, K_LM + 64 * lv:K_LM + 64 * lv + 64] = (s // span == col // half) & (s % span < half)
    key = np.arange(2 * P)[None, :]
    chunk = s // CHUNK
    seen = (key // CHUNK >= chunk) & (key // CHUNK <= chunk + WIN // CHUNK)
    c[:, K_BAND:K_BAND + 2 * P] = np.where(seen, 0.0, MASKED)
    c[:, K_RST:K_RST + T] = (np.arange(T) % P != 0)[None, :]
    c[:, K_EPS] = EPS
    c[:, K_EPS + 1] = 1.0
    return c


class Tally:

    def __init__(self, sem):
        self.sem, self.base, self.local, self.turn, self.per = sem, 0, 0, None, 0

    def add(self, n=1):
        self.local += n
        return self.value()

    def value(self):
        v = self.base + self.local
        return v if self.turn is None else self.turn * self.per + v


class Loop:

    def __init__(self, eng, count, *counted):
        self.eng, self.count, self.counted = eng, count, counted

    def __enter__(self):
        self.fori = self.eng.Fori(0, self.count)
        i = self.fori.__enter__()
        for tally, per in self.counted:
            tally.base += tally.local
            tally.local, tally.turn, tally.per = 0, i, per
        return i

    def __exit__(self, kind, *exc):
        self.fori.__exit__(kind, *exc)
        if kind is None:
            for tally, per in self.counted:
                assert tally.local == per, (tally.sem, tally.local, per)
                tally.base += self.count * per
                tally.local, tally.turn = 0, None


def build(nc, a, outs):
    (x_prompt, x_sample, state_gla, cache_k, cache_v, norm_ffn1, w_f1i, w_f1o, norm_mix, w_in, w_gup, b_gate,
     gla_norm, sinks, w_bgla, w_bswa, w_out, norm_ffn2, w_f2i, w_f2o, norm_final, table) = a
    y_p, y_s, sg_p, ck_p, cv_p, sg_s, ck_s, cv_s = outs

    with ExitStack() as ctx:
        at = [(nc.sbuf_base + 63) // 64 * 64]

        def place(name, shape, dt=F32, offset=None):
            size = (int(np.prod(shape[1:])) * 4 + 31) // 32 * 32
            if offset is None:
                offset = at[0]
                at[0] += size
            return nc.alloc_sbuf_tensor_at(name, shape, dt, offset=offset)

        def sem(name):
            return ctx.enter_context(nc.semaphore(name))

        ROW = T * 4
        xT = place("xT", [P, KD, T])
        hH = place("hH", [P, KD, T], F32R)
        hL = place("hL", [P, KD, T], F32R)
        R = at[0]
        at[0] += 48 * ROW
        raw = place("raw", [P, 4, UW])
        wH = place("wH", [P, 4, UW], F32R)
        wL = place("wL", [P, 4, UW], F32R)
        N = at[0]
        sq = place("sq", [P, T])
        acc = place("acc", [P, T])
        rstd = place("rstd", [P, T])
        tab = place("tab", [P, NK])
        gains = place("gains", [P, 40])
        small = place("small", [P, 128])
        state = place("state", [P, GH, GDV])
        assert at[0] <= nc.sbuf_usable_end, (at[0], nc.sbuf_usable_end)

        hidH = place("hidH", [P, KF, T], F32R, R)
        hidL = place("hidL", [P, KF, T], F32R, R + KF * ROW)
        ft = place("ft", [P, T], F32, R + 44 * ROW)
        fs = place("fs", [P, T], F32, R + 45 * ROW)
        fp = place("fp", [P, T], F32, R + 46 * ROW)
        ht = place("ht", [P, 2, T], F32, R + 46 * ROW)
        xtok = place("xtok", [P, TB + 1, D], F32, R)
        vrow = place("vrow", [NG, P], F32, R + 20 * ROW)
        qs = place("qs", [P, SG, T], F32, R)
        gq = place("gq", [P, GH, T], F32, R + 8 * ROW)
        gk = place("gk", [P, GH, T], F32, R + 12 * ROW)
        gb = place("gb", [P, GH, T], F32, R + 16 * ROW)
        gv = place("gv", [P, TB + 1, GH * GDV], F32, R + 20 * ROW)
        go = place("go", [P, KD, T], F32, R + 30 * ROW)
        M0 = R + 38 * ROW
        kT = place("kT", [P, T], F32, M0)
        vtok = place("vtok", [P, TB + 1, P], F32, M0 + ROW)
        M1 = M0 + ROW + (TB + 1) * P * 4
        glr = place("glr", [GRANK, T], F32, M1)
        gup = place("gup", [GRANK, GH * GDK], F32, M1 + ROW)
        vtmp = place("vtmp", [P, 2, T], F32, M1 + 2 * ROW)
        la1 = place("la1", [P, T], F32, M1 + 4 * ROW)
        la2 = place("la2", [P, T], F32, M1 + 5 * ROW)
        ktok = place("ktok", [P, 2, P], F32, at[0]); at[0] += 1024
        qst = place("qst", [P, SG, P], F32, M1)
        M2 = M1 + SG * P * 4
        kst = place("kst", [P, SKV, 2 * P], F32, M2)
        pts = place("pts", [P, 2, 2, 2, P], F32, M2 + 2048)
        otok = place("otok", [P, SG, P // 2], F32, M2 + 2048 + 4096)
        probs = place("probs", [P, 2, 2, 2 * P], F32, M2 + 8192)
        assert M2 + 8192 + 4096 <= M0 + 10 * ROW
        smax = place("smax", [P, 2, 2, 2 * P], F32, N)
        ckc = place("ckc", [P, P], F32, N + 4096)
        cvc = place("cvc", [P, P], F32, N + 4096 + 512)
        M3 = M0
        lev = place("lev", [P, NLV, GH, P], F32, M3)
        M4 = M3 + NLV * GH * P * 4
        qeb = place("qeb", [P, GH, P], F32, M4)
        kdec = place("kdec", [P, GH, P], F32, M4 + 2048)
        A = place("A", [P, P], F32, M4 + 4096)
        kdT = place("kdT", [P, P], F32, M4 + 4608)
        osb = place("osb", [P, GDV], F32, M4 + 5120)
        gsq = place("gsq", [P, GDV], F32, M4 + 6144)
        assert M4 + 7168 <= M0 + 10 * ROW
        qg = place("qg", [P, GH, P], F32, N)
        kg = place("kg", [P, GH, P], F32, N + 2048)
        alev = place("alev", [P, NLV, 64], F32, N + 4096)
        ogH = place("ogH", [P, KD, T], F32R, R + 8 * ROW)
        ogL = place("ogL", [P, KD, T], F32R, R + 16 * ROW)
        osH = place("osH", [P, KD, T], F32R, R + 24 * ROW)
        osL = place("osL", [P, KD, T], F32R, R + 32 * ROW)
        mH = place("mH", [P, KD, T], F32R, R)
        mL = place("mL", [P, KD, T], F32R, R + 40 * ROW)
        tA = sq
        tB = acc
        mA = rstd
        mB = place("mB", [P, T], F32, at[0]); at[0] += ROW
        assert at[0] <= nc.sbuf_usable_end, (at[0], nc.sbuf_usable_end)

        ident = tab[:, K_ID:K_ID + P]
        ones = tab[:, K_ONE:K_ONE + P]
        band = tab[:, K_BAND:K_BAND + 2 * P]
        eps = tab[:, K_EPS:K_EPS + 1]
        one = tab[:, K_EPS + 1:K_EPS + 2]
        negsink, sink = small[:, 0:16], small[:, 16:32]
        mx, nmax, den, esum = small[:, 32:48], small[:, 48:64], small[:, 64:80], small[:, 80:96]
        rden = small[:, 96:112]
        ssq, sln, srs = small[:, 112:113], small[:, 113:114], small[:, 114:115]
        sgain = small[:, 116:118]
        eL = small[:, 120:124]

        slot = [ctx.enter_context(nc.psum_tensor(f"slot{i}", [P, 2, 512], F32)) for i in range(2)]
        side = ctx.enter_context(nc.psum_tensor("side", [P, 4, 512], F32))
        slot_t = [p[:, :, :].rearrange("p a b -> p (a b)")[:, 0:T] for p in slot]
        slot_h = [p[:, :, 0:TH] for p in slot]

        def two(ap):
            return ap.rearrange("p (a b) -> p a b", a=2)

        s_table = sem("s_table")
        s_tokens = sem("s_tokens")
        s_mixin = sem("s_mixin")
        s_raw = [sem(f"s_raw{i}") for i in range(4)]
        s_wH = sem("s_wH")
        s_wL = sem("s_wL")
        s_unit = sem("s_unit")
        s_slot = sem("s_slot")
        s_tanh = sem("s_tanh")
        s_in = sem("s_in")
        s_ss = sem("s_ss")
        s_ssum = sem("s_ssum")
        s_rstd = sem("s_rstd")
        s_ht = sem("s_ht")
        s_inH = sem("s_inH")
        s_tr = sem("s_tr")
        s_trd = sem("s_trd")
        s_lg = sem("s_lg")
        s_lgx = sem("s_lgx")
        s_sp = sem("s_sp")
        s_dve = sem("s_dve")
        s_act = sem("s_act")
        s_store = sem("s_store")
        s_ktok = sem("s_ktok")
        s_qk = sem("s_qk")
        s_sc = sem("s_sc")
        s_nm = sem("s_nm")
        s_pr = sem("s_pr")
        s_pt = sem("s_pt")
        s_pts = sem("s_pts")
        s_esx = sem("s_esx")
        s_es = sem("s_es")
        s_av = sem("s_av")
        s_ot = sem("s_ot")
        s_ott = sem("s_ott")
        s_oc = sem("s_oc")
        s_cache = sem("s_cache")
        s_gd = sem("s_gd")
        s_ge = sem("s_ge")
        s_gx = sem("s_gx")
        s_ga = sem("s_ga")
        s_gA = sem("s_gA")
        s_go = sem("s_go")
        s_gs = sem("s_gs")
        s_gr = sem("s_gr")
        s_gn = sem("s_gn")
        s_gt = sem("s_gt")
        s_gf = sem("s_gf")
        s_state = sem("s_state")
        s_stout = sem("s_stout")

        U_F1I = 0
        U_F1O = U_F1I + 2 * KF
        U_MIX = U_F1O + 4 * KD
        U_SQ = U_MIX + 3
        U_GQ = U_SQ + SG
        U_GK = U_GQ + GH
        U_GV = U_GK + GH
        U_GR = U_GV + KD
        U_BR = U_GR + KD
        U_WO = U_BR + 4 * KD
        U_F2I = U_WO + KD
        U_F2O = U_F2I + 2 * KF
        U_END = U_F2O + 4 * KD

        block = ctx.enter_context(nc.Block())

        @block.sync
        def _(sp):
            sp.dma_start(tab[:, :], table).then_inc(s_table, 16)
            sp.dma_start(xtok[:, 0:TB, :], x_prompt[0].rearrange("(b p) d -> p b d", p=P)).then_inc(s_tokens, 16)
            sp.dma_start(xtok[0:NS, TB, :], x_sample[0]).then_inc(s_tokens, 16)
            for c0, v, n in ((G_FFN1, norm_ffn1[0], 8), (G_MIX, norm_mix[0], 8), (G_FFN2, norm_ffn2[0], 8),
                             (G_FIN, norm_final, 8), (G_BG, b_gate[0], 4), (G_GLA, gla_norm[0], 2)):
                sp.dma_start(vrow[c0:c0 + n, :], v.rearrange("(k p) -> k p", p=P)).then_inc(s_tokens, 16)

            def buffer(u, i=0):
                if u >= 4:
                    sp.wait_ge(s_wL, 4 * i + (u - 3))
                return raw[:, u % 4]

            def load(u, i, src, waits=True):
                k = src.shape[1]
                dst = buffer(u, i) if waits else raw[:, u % 4]
                sp.dma_start(dst[:, 0:k * P].rearrange("p (k n) -> p k n", k=k), src
                             ).then_inc(s_raw[u % 4], 32)

            def cols(w, c0, k0=0, k=KD):
                c0 = c0 if isinstance(c0, int) else sp.snap(c0)
                return w[0].rearrange("(k p) n -> p k n", p=P)[:, k0:k0 + k, bass.ds(c0, P)]

            for r in range(4):
                load(r, 0, cols(w_f1i, (r // 2) * P + (r % 2) * DFF))
            with sp.Fori(1, KF // 2) as i:
                for r in range(4):
                    src = cols(w_f1i, i * (2 * P) + (r // 2) * P + (r % 2) * DFF)
                    sp.wait_ge(s_wL, 4 * i + (r - 3))
                    sp.dma_start(raw[:, r].rearrange("p (k n) -> p k n", k=KD), src).then_inc(s_raw[r], 32)
            with sp.Fori(0, KD) as i:
                for r, (k0, k) in enumerate(FO_SPLIT):
                    load(U_F1O + r, i, cols(w_f1o, i * P, k0, k))
            for r, c0 in enumerate((C_SK, C_SV, C_GLR)):
                load(U_MIX + r, 0, cols(w_in, c0))
            sp.wait_ge(s_unit, U_F1O + 4 * KD)
            sp.dma_start(gup[:, :], w_gup[0]).then_inc(s_mixin, 16)
            sp.dma_start(rden, sinks.broadcast_to([P, SH])).then_inc(s_mixin, 16)
            with sp.Fori(0, 2) as i:
                for r in range(4):
                    srcs = [w_in[0].rearrange("(k p) n -> p k n", p=P)[:, :, bass.ds(sp.snap(
                        i * (4 * SHD) + (C_SQ + g * SG * SHD + r * SHD)), SHD)] for g in range(SKV)]
                    dst = buffer(U_SQ + r, i).rearrange("p (k g n) -> p k g n", k=KD, g=SKV)
                    for g in range(SKV):
                        sp.dma_start(dst[:, :, g], srcs[g]).then_inc(s_raw[(U_SQ + r) % 4], 16)
            for r in range(4):
                load(U_GQ + r, 0, cols(w_in, C_GQ + r * P))
            for r in range(4):
                load(U_GK + r, 0, cols(w_in, C_GK + r * P))
            for u0, c0 in ((U_GV, C_GV), (U_GR, C_GR)):
                with sp.Fori(0, 2) as i:
                    for r in range(4):
                        load(u0 + r, i, cols(w_in, i * (4 * P) + (c0 + r * P)))

            sp.wait_ge(s_ktok, 1)
            sp.dma_start(ck_p[0, 0].rearrange("t h d -> t (h d)"), ktok[:, 0, :]).then_inc(s_store, 16)
            sp.dma_start(cv_p[0, 0].rearrange("t h d -> t (h d)"), vtok[:, TB - 1, :]).then_inc(s_store, 16)
            for new, old, rows in ((ck_s, cache_k, ktok[0:NS, 1, :]), (cv_s, cache_v, vtok[0:NS, TB, :])):
                sp.dma_start(new[0, 0, WIN - NS:].rearrange("t h d -> t (h d)"), rows).then_inc(s_store, 16)
                sp.dma_start(new[0, 0, 0:WIN - NS], old[0, 0, NS:]).then_inc(s_store, 16)
            sp.dma_start(ckc[:, :], cache_k[0, 0].rearrange("t h d -> t (h d)")).then_inc(s_cache, 16)
            sp.dma_start(cvc[:, :], cache_v[0, 0].rearrange("t h d -> t (h d)")).then_inc(s_cache, 16)

            sp_first = [(0, cols(w_in, C_GA)), (1, cols(w_bgla, 0)), (2, cols(w_in, C_GB))]
            for r, src in sp_first:
                load(U_BR + r, 0, src)

            def branch_swa(i, c0):
                c0 = c0 if isinstance(c0, int) else sp.snap(c0)
                dst = buffer(U_BR + 3, i).rearrange("p (k n) -> p k n", k=KD)
                src = w_bswa[0].rearrange("(g j n) c -> g n j c", g=SKV, n=SHD)
                for g in range(SKV):
                    sp.dma_start(dst[g * SHD:(g + 1) * SHD], src[g][:, :, bass.ds(c0, P)]
                                 ).then_inc(s_raw[(U_BR + 3) % 4], 16)

            branch_swa(0, 0)
            sp.wait_ge(s_gs, GH * TB)
            sp.dma_start(sg_p[0, 0].rearrange("h d e -> d h e"), state[:, :, :]).then_inc(s_stout, 16)
            sp.wait_ge(s_stout, 16)
            sp.dma_start(state[:, :, :], state_gla[0, 0].rearrange("h d e -> d h e")).then_inc(s_state, 16)
            sp.wait_ge(s_gs, GH * TB + GH)
            sp.dma_start(sg_s[0, 0].rearrange("h d e -> d h e"), state[:, :, :]).then_inc(s_store, 16)

            with sp.Fori(1, KD) as i:
                buffer(U_BR + 1, i)
                load(U_BR, i, cols(w_in, i * P + C_GA), waits=False)
                load(U_BR + 1, i, cols(w_bgla, i * P), waits=False)
                load(U_BR + 2, i, cols(w_in, i * P + C_GB))
                branch_swa(i, i * P)
            with sp.Fori(0, 2) as i:
                for r in range(4):
                    load(U_WO + r, i, cols(w_out, i * (4 * P) + r * P))
            with sp.Fori(0, KF // 2) as i:
                for r in range(4):
                    load(U_F2I + r, i, cols(w_f2i, i * (2 * P) + (r // 2) * P + (r % 2) * DFF))
            with sp.Fori(0, KD) as i:
                for r, (k0, k) in enumerate(FO_SPLIT):
                    load(U_F2O + r, i, cols(w_f2o, i * P, k0, k))
            yt = Tally(s_trd)
            yt.add(N_TRD)
            for b in range(TB + 1):
                sp.wait_ge(s_trd, yt.add(2))
                if b < TB:
                    sp.dma_start(y_p[0, b * P:(b + 1) * P], xtok[:, b, :]).then_inc(s_store, 16)
                else:
                    sp.dma_start(y_s[0], xtok[0:NS, TB, :]).then_inc(s_store, 16)
            sp.wait_ge(s_store, 16 * (6 + 1 + TB + 1))

        @block.gpsimd
        def _(pool):
            def low(n, s):
                pool.wait_ge(s_wH, n)
                pool.tensor_tensor(wL[:, s], raw[:, s], wH[:, s].bitcast(F32), ALU.subtract).then_inc(s_wL, 1)

            with pool.Fori(0, U_END // 4) as i:
                for s in range(4):
                    low(4 * i + (s + 1), s)
            for s in range(U_END % 4):
                low(U_END // 4 * 4 + s + 1, s)

        @block.tensor
        def _(pe):
            unit, blocks = Tally(s_unit), Tally(s_slot)
            inp, ss, trd = Tally(s_in), Tally(s_ss), Tally(s_trd)

            def mm(out, lhsT, rhs, start=True, stop=True):
                return pe.matmul(out, lhsT, rhs, start=start, stop=stop, skip_group_check=True)

            def run(s, b, xH, xL, k0=0, k=KD, last=True, wait_in=None):
                pe.wait_ge(s_wL, unit.add())
                for c in range(k0, k0 + k):
                    if wait_in is not None:
                        pe.wait_ge(s_in, wait_in + c + 1)
                    w = slice((c - k0) * P, (c - k0 + 1) * P)
                    for n, (wt, x) in enumerate(((wH, xH), (wH, xL), (wL, xH))):
                        for h in range(2):
                            m = mm(slot[b][:, h, 0:TH], wt[:, s, w], x[:, c, h * TH:(h + 1) * TH],
                                   start=(c == 0 and n == 0), stop=(last and c == k0 + k - 1 and n == 2))
                m.then_inc(s_unit, 1)

            def slot_free():
                pe.wait_ge(s_slot, blocks.add() - 2)

            def ffn_in(u0, b0, in0):
                for r in range(4):
                    if b0 + u0 + r < 2:
                        blocks.add()
                    else:
                        slot_free()
                    run((u0 + r) % 4, (b0 + r) % 2, hH, hL, wait_in=in0 if r == 0 else None)
                with Loop(pe, KF // 2 - 1, (unit, 4), (blocks, 4)):
                    for r in range(4):
                        slot_free()
                        run((u0 + r) % 4, (b0 + r) % 2, hH, hL)

            def ffn_out(u0, b0, in0):
                pe.wait_ge(s_in, in0 + KF)
                with Loop(pe, KD // 2, (unit, 8), (blocks, 2)):
                    for b in range(2):
                        slot_free()
                        for r, (k0, k) in enumerate(FO_SPLIT):
                            run((u0 + r) % 4, (b0 + b) % 2, hidH, hidL, k0, k, last=(r == 3))

            def norm():
                pe.wait_ge(s_ss, ss.add())
                for h in range(2):
                    m = mm(side[:, h, 0:TH], ones, acc[:, h * TH:(h + 1) * TH])
                m.then_inc(s_ssum, 1)

            pe.wait_ge(s_table, 16)
            pe.wait_ge(s_tokens, 16 * 8)
            pe.transpose(side[:, 2, 0:NG], vrow[:, :], ident[0:NG, 0:NG]).then_inc(s_tr, 1)
            for k in range(KD):
                if k >= 2:
                    pe.wait_ge(s_trd, k)
                for b in range(TB + 1):
                    n = P if b < TB else NS
                    m = pe.transpose(slot_t[k % 2][:, b * P:b * P + n], xtok[0:n, b, k * P:(k + 1) * P],
                                     ident[0:n, 0:n])
                m.then_inc(s_tr, 1)
            norm()
            ffn_in(U_F1I, 0, 0)
            ffn_out(U_F1O, 0, KD)
            norm()

            IN = KD + KF
            for r in range(3):
                slot_free()
                run((U_MIX + r) % 4, r % 2, hH, hL, wait_in=IN if r == 0 else None)
            pe.wait_ge(s_slot, blocks.value())
            for b in range(TB + 1):
                n = P if b < TB else NS
                m = pe.transpose(side[0:n, 2 + b // TB, (b % TB) * P:(b % TB + 1) * P],
                                 vtmp[:, 0, b * P:b * P + n], ident)
            pe.transpose(side[:, 3, P:2 * P], kT[:, NP - P:NP], ident)
            pe.transpose(side[0:NS, 3, 2 * P:3 * P], kT[:, NP:T], ident).then_inc(s_tr, 1)
            with Loop(pe, 2, (unit, 4), (blocks, 4)):
                for r in range(4):
                    slot_free()
                    run((U_SQ + r) % 4, (3 + r) % 2, hH, hL)
            pe.wait_ge(s_mixin, 32)
            for r in range(GH):
                slot_free()
                run((U_GQ + r) % 4, (3 + r) % 2, hH, hL)
                if r:
                    pe.wait_ge(s_lgx, r)
                for h in range(2):
                    m = mm(side[:, h, 0:TH], gup[:, r * P:(r + 1) * P], glr[:, h * TH:(h + 1) * TH])
                m.then_inc(s_lg, 1)
            for r in range(GH):
                slot_free()
                run((U_GK + r) % 4, (3 + r) % 2, hH, hL)
            trv = Tally(s_trd)
            trv.add(KD + 2)
            with Loop(pe, 2, (unit, 4), (blocks, 4), (trv, 4)):
                for r in range(4):
                    slot_free()
                    run((U_GV + r) % 4, (3 + r) % 2, hH, hL)
                    pe.wait_ge(s_slot, blocks.value())
                    pe.wait_ge(s_trd, trv.add() - 1)
                    for b in range(TB + 1):
                        n = P if b < TB else NS
                        m = pe.transpose(side[0:n, 2 + b // TB, (b % TB) * P:(b % TB + 1) * P],
                                         vtmp[:, r % 2, b * P:b * P + n], ident)
                    m.then_inc(s_tr, 1)
            with Loop(pe, 2, (unit, 4), (blocks, 4)):
                for r in range(4):
                    slot_free()
                    run((U_GR + r) % 4, (3 + r) % 2, hH, hL)

            qk, nm, pr, pts_, ot, oc = (Tally(x) for x in (s_qk, s_nm, s_pr, s_pts, s_ot, s_oc))
            pe.wait_ge(s_trd, KD + 2 + KD)

            def swa(n, tiles, first=False):
                keys = sum(m for m, _ in tiles)
                pe.wait_ge(s_qk, qk.add())

                def scores(j):
                    if j >= 2:
                        pe.wait_ge(s_nm, nm.value() + (j - 1))
                    mm(side[0:n, j % 2, :].rearrange("p (g k) -> p g k", g=SKV)[:, :, 0:keys],
                       qst[:, j, 0:n], kst[:, :, 0:keys]).then_inc(s_sc, 1)

                def turn(j):
                    pe.wait_ge(s_pr, pr.add())
                    if not (first and j == 0):
                        pe.wait_ge(s_pts, pts_.value())
                    if j == 0 and not first or j == 4:
                        pe.wait_ge(s_oc, oc.value())
                    for g in range(SKV):
                        k0 = 0
                        for i, (m_, _) in enumerate(tiles):
                            m = pe.transpose(side[0:m_, 2, (2 * g + i) * P:(2 * g + i) * P + n],
                                             probs[0:n, j % 2, g, k0:k0 + m_], ident[0:n, 0:n])
                            k0 += m_
                    m.then_inc(s_pt, 1)

                def values(j):
                    pe.wait_ge(s_pts, pts_.add())
                    if j % 4 == 0 and not (first and j == 0):
                        pe.wait_ge(s_ot, ot.value())
                    for g in range(SKV):
                        for i, (m_, v) in enumerate(tiles):
                            c = ((j % 4) * SKV + g) * SHD
                            m = mm(side[0:n, 3, c:c + SHD], pts[0:m_, j % 2, g, i, 0:n],
                                   v[:, g * SHD:(g + 1) * SHD], start=(i == 0), stop=(i == len(tiles) - 1))
                    if j % 4 == 3:
                        m.then_inc(s_av, 1)

                def out(q):
                    pe.wait_ge(s_ot, ot.add())
                    for j in range(4):
                        m = pe.transpose(side[:, 2, j * P:j * P + n],
                                         otok[0:n, 2 * j:2 * j + 2, :].rearrange("p a b -> p (a b)"),
                                         ident[0:n, 0:n])
                    m.then_inc(s_ott, 1)
                    oc.add()

                scores(0)
                for j in range(SG):
                    if j + 1 < SG:
                        scores(j + 1)
                    turn(j)
                    values(j)
                    if j % 4 == 3:
                        out(j // 4)
                nm.add(SG)

            swa(P, [(P, vtok[:, 0, :])], first=True)
            with Loop(pe, TB - 1, (qk, 1), (nm, SG), (pr, SG), (pts_, SG), (ot, 2), (oc, 2)) as i:
                swa(P, [(P, vtok[:, bass.ds(i, 1), :].rearrange("p a d -> p (a d)")),
                        (P, vtok[:, bass.ds(i + 1, 1), :].rearrange("p a d -> p (a d)"))])
            pe.wait_ge(s_cache, 32)
            pe.wait_ge(s_oc, oc.value())
            pe.transpose(side[:, 2, 0:P], ckc[:, :], ident).then_inc(s_tr, 1)
            swa(NS, [(P, cvc[:, :]), (NS, vtok[0:NS, TB, :])])
            pe.wait_ge(s_oc, oc.value())

            gx, gA, gn, gf = (Tally(x) for x in (s_gx, s_gA, s_gn, s_gf))

            def gla(n, v):
                lv0 = NLV - n.bit_length() + 1
                pe.wait_ge(s_gx, gx.add())

                def levels(h):
                    for lv in range(lv0, NLV):
                        f = (P >> lv) // 2
                        mm(side[0:n, 0, lv * 64:lv * 64 + n // 2], lev[:, lv, h, 0:n],
                           lev[:, lv, h, 0:n].rearrange("p (a t f) -> p a t f", t=2, f=f)[:, :, 1, :])
                    mm(side[0:n, 1, 0:n], kg[:, h, 0:n], qg[:, h, 0:n])
                    pe.transpose(side[0:n, 1, P:2 * P], kdec[:, h, 0:n], ident).then_inc(s_ga, 1)

                levels(0)
                for h in range(GH):
                    pe.wait_ge(s_gA, gA.add())
                    vh = v[:, h * GDV:(h + 1) * GDV]
                    mm(side[0:n, 2, 0:GDV], A[0:n, 0:n], vh, stop=False)
                    mm(side[0:n, 2, 0:GDV], qeb[:, h, 0:n], state[:, h, :], start=False)
                    mm(side[:, 2, GDV:2 * GDV], kdT[0:n, :], vh).then_inc(s_go, 1)
                    if h + 1 < GH:
                        levels(h + 1)
                    pe.wait_ge(s_gn, gn.add())
                    if h:
                        pe.wait_ge(s_gf, gf.add())
                    for e in range(2):
                        m = pe.transpose(side[:, 3, e * P:e * P + n], osb[0:n, e * P:(e + 1) * P],
                                         ident[0:n, 0:n])
                    m.then_inc(s_gt, 1)
                gf.add()

            with Loop(pe, TB, (gx, 1), (gA, GH), (gn, GH), (gf, GH)) as i:
                gla(P, gv[:, bass.ds(i, 1), :].rearrange("p a d -> p (a d)"))
            pe.wait_ge(s_state, 16)
            gla(NS, gv[0:NS, TB, :])

            pe.wait_ge(s_in, IN + KD + 2 * KD)
            with Loop(pe, KD, (unit, 4), (blocks, 4)):
                for r, (xH, xL) in enumerate(((hH, hL), (ogH, ogL), (hH, hL), (osH, osL))):
                    slot_free()
                    run((U_BR + r) % 4, (3 + r) % 2, xH, xL)
            pe.wait_ge(s_in, IN + 4 * KD)
            with Loop(pe, 2, (unit, 4), (blocks, 4)):
                for r in range(4):
                    slot_free()
                    run((U_WO + r) % 4, (3 + r) % 2, mH, mL)
            norm()
            ffn_in(U_F2I, 1, IN + 4 * KD)
            ffn_out(U_F2O, 1, IN + 5 * KD)
            norm()
            tr = Tally(s_trd)
            tr.add(N_TRD)
            for b in range(TB + 1):
                n = P if b < TB else NS
                for q in range(2):
                    g = 2 * b + q
                    if g == 0:
                        pe.wait_ge(s_ht, N_HT + KD)
                    if g >= 2:
                        pe.wait_ge(s_trd, tr.value() + g - 1)
                    for k in range(4):
                        m = pe.transpose(side[0:n, g % 2, k * P:(k + 1) * P],
                                         xT[:, 4 * q + k, b * P:b * P + n], ident)
                    m.then_inc(s_tr, 1)

        @block.scalar
        def _(act):
            chain, slots, units = Tally(s_act), Tally(s_slot), Tally(s_unit)

            def link(ins):
                ins.then_inc(s_act, 1)
                act.wait_ge(s_act, chain.add())

            def split(u, i=0):
                if u >= U_END and isinstance(i, int):
                    return
                act.wait_ge(s_raw[u % 4], 32 * i + 32 * (u // 4 + 1))
                if u >= 4:
                    act.wait_ge(s_unit, 4 * i + (u - 3))
                act.activation(wH[:, u % 4], raw[:, u % 4], ACT.Copy).then_inc(s_wH, 1)

            def tanh_of(dst, b, unit_no):
                act.wait_ge(s_unit, unit_no)
                act.activation(two(dst[:, :]), slot_h[b], ACT.Tanh, scale=0.5).then_inc(s_tanh, 1)

            def ffn_in(u0, b0):
                for r in range(4):
                    split(u0 + r + 2)
                    blk = slots.add()
                    if r % 2 == 0:
                        if blk > 2:
                            act.wait_ge(s_slot, blk - 2)
                        tanh_of(ft, (b0 + r) % 2, u0 + r + 1)
                with Loop(act, KF // 2 - 1, (slots, 4)) as i:
                    for r in range(4):
                        split(u0 + 4 + r + 2, i)
                        blk = slots.add()
                        if r % 2 == 0:
                            act.wait_ge(s_slot, blk - 2)
                            tanh_of(ft, (b0 + r) % 2, 4 * i + (u0 + 4 + r + 1))

            def ffn_out(u0, last=False):
                with act.Fori(0, KD - 1) as i:
                    for r in range(4):
                        split(u0 + r + 2, i)
                for r in range(4):
                    split(u0 + 4 * (KD - 1) + r + 2)
                slots.add(KD)

            def norm(n, parts):
                act.wait_ge(s_ssum, n + 1)
                link(act.activation(two(rstd[:, :]), side[:, 0:2, 0:TH], ACT.Ln, scale=1.0 / D, bias=eps))
                act.activation(rstd[:, :], rstd[:, :], ACT.Exp, scale=-0.5).then_inc(s_rstd, 1)
                for k in range(parts):
                    act.wait_ge(s_ht, n * KD + k + 1)
                    act.activation(hH[:, k], ht[:, k % 2], ACT.Copy).then_inc(s_inH, 1)

            act.wait_ge(s_table, 16)
            split(0)
            split(1)
            norm(0, KD)
            ffn_in(U_F1I, 0)
            ffn_out(U_F1O)
            norm(1, KD)
            for r in range(3):
                split(U_MIX + r + 2)
            with act.Fori(0, 2) as i:
                for r in range(4):
                    split(U_SQ + r + 2, i)
            act.preload_act_table_set("natural_log_exp_and_others")
            for r in range(GH):
                split(U_GQ + r + 2)
                act.wait_ge(s_lgx, r + 1)
                link(act.activation(la1[:, :], la2[:, :], ACT.Abs))
                link(act.activation(la1[:, :], la1[:, :], ACT.Exp, scale=-1.0))
                act.activation(la1[:, :], la1[:, :], ACT.Ln, bias=one).then_inc(s_sp, 1)
            for r in range(GH):
                split(U_GK + r + 2)
            with act.Fori(0, 2) as i:
                for r in range(4):
                    split(U_GV + r + 2, i)
            slots.add(3 + SG + 2 * GH + KD)
            with Loop(act, 2, (slots, 4)) as i:
                for r in range(4):
                    split(U_GR + r + 2, i)
                    blk = slots.add()
                    act.wait_ge(s_slot, blk - 1)
                    tanh_of(la1, (3 + r) % 2, 4 * i + (U_GR + r + 1))

            act.preload_act_table_set("natural_log_exp_and_others")
            nm, pt, esx = Tally(s_nm), Tally(s_pt), Tally(s_esx)

            def swa(n, keys, first=False):
                for j in range(SG):
                    act.wait_ge(s_nm, nm.add())
                    if not (first and j < 2):
                        act.wait_ge(s_pt, pt.value() + (j - 1))
                    for g in range(SKV):
                        c = 2 * j + g
                        m = act.activation(probs[0:n, j % 2, g, 0:keys], smax[0:n, j % 2, g, 0:keys], ACT.Exp,
                                           scale=SHD ** -0.5, bias=nmax[0:n, c:c + 1],
                                           accum_out=den[0:n, c:c + 1])
                    m.then_inc(s_pr, 1)
                    if j % 4 == 3:
                        act.wait_ge(s_esx, esx.add())
                        c = 8 * (j // 4)
                        act.activation(esum[0:n, c:c + 8], esum[0:n, c:c + 8], ACT.Exp).then_inc(s_es, 1)
                pt.add(SG)

            swa(P, P, first=True)
            with Loop(act, TB - 1, (nm, SG), (pt, SG), (esx, 2)):
                swa(P, 2 * P)
            swa(NS, P + NS)

            gd, gs = Tally(s_gd), Tally(s_gs)

            def gla(n):
                lv0 = NLV - n.bit_length() + 1
                act.wait_ge(s_gd, gd.add())
                act.activation(lev[:, lv0:NLV, :, 0:n], lev[:, lv0:NLV, :, 0:n], ACT.Exp, scale=1.0 / GTAU)
                act.activation(qeb[:, :, 0:n], qeb[:, :, 0:n], ACT.Exp, scale=1.0 / GTAU)
                act.activation(kdec[:, :, 0:n], kdec[:, :, 0:n], ACT.Exp, scale=1.0 / GTAU).then_inc(s_ge, 1)
                for h in range(GH):
                    act.wait_ge(s_gs, gs.add())
                    link(act.activation(gsq[0:n, :], side[0:n, 2, 0:GDV], ACT.Square, accum_out=ssq[0:n]))
                    link(act.activation(sln[0:n], ssq[0:n], ACT.Ln, scale=1.0 / GDV, bias=eps[0:n]))
                    act.activation(srs[0:n], sln[0:n], ACT.Exp, scale=-0.5).then_inc(s_gr, 1)

            with Loop(act, TB, (gd, 1), (gs, GH), (chain, 2 * GH)):
                gla(P)
            gla(NS)

            IN = KD + KF
            act.wait_ge(s_gf, GH * (TB + 1))
            for k in range(KD):
                act.activation(ogH[:, k], go[:, k], ACT.Copy).then_inc(s_inH, 1)
            act.wait_ge(s_in, IN + 2 * KD)
            for k in range(KD):
                act.activation(osH[:, k], qs[:, k], ACT.Copy).then_inc(s_inH, 1)

            with Loop(act, KD, (slots, 4)) as i:
                for r in range(4):
                    split(U_BR + r + 2, i)
                    blk = slots.add()
                    if r % 2 == 0:
                        act.wait_ge(s_slot, blk - 3)
                        tanh_of((tA, tB)[r // 2], (3 + r) % 2, 4 * i + (U_BR + r + 1))
            with act.Fori(0, 2) as i:
                for r in range(4):
                    split(U_WO + r + 2, i)
            slots.add(KD)
            norm(2, KD)
            ffn_in(U_F2I, 1)
            ffn_out(U_F2O)
            norm(3, 0)

        @block.vector
        def _(dve):
            chain, slots, units = Tally(s_dve), Tally(s_slot), Tally(s_unit)
            inp, inH, tanh = Tally(s_in), Tally(s_inH), Tally(s_tanh)
            trd, tr = Tally(s_trd), Tally(s_tr)
            ssn = Tally(s_ss)

            def link(ins):
                ins.then_inc(s_dve, 1)
                dve.wait_ge(s_dve, chain.add())

            def copy(dst, src):
                return dve.tensor_scalar(dst, src, 1.0, None, ALU.mult)

            def free(ins):
                ins.then_inc(s_slot, 1)
                slots.add()

            def squares(x, first=False, last=False):
                if first:
                    link(dve.tensor_tensor(acc[:, :], x, x, ALU.mult))
                    return
                link(dve.tensor_tensor(sq[:, :], x, x, ALU.mult))
                m = dve.tensor_tensor(acc[:, :], acc[:, :], sq[:, :], ALU.add)
                if last:
                    m.then_inc(s_ss, 1)
                    ssn.add()
                else:
                    link(m)

            def norm(n, gain):
                dve.wait_ge(s_rstd, n + 1)

                def low(k):
                    dve.wait_ge(s_inH, inH.add())
                    dve.tensor_tensor(hL[:, k], ht[:, k % 2], hH[:, k].bitcast(F32), ALU.subtract
                                      ).then_inc(s_in, 1)
                    inp.add()

                for k in range(KD):
                    if k >= 2:
                        dve.wait_ge(s_in, inp.value())
                    dve.scalar_tensor_tensor(out=ht[:, k % 2], in0=xT[:, k], scalar=gains[:, gain + k:gain + k + 1],
                                             in1=rstd[:, :], op0=ALU.mult, op1=ALU.mult).then_inc(s_ht, 1)
                    if k:
                        low(k - 1)
                low(KD - 1)

            def ffn_in(u0, b0):
                def pair(b, r, i, j):
                    g, u = slot_h[b], slot_h[1 - b]
                    dve.wait_ge(s_tanh, tanh.add())
                    free(dve.scalar_tensor_tensor(out=two(fs[:, :]), in0=two(ft[:, :]), scalar=1.0, in1=g,
                                                  op0=ALU.add, op1=ALU.mult))
                    dve.wait_ge(s_unit, units.value() + (r + 2))
                    dve.wait_ge(s_slot, slots.value())
                    dve.wait_ge(s_in, inp.value())
                    free(dve.tensor_tensor(two(fp[:, :]), two(fs[:, :]), u, ALU.mult))
                    dve.wait_ge(s_slot, slots.value())
                    hj = hidH[:, bass.ds(j, 1), :].rearrange("p a t -> p (a t)")
                    lj = hidL[:, bass.ds(j, 1), :].rearrange("p a t -> p (a t)")
                    link(copy(hj, fp[:, :]))
                    dve.tensor_tensor(lj, fp[:, :], hj.bitcast(F32), ALU.subtract).then_inc(s_in, 1)
                    inp.add()

                with Loop(dve, KF // 2, (tanh, 2), (slots, 4), (units, 4), (inp, 2), (chain, 2)) as i:
                    for q in range(2):
                        pair(b0, 2 * q, i, 2 * i + q)
                    units.add(4)

            def residual(u_per, b0, scale, nblk):
                assert nblk == KD
                link(dve.memset(acc[:, :], 0.0))
                with Loop(dve, KD // 2, (slots, 2), (units, 2 * u_per), (chain, 4)) as i:
                    for b in range(2):
                        dve.wait_ge(s_unit, units.add(u_per))
                        x = xT[:, bass.ds(2 * i + b, 1), :].rearrange("p a t -> p (a t)")
                        free(dve.scalar_tensor_tensor(out=two(x), in0=slot_h[(b0 + b) % 2], scalar=scale,
                                                      in1=two(x), op0=ALU.mult, op1=ALU.add))
                        dve.wait_ge(s_slot, slots.value())
                        link(dve.tensor_tensor(sq[:, :], x, x, ALU.mult))
                        link(dve.tensor_tensor(acc[:, :], acc[:, :], sq[:, :], ALU.add))
                dve.tensor_scalar(acc[:, :], acc[:, :], 1.0, None, ALU.mult).then_inc(s_ss, 1)
                ssn.add()
                dve.wait_ge(s_ss, ssn.value())

            dve.wait_ge(s_tr, tr.add())
            dve.tensor_copy(gains[:, 0:NG], side[:, 2, 0:NG]).then_inc(s_trd, 1)
            trd.add()
            dve.wait_ge(s_trd, trd.value())
            link(dve.tensor_scalar(sgain, gains[:, G_GLA:G_GLA + 2], 0.5, None, ALU.mult))
            for k in range(KD):
                dve.wait_ge(s_tr, tr.add())
                dve.tensor_copy(xT[:, k], slot_t[k % 2]).then_inc(s_trd, 1)
                dve.wait_ge(s_trd, trd.add())
                squares(xT[:, k], first=(k == 0), last=(k == KD - 1))
            norm(0, G_FFN1)
            ffn_in(U_F1I, 0)
            residual(4, 0, 0.25, KD)
            norm(1, G_MIX)

            def block_done(b, dst, src_rows=P):
                dve.wait_ge(s_unit, units.add())
                free(dve.tensor_scalar(two(dst), slot_h[b][0:src_rows], 1.0, None, ALU.mult))

            block_done(0, kT[:, :])
            block_done(1, vtmp[:, 0])
            block_done(0, glr[:, :], GRANK)
            dve.wait_ge(s_tr, tr.add())
            dve.tensor_copy(vtok[:, 0:TB, :], side[:, 2, :].rearrange("p (b d) -> p b d", b=TB))
            dve.tensor_copy(vtok[0:NS, TB, :], side[0:NS, 3, 0:P])
            dve.tensor_copy(ktok[:, 0, :], side[:, 3, P:2 * P])
            dve.tensor_copy(ktok[0:NS, 1, :], side[0:NS, 3, 2 * P:3 * P]).then_inc(s_trd, 1)
            dve.wait_ge(s_trd, trd.add())
            dve.wait_ge(s_mixin, 32)
            link(dve.tensor_copy(sink.rearrange("p (j g) -> p g j", g=SKV), rden.rearrange("p (g j) -> p g j", g=SKV)))
            dve.tensor_scalar(negsink, sink, -1.0, None, ALU.mult).then_inc(s_ktok, 1)

            def row(t, j):
                return t[:, bass.ds(j, 1), :].rearrange("p a t -> p (a t)")

            with Loop(dve, 2, (slots, 4), (units, 4)) as i:
                for r in range(4):
                    block_done((3 + r) % 2, row(qs, 4 * i + r))
            for r in range(GH):
                dve.wait_ge(s_unit, units.add())
                free(dve.tensor_scalar(two(gq[:, r]), slot_h[(3 + r) % 2], GDK ** -0.5, None, ALU.mult))
                dve.wait_ge(s_lg, r + 1)
                dve.tensor_scalar(two(la2[:, :]), side[:, 0:2, 0:TH], gains[:, G_BG + r:G_BG + r + 1], None,
                                  ALU.add).then_inc(s_lgx, 1)
                dve.wait_ge(s_sp, r + 1)
                dve.wait_ge(s_lgx, r + 1)
                link(dve.scalar_tensor_tensor(out=la2[:, :], in0=la2[:, :], scalar=0.0, in1=la1[:, :],
                                              op0=ALU.min, op1=ALU.subtract))
                link(dve.tensor_tensor_scan(gb[:, r], tab[:, K_RST:K_RST + T], la2[:, :], 0.0,
                                            ALU.mult, ALU.add))
            for r in range(GH):
                block_done((3 + r) % 2, gk[:, r])
            with Loop(dve, 2, (slots, 4), (units, 4), (tr, 4), (trd, 4)) as i:
                for r in range(4):
                    block_done((3 + r) % 2, vtmp[:, r % 2])
                    dve.wait_ge(s_tr, tr.add())
                    copy(gv[:, 0:TB, bass.ds(i * (4 * P) + r * P, P)],
                         side[:, 2, :].rearrange("p (b d) -> p b d", b=TB))
                    copy(gv[0:NS, TB, bass.ds(i * (4 * P) + r * P, P)], side[0:NS, 3, 0:P]).then_inc(s_trd, 1)
                    trd.add()
            with Loop(dve, 2, (slots, 4), (units, 4), (tanh, 4)) as i:
                for r in range(4):
                    units.add()
                    dve.wait_ge(s_tanh, tanh.add())
                    free(dve.scalar_tensor_tensor(out=two(row(go, 4 * i + r)), in0=two(la1[:, :]), scalar=1.0,
                                                  in1=slot_h[(3 + r) % 2], op0=ALU.add, op1=ALU.mult))
            dve.wait_ge(s_slot, slots.value())
            dve.wait_ge(s_trd, trd.value())

            sc, pr, pt, av, es, ott, pts_ = (Tally(x) for x in (s_sc, s_pr, s_pt, s_av, s_es, s_ott, s_pts))
            oc, qk, esx, otl = Tally(s_oc), Tally(s_qk), Tally(s_esx), Tally(s_ot)

            def swa(n, tiles, mask, t0, stage, first=False):
                keys = sum(tiles)
                stage()
                dve.wait_ge(s_qk, qk.add())

                def scores(j):
                    dve.wait_ge(s_sc, sc.add())
                    if not (first and j < 2):
                        dve.wait_ge(s_pr, pr.value() + (j - 1))
                    c = slice(2 * j, 2 * j + 2)
                    masked = smax[0:n, j % 2, :, 0:keys]
                    link(dve.tensor_tensor(
                        masked, side[0:n, j % 2, :].rearrange("p (g k) -> p g k", g=SKV)[:, :, 0:keys],
                        mask.unsqueeze(1).broadcast_to([n, SKV, keys]), ALU.add))
                    link(dve.tensor_reduce(mx[0:n, c], masked, AX_X, ALU.max))
                    dve.scalar_tensor_tensor(out=nmax[0:n, c], in0=mx[0:n, c], scalar=-SHD ** -0.5,
                                             in1=negsink[0:n, c], op0=ALU.mult, op1=ALU.min).then_inc(s_nm, 1)
                    if j % 4 == 3:
                        c = slice(8 * (j // 4), 8 * (j // 4) + 8)
                        dve.wait_ge(s_nm, nmt.value() + (j + 1))
                        dve.tensor_tensor(esum[0:n, c], sink[0:n, c], nmax[0:n, c], ALU.add).then_inc(s_esx, 1)
                        esx.add()

                def turned(j):
                    dve.wait_ge(s_pt, pt.add())
                    src = side[:, 2, :].rearrange("p (g i q) -> p g i q", g=SKV, i=2)
                    if tiles == [P, P]:
                        m = dve.tensor_copy(pts[:, j % 2], src)
                    else:
                        for i, k in enumerate(tiles):
                            m = dve.tensor_copy(pts[0:k, j % 2, :, i, 0:n], src[0:k, :, i, 0:n])
                    m.then_inc(s_pts, 1)
                    pts_.add()

                def output(q):
                    c = slice(8 * q, 8 * q + 8)
                    dve.wait_ge(s_es, es.add())
                    link(dve.tensor_tensor(rden[0:n, c], den[0:n, c], esum[0:n, c], ALU.add))
                    link(dve.reciprocal(rden[0:n, c], rden[0:n, c]))
                    dve.wait_ge(s_av, av.add())
                    dve.tensor_tensor(otok[0:n], side[0:n, 3, :].rearrange("p (a d) -> p a d", d=SHD),
                                      rden[0:n, c].unsqueeze(2).broadcast_to([n, 8, SHD]), ALU.mult
                                      ).then_inc(s_ot, 1)
                    otl.add()
                    dve.wait_ge(s_ott, ott.add())
                    copy(qs[:, 4 * q:4 * q + 4, bass.ds(t0, n)],
                         side[:, 2, :].rearrange("p (j q) -> p j q", j=4)[:, :, 0:n]).then_inc(s_oc, 1)
                    oc.add()

                scores(0)
                for j in range(SG):
                    if j + 1 < SG:
                        scores(j + 1)
                    turned(j)
                    if j % 4 == 3:
                        output(j // 4)
                pr.add(SG)
                nmt.add(SG)

            nmt = Tally(s_nm)

            def stage(t0, k0, keys):
                link(copy(qst[:, :, :], qs[:, :, bass.ds(t0, P)]))
                for g in range(SKV):
                    rows = slice(g * SHD, (g + 1) * SHD)
                    m = copy(kst[rows, g, 0:keys], kT[rows, bass.ds(k0, keys)])
                m.then_inc(s_qk, 1)

            dve.wait_ge(s_lgx, GH)
            link(dve.memset(kst[:, :, :], 0.0))
            swa(P, [P], band[:, P:2 * P], 0, lambda: stage(0, 0, P), first=True)
            with Loop(dve, TB - 1, (sc, SG), (pr, SG), (pt, SG), (av, 2), (es, 2), (ott, 2), (pts_, SG), (oc, 2),
                      (qk, 1), (esx, 2), (otl, 2), (nmt, SG), (chain, 2 * SG + 5)) as i:
                swa(P, [P, P], band, i * P + P, lambda: stage(i * P + P, i * P, 2 * P))

            def stage_sample():
                dve.wait_ge(s_oc, oc.value())
                link(copy(qst[:, :, 0:NS], qs[:, :, NP:T]))
                dve.wait_ge(s_tr, tr.add())
                for g in range(SKV):
                    rows = slice(g * SHD, (g + 1) * SHD)
                    copy(kst[rows, g, P:P + NS], kT[rows, NP:T])
                    m = dve.tensor_copy(kst[rows, g, 0:P], side[rows, 2, 0:P])
                m.then_inc(s_qk, 1)

            swa(NS, [P, NS], band[0:NS, 0:P + NS], NP, stage_sample)
            dve.wait_ge(s_oc, oc.value())

            dve.wait_ge(s_store, 16 * 6)
            link(dve.memset(state[:, :, :], 0.0))
            ge, ga, go_, gr, gt, gA, gs, gn, gf = (Tally(x) for x in (s_ge, s_ga, s_go, s_gr, s_gt, s_gA, s_gs,
                                                                      s_gn, s_gf))
            gx, gd = Tally(s_gx), Tally(s_gd)

            def gla(n, t0):
                lv0 = NLV - n.bit_length() + 1
                tok = bass.ds(t0, n)

                def nodes(x, f, t):
                    return x.rearrange("p h (a t f) -> p h a t f", t=2, f=f)[:, :, :, t, :]

                for lv in range(lv0, NLV):
                    f = (P >> lv) // 2
                    x, b = lev[:, lv, :, 0:n], gb[:, :, tok]
                    ref = nodes(b, f, 0)[:, :, :, f - 1:f].broadcast_to([P, GH, n // (2 * f), f])
                    dve.tensor_tensor(nodes(x, f, 0), ref, nodes(b, f, 0), ALU.subtract)
                    dve.tensor_tensor(nodes(x, f, 1), nodes(b, f, 1), ref, ALU.subtract)
                copy(qeb[:, :, 0:n], gb[:, :, tok])
                dve.tensor_tensor(kdec[:, :, 0:n],
                                  gb[:, :, bass.ds(t0 + (n - 1), 1)].broadcast_to([P, GH, n]), gb[:, :, tok],
                                  ALU.subtract).then_inc(s_gd, 1)
                copy(qg[:, :, 0:n], gq[:, :, tok])
                link(copy(kg[:, :, 0:n], gk[:, :, tok]))
                dve.wait_ge(s_ge, ge.add())
                link(dve.tensor_copy(eL.unsqueeze(2), qeb[:, :, n - 1:n]))
                for lv in range(lv0, NLV):
                    f = (P >> lv) // 2
                    x = lev[:, lv, :, 0:n]
                    dve.tensor_tensor(nodes(x, f, 0), nodes(x, f, 0), nodes(kg[:, :, 0:n], f, 0), ALU.mult)
                    dve.tensor_tensor(nodes(x, f, 1), nodes(x, f, 1), nodes(qg[:, :, 0:n], f, 1), ALU.mult)
                dve.tensor_tensor(qeb[:, :, 0:n], qeb[:, :, 0:n], qg[:, :, 0:n], ALU.mult)
                dve.tensor_tensor(kdec[:, :, 0:n], kdec[:, :, 0:n], kg[:, :, 0:n], ALU.mult).then_inc(s_gx, 1)

                def attention():
                    dve.wait_ge(s_ga, ga.add())
                    link(dve.tensor_tensor(A[0:n, 0:n], side[0:n, 1, 0:n], ident[0:n, 0:n], ALU.mult))
                    dve.tensor_copy(kdT[0:n, :], side[0:n, 1, P:2 * P])
                    link(dve.tensor_tensor(
                        alev[0:n, lv0:NLV, 0:n // 2],
                        side[0:n, 0, 0:NLV * 64].rearrange("p (l c) -> p l c", l=NLV)[:, lv0:NLV, 0:n // 2],
                        tab[0:n, K_LM:K_LM + NLV * 64].rearrange("p (l c) -> p l c", l=NLV)[:, lv0:NLV, 0:n // 2],
                        ALU.mult))
                    for lv in range(lv0, NLV):
                        f = (P >> lv) // 2
                        late = A[0:n, 0:n].rearrange("p (a t f) -> p a t f", t=2, f=f)[:, :, 1, :]
                        m = dve.tensor_tensor(late, late, alev[0:n, lv, 0:n // 2].rearrange("p (a f) -> p a f", f=f),
                                              ALU.add)
                        if lv + 1 < NLV:
                            link(m)
                    m.then_inc(s_gA, 1)
                    gA.add()

                attention()
                for h in range(GH):
                    dve.wait_ge(s_go, go_.add())
                    dve.scalar_tensor_tensor(out=state[:, h, :], in0=state[:, h, :], scalar=eL[:, h:h + 1],
                                             in1=side[:, 2, GDV:2 * GDV], op0=ALU.mult, op1=ALU.add
                                             ).then_inc(s_gs, 1)
                    gs.add()
                    if h + 1 < GH:
                        attention()
                    dve.wait_ge(s_gr, gr.add())
                    dve.tensor_scalar(osb[0:n, :], side[0:n, 2, 0:GDV], srs[0:n], None, ALU.mult
                                      ).then_inc(s_gn, 1)
                    dve.wait_ge(s_gt, gt.add())
                    for e in range(2):
                        g = go[:, 2 * h + e, tok]
                        m = dve.scalar_tensor_tensor(out=g, in0=side[:, 3, e * P:e * P + n],
                                                     scalar=sgain[:, e:e + 1], in1=g, op0=ALU.mult, op1=ALU.mult)
                    m.then_inc(s_gf, 1)
                    gf.add()
                dve.wait_ge(s_gs, gs.value())
                dve.wait_ge(s_gf, gf.value())

            with Loop(dve, TB, (ge, 1), (ga, GH), (go_, GH), (gr, GH), (gt, GH), (gA, GH), (gs, GH), (gf, GH),
                      (chain, 2 + GH * (1 + NLV))) as i:
                gla(P, i * P)
            dve.wait_ge(s_state, 16)
            gla(NS, NP)

            for xs, H, L in ((go, ogH, ogL), (qs, osH, osL)):
                for k in range(KD):
                    dve.wait_ge(s_inH, inH.add())
                    dve.tensor_tensor(L[:, k], xs[:, k], H[:, k].bitcast(F32), ALU.subtract).then_inc(s_in, 1)
                    inp.add()
            dve.wait_ge(s_in, inp.value())

            with Loop(dve, KD, (slots, 4), (units, 4), (tanh, 2), (chain, 2), (inp, 1)) as i:
                for r, (t, m) in enumerate(((tA, mA), (tB, mB))):
                    b = (3 + 2 * r) % 2
                    dve.wait_ge(s_tanh, tanh.add())
                    free(dve.tensor_scalar(t[:, :], t[:, :], 1.0, None, ALU.add))
                    dve.wait_ge(s_slot, slots.value())
                    dve.wait_ge(s_unit, units.add(2))
                    if r == 0:
                        dve.wait_ge(s_in, inp.value())
                    free(dve.tensor_tensor(two(m[:, :]), two(t[:, :]), slot_h[1 - b], ALU.mult))
                dve.wait_ge(s_slot, slots.value())
                link(dve.tensor_tensor(mB[:, :], mA[:, :], mB[:, :], ALU.add))
                link(copy(row(mH, i), mB[:, :]))
                dve.tensor_tensor(row(mL, i), mB[:, :], row(mH, i).bitcast(F32), ALU.subtract).then_inc(s_in, 1)
                inp.add()
            residual(1, 1, 0.5, KD)
            norm(2, G_FFN2)
            ffn_in(U_F2I, 1)
            residual(4, 1, 0.25, KD)

            dve.wait_ge(s_rstd, 4)
            for k in range(KD):
                m = dve.scalar_tensor_tensor(out=xT[:, k], in0=xT[:, k], scalar=gains[:, G_FIN + k:G_FIN + k + 1],
                                             in1=rstd[:, :], op0=ALU.mult, op1=ALU.mult).then_inc(s_ht, 1)
            for b in range(TB + 1):
                n = P if b < TB else NS
                for q in range(2):
                    dve.wait_ge(s_tr, tr.add())
                    dve.tensor_copy(xtok[0:n, b, q * 512:(q + 1) * 512], side[0:n, (2 * b + q) % 2, :]
                                    ).then_inc(s_trd, 1)


_INS = ["x_prompt", "x_sample", "state_gla", "cache_swa_k", "cache_swa_v", "norm_ffn1", "w_ffn1_in", "w_ffn1_out",
        "norm_mix", "w_in", "w_gla_gate_up", "b_gla_gate", "gla_norm", "swa_sinks", "w_branch_gla",
        "w_branch_swa", "w_out", "norm_ffn2", "w_ffn2_in", "w_ffn2_out", "norm_final"]
_OUTS = [(1, NP, D), (1, NS, D), (1, 1, GH, GDK, GDV), (1, 1, WIN, SKV, SHD), (1, 1, WIN, SKV, SHD),
         (1, 1, GH, GDK, GDV), (1, 1, WIN, SKV, SHD), (1, 1, WIN, SKV, SHD)]


def kernel(**inputs):
    import concourse.bacc as bacc
    from concourse.bass_utils import run_bass_kernel_spmd

    nc = bacc.Bacc("TRN2", target_bir_lowering=False, num_devices=1, dynamic_dma_scratch_size=1024)
    arrays, args = {}, []
    for name, a in [(n, inputs[n]) for n in _INS] + [("table", constants())]:
        a = np.ascontiguousarray(a)
        arrays[f"in_{name}"] = a
        args.append(nc.dram_tensor(f"in_{name}", a.shape, mybir.dt.from_np(a.dtype), kind="ExternalInput").ap())
    outs = [nc.dram_tensor(f"out_{i}", shape, F32, kind="ExternalOutput").ap() for i, shape in enumerate(_OUTS)]
    build(nc, args, outs)
    r = run_bass_kernel_spmd(nc, [arrays], core_ids=[0])
    return tuple(r.results[0][f"out_{i}"] for i in range(len(_OUTS)))
```

```python
from contextlib import ExitStack

import concourse.bass as bass
from concourse import mybir
import numpy as np

ALU = mybir.AluOpType
ACT = mybir.ActivationFunctionType
F32 = mybir.dt.float32
F32R = mybir.dt.float32r
U32 = mybir.dt.uint32
AX_X = mybir.AxisListType.X

P = 128
D = 1024
NP, NS = 512, 32
T = NP + NS
TH = T // 2
KD = D // P
DFF = 2816
KF = DFF // P
TB = NP // P
EPS = 1e-6

GH, GDK, GDV, GRANK = 4, 128, 256, 16
GTAU = 16.0
SH, SKV, SHD, WIN, CHUNK = 16, 2, 64, 128, 64
SG = SH // SKV
NLV = 7

C_GQ, C_GK, C_GV, C_GR, C_GLR = 0, 512, 1024, 2048, 3072
C_SQ, C_SK, C_SV, C_GA, C_GB = 3088, 4112, 4240, 4368, 5392

UW = KD * P
FO_SPLIT = ((0, 6), (6, 6), (12, 5), (17, 5))

G_FFN1, G_MIX, G_FFN2, G_FIN, G_BG, G_GLA = 0, 8, 16, 24, 32, 36
NG = 38

K_ID, K_ONE, K_LM = 0, P, 2 * P
K_BAND = K_LM + NLV * 64
K_RST = K_BAND + 2 * P
K_EPS = K_RST + T
NK = K_EPS + 2
MASKED = -1e30
N_TRD = KD + 2
N_HT = 3 * KD


def constants():
    c = np.zeros((P, NK), np.float32)
    s = np.arange(P)[:, None]
    c[:, K_ID:K_ID + P] = np.eye(P)
    c[:, K_ONE:K_ONE + P] = 1.0
    for lv in range(NLV):
        span = P >> lv
        half = span // 2
        col = np.arange(64)[None, :]
        c[:, K_LM + 64 * lv:K_LM + 64 * lv + 64] = (s // span == col // half) & (s % span < half)
    key = np.arange(2 * P)[None, :]
    chunk = s // CHUNK
    seen = (key // CHUNK >= chunk) & (key // CHUNK <= chunk + WIN // CHUNK)
    c[:, K_BAND:K_BAND + 2 * P] = np.where(seen, 0.0, MASKED)
    c[:, K_RST:K_RST + T] = (np.arange(T) % P != 0)[None, :]
    c[:, K_EPS] = EPS
    c[:, K_EPS + 1] = 1.0
    return c


class Tally:

    def __init__(self, sem):
        self.sem, self.base, self.local, self.turn, self.per = sem, 0, 0, None, 0

    def add(self, n=1):
        self.local += n
        return self.value()

    def value(self):
        v = self.base + self.local
        return v if self.turn is None else self.turn * self.per + v


class Loop:

    def __init__(self, eng, count, *counted):
        self.eng, self.count, self.counted = eng, count, counted

    def __enter__(self):
        self.fori = self.eng.Fori(0, self.count)
        i = self.fori.__enter__()
        for tally, per in self.counted:
            tally.base += tally.local
            tally.local, tally.turn, tally.per = 0, i, per
        return i

    def __exit__(self, kind, *exc):
        self.fori.__exit__(kind, *exc)
        if kind is None:
            for tally, per in self.counted:
                assert tally.local == per, (tally.sem, tally.local, per)
                tally.base += self.count * per
                tally.local, tally.turn = 0, None


def build(nc, a, outs):
    (x_prompt, x_sample, state_gla, cache_k, cache_v, norm_ffn1, w_f1i, w_f1o, norm_mix, w_in, w_gup, b_gate,
     gla_norm, sinks, w_bgla, w_bswa, w_out, norm_ffn2, w_f2i, w_f2o, norm_final, table) = a
    y_p, y_s, sg_p, ck_p, cv_p, sg_s, ck_s, cv_s = outs

    with ExitStack() as ctx:
        at = [(nc.sbuf_base + 63) // 64 * 64]

        def place(name, shape, dt=F32, offset=None):
            size = (int(np.prod(shape[1:])) * 4 + 31) // 32 * 32
            if offset is None:
                offset = at[0]
                at[0] += size
            return nc.alloc_sbuf_tensor_at(name, shape, dt, offset=offset)

        def sem(name):
            return ctx.enter_context(nc.semaphore(name))

        ROW = T * 4
        X = at[0]
        xT = place("xT", [P, KD, T])
        hH = place("hH", [P, KD, T], F32R)
        hL = place("hL", [P, KD, T], F32R)
        R = at[0]
        at[0] += 48 * ROW
        raw = place("raw", [P, 4, UW])
        wH = place("wH", [P, 4, UW], F32R)
        wL = place("wL", [P, 4, UW], F32R)
        N = at[0]
        sq = place("sq", [P, T])
        acc = place("acc", [P, T])
        rstd = place("rstd", [P, T])
        tab = place("tab", [P, NK])
        gains = place("gains", [P, 40])
        small = place("small", [P, 128])
        S0 = at[0]
        state = place("state", [P, GH, GDV])
        assert at[0] <= nc.sbuf_usable_end, (at[0], nc.sbuf_usable_end)

        hidH = place("hidH", [P, KF, T], F32R, R)
        hidL = place("hidL", [P, KF, T], F32R, R + KF * ROW)
        ft = place("ft", [P, T], F32, R + 44 * ROW)
        fs = place("fs", [P, T], F32, R + 45 * ROW)
        fp = place("fp", [P, T], F32, R + 46 * ROW)
        ht = place("ht", [P, 2, T], F32, R + 46 * ROW)
        xtok = place("xtok", [P, TB + 1, D], F32, R)
        vrow = place("vrow", [NG, P], F32, R + 20 * ROW)
        qs = place("qs", [P, SG, T], F32, R)
        gqk = place("gqk", [P, 2 * GH, T], F32, R + 8 * ROW)
        gq, gk = gqk[:, 0:GH], gqk[:, GH:2 * GH]
        go = place("go", [P, KD, T], F32, R + 16 * ROW)
        gb = place("gb", [P, GH, T], F32, R + 24 * ROW)
        gv = place("gv", [P, TB + 1, GH * GDV], F32, R + 28 * ROW)
        gB = place("gB", [P, KD, T], F32, X)
        vtmp = place("vtmp", [P, 2, T], F32, R + 16 * ROW)
        la1 = place("la1", [P, T], F32, R + 18 * ROW)
        la2 = place("la2", [P, T], F32, R + 19 * ROW)
        glr = place("glr", [GRANK, T], F32, R + 20 * ROW)
        gup = place("gup", [GRANK, GH * GDK], F32, R + 21 * ROW)
        ktok = place("ktok", [P, 2, P])
        gups = place("gups", [GRANK, GDK])
        bgs = place("bgs", [P, 1])
        M0 = R + 38 * ROW
        kT = place("kT", [P, P + T], F32, M0)
        vtok = place("vtok", [P, TB + 2, P], F32, M0 + (P + T) * 4)
        M1 = M0 + (P + T) * 4 + (TB + 2) * P * 4
        qst = place("qst", [P, SG, P], F32, M1)
        M2 = M1 + SG * P * 4
        kst = place("kst", [P, SKV, 2 * P], F32, M2)
        pts = place("pts", [P, 2, 2, 2, P], F32, M2 + 2048)
        probs = place("probs", [P, 2, 2, 2 * P], F32, M2 + 6144)
        assert M2 + 6144 + 4096 <= M0 + 10 * ROW
        otok = place("otok", [P, SG, P // 2])
        masks = place("masks", [P, TB, 2 * P], F32, S0)
        smax = place("smax", [P, 2, 2, 2 * P], F32, N)
        ckc = place("ckc", [P, P], F32, N + 4096)
        cvc = place("cvc", [P, P], F32, N + 4096 + 512)
        M3 = M0
        lev = place("lev", [P, NLV, GH, P], F32, M3)
        M4 = M3 + NLV * GH * P * 4
        qeb = place("qeb", [P, GH, P], F32, M4)
        kdec = place("kdec", [P, GH, P], F32, M4 + 2048)
        A = place("A", [P, P], F32, M4 + 4096)
        kdT = place("kdT", [P, P], F32, M4 + 4608)
        osb = place("osb", [P, GDV], F32, M4 + 5120)
        gsq = place("gsq", [P, GDV], F32, M4 + 6144)
        assert M4 + 7168 <= M0 + 10 * ROW
        qg = place("qg", [P, GH, P], F32, N)
        kg = place("kg", [P, GH, P], F32, N + 2048)
        alev = place("alev", [P, NLV, 64], F32, N + 4096)
        osH = place("osH", [P, KD, T], F32R, R + 16 * ROW)
        osL = place("osL", [P, KD, T], F32R, R)
        ogH = place("ogH", [P, KD, T], F32R, R + 8 * ROW)
        ogL = place("ogL", [P, KD, T], F32R, R + 16 * ROW)
        tA = place("tA", [P, KD, T], F32, R)
        mH = place("mH", [P, KD, T], F32R, R + 24 * ROW)
        mL = place("mL", [P, KD, T], F32R, R + 32 * ROW)
        t1 = sq
        t2 = acc
        mA = rstd
        mB = place("mB", [P, T], F32, (at[0] - P * SG // 2 * 4) // 32 * 32)
        at[0] += ROW - P * SG // 2 * 4
        mts = (mA, mB)
        assert at[0] <= nc.sbuf_usable_end, (at[0], nc.sbuf_usable_end)

        ident = tab[:, K_ID:K_ID + P]
        ones = tab[:, K_ONE:K_ONE + P]
        band = tab[:, K_BAND:K_BAND + 2 * P]
        eps = tab[:, K_EPS:K_EPS + 1]
        one = tab[:, K_EPS + 1:K_EPS + 2]
        negsink, sink = small[:, 0:16], small[:, 16:32]
        mx, nmax, den, esum = small[:, 32:48], small[:, 48:64], small[:, 64:80], small[:, 80:96]
        rden = small[:, 96:112]
        ssq, sln, srs = small[:, 112:113], small[:, 113:114], small[:, 114:115]
        sgain = small[:, 116:118]
        eL = small[:, 120:124]

        slot = [ctx.enter_context(nc.psum_tensor(f"slot{i}", [P, 2, 512], F32)) for i in range(2)]
        side = ctx.enter_context(nc.psum_tensor("side", [P, 4, 512], F32))
        slot_t = [p[:, :, :].rearrange("p a b -> p (a b)")[:, 0:T] for p in slot]
        slot_h = [p[:, :, 0:TH] for p in slot]

        def two(ap):
            return ap.rearrange("p (a b) -> p a b", a=2)

        s_table = sem("s_table")
        s_tokens = sem("s_tokens")
        s_mixin = sem("s_mixin")
        s_raw = [sem(f"s_raw{i}") for i in range(4)]
        s_wH = sem("s_wH")
        s_wL = sem("s_wL")
        s_unit = sem("s_unit")
        s_slot = sem("s_slot")
        s_tanh = sem("s_tanh")
        s_in = sem("s_in")
        s_ss = sem("s_ss")
        s_ssum = sem("s_ssum")
        s_rstd = sem("s_rstd")
        s_ht = sem("s_ht")
        s_inH = sem("s_inH")
        s_tr = sem("s_tr")
        s_trd = sem("s_trd")
        s_lg = sem("s_lg")
        s_sp = sem("s_sp")
        s_dve = sem("s_dve")
        s_act = sem("s_act")
        s_store = sem("s_store")
        s_ktok = sem("s_ktok")
        s_qk = sem("s_qk")
        s_sc = sem("s_sc")
        s_nm = sem("s_nm")
        s_pr = sem("s_pr")
        s_pt = sem("s_pt")
        s_pts = sem("s_pts")
        s_esx = sem("s_esx")
        s_es = sem("s_es")
        s_av = sem("s_av")
        s_ot = sem("s_ot")
        s_ott = sem("s_ott")
        s_oc = sem("s_oc")
        s_cache = sem("s_cache")
        s_gd = sem("s_gd")
        s_ge = sem("s_ge")
        s_gx = sem("s_gx")
        s_ga = sem("s_ga")
        s_gA = sem("s_gA")
        s_go = sem("s_go")
        s_gs = sem("s_gs")
        s_gr = sem("s_gr")
        s_gn = sem("s_gn")
        s_gt = sem("s_gt")
        s_gf = sem("s_gf")
        s_state = sem("s_state")
        s_stout = sem("s_stout")
        s_xsave = sem("s_xsave")
        s_xback = sem("s_xback")
        s_gbt = sem("s_gbt")
        s_og = sem("s_og")

        U_F1I = 0
        U_F1O = U_F1I + 2 * KF
        U_MIX = U_F1O + 4 * KD
        U_SQ = U_MIX + 3
        U_SA = U_SQ + SG
        U_GA = U_SA + 4 * TB
        U_GR = U_GA + 4 * TB
        U_A = U_GR + KD
        U_BR = U_A + KD
        U_WO = U_BR + KD
        U_F2I = U_WO + KD
        U_F2O = U_F2I + 2 * KF
        U_END = U_F2O + 4 * KD

        xsave = nc.dram_tensor("xsave", (P, KD * T), F32).ap()

        def cut(counts):
            ends = [sum(counts[:n + 1]) for n in range(len(counts))]
            assert ends[-1] % KD == 0
            return [[(c // KD, c % KD) for c in range(e - n, e)] for n, e in zip(counts, ends)]

        SWA_FILL = cut([2, 3, 3, 3, 3, 3, 1, 2, 3, 3, 3, 1, 2])
        GLA_FILL = cut([12] + [1, 4] * GH)
        GLA_SAMPLE_FILL = cut([16] + [3, 5] * GH)
        FREED = 6

        block = ctx.enter_context(nc.Block())

        @block.sync
        def _(sp):
            sp.dma_start(tab[:, :], table).then_inc(s_table, 16)
            sp.dma_start(xtok[:, 0:TB, :], x_prompt[0].rearrange("(b p) d -> p b d", p=P)).then_inc(s_tokens, 16)
            sp.dma_start(xtok[0:NS, TB, :], x_sample[0]).then_inc(s_tokens, 16)
            for c0, v, n in ((G_FFN1, norm_ffn1[0], 8), (G_MIX, norm_mix[0], 8), (G_FFN2, norm_ffn2[0], 8),
                             (G_FIN, norm_final, 8), (G_BG, b_gate[0], 4), (G_GLA, gla_norm[0], 2)):
                sp.dma_start(vrow[c0:c0 + n, :], v.rearrange("(k p) -> k p", p=P)).then_inc(s_tokens, 16)

            def buffer(u, i=0):
                if u >= 4:
                    sp.wait_ge(s_wL, 4 * i + (u - 3))
                return raw[:, u % 4]

            def load(u, i, src, waits=True):
                k = src.shape[1]
                dst = buffer(u, i) if waits else raw[:, u % 4]
                sp.dma_start(dst[:, 0:k * P].rearrange("p (k n) -> p k n", k=k), src
                             ).then_inc(s_raw[u % 4], 32)

            def cols(w, c0, k0=0, k=KD):
                c0 = c0 if isinstance(c0, int) else sp.snap(c0)
                return w[0].rearrange("(k p) n -> p k n", p=P)[:, k0:k0 + k, bass.ds(c0, P)]

            for r in range(4):
                load(r, 0, cols(w_f1i, (r // 2) * P + (r % 2) * DFF))
            with sp.Fori(1, KF // 2) as i:
                for r in range(4):
                    src = cols(w_f1i, i * (2 * P) + (r // 2) * P + (r % 2) * DFF)
                    sp.wait_ge(s_wL, 4 * i + (r - 3))
                    sp.dma_start(raw[:, r].rearrange("p (k n) -> p k n", k=KD), src).then_inc(s_raw[r], 32)
            with sp.Fori(0, KD) as i:
                for r, (k0, k) in enumerate(FO_SPLIT):
                    load(U_F1O + r, i, cols(w_f1o, i * P, k0, k))
            for r, c0 in enumerate((C_SK, C_SV, C_GLR)):
                load(U_MIX + r, 0, cols(w_in, c0))
            sp.wait_ge(s_unit, U_F1O + 4 * KD)
            sp.dma_start(gup[:, :], w_gup[0]).then_inc(s_mixin, 16)
            sp.dma_start(rden, sinks.broadcast_to([P, SH])).then_inc(s_mixin, 16)
            with sp.Fori(0, 2) as i:
                for r in range(4):
                    srcs = [w_in[0].rearrange("(k p) n -> p k n", p=P)[:, :, bass.ds(sp.snap(
                        i * (4 * SHD) + (C_SQ + g * SG * SHD + r * SHD)), SHD)] for g in range(SKV)]
                    dst = buffer(U_SQ + r, i).rearrange("p (k g n) -> p k g n", k=KD, g=SKV)
                    for g in range(SKV):
                        sp.dma_start(dst[:, :, g], srcs[g]).then_inc(s_raw[(U_SQ + r) % 4], 16)
            with sp.Fori(0, TB) as i:
                load(U_SA, i, cols(w_in, i * (2 * P) + C_GV))
                load(U_SA + 1, i, cols(w_in, i * (2 * P) + (C_GV + P)))
                load(U_SA + 2, i, cols(w_in, i * P + C_GQ))
                load(U_SA + 3, i, cols(w_in, i * P + C_GK))
            def branch_swa(u, i, c0):
                c0 = sp.snap(c0)
                dst = buffer(u, i).rearrange("p (k n) -> p k n", k=KD)
                src = w_bswa[0].rearrange("(g j n) c -> g n j c", g=SKV, n=SHD)
                for g in (1, 0):
                    sp.dma_start(dst[g * SHD:(g + 1) * SHD], src[g][:, :, bass.ds(c0, P)]
                                 ).then_inc(s_raw[u % 4], 16)

            with sp.Fori(0, TB) as i:
                load(U_GA, i, cols(w_in, i * (2 * P) + C_GB))
                load(U_GA + 1, i, cols(w_in, i * (2 * P) + (C_GB + P)))
                branch_swa(U_GA + 2, i, i * (2 * P))
                branch_swa(U_GA + 3, i, i * (2 * P) + P)
            for u0, w, c0 in ((U_GR, w_in, C_GR), (U_A, w_in, C_GA), (U_BR, w_bgla, 0)):
                with sp.Fori(0, 2) as i:
                    for r in range(4):
                        load(u0 + r, i, cols(w, i * (4 * P) + (c0 + r * P)))
            with sp.Fori(0, 2) as i:
                for r in range(4):
                    load(U_WO + r, i, cols(w_out, i * (4 * P) + r * P))
            with sp.Fori(0, KF // 2) as i:
                for r in range(4):
                    load(U_F2I + r, i, cols(w_f2i, i * (2 * P) + (r // 2) * P + (r % 2) * DFF))
            with sp.Fori(0, KD) as i:
                for r, (k0, k) in enumerate(FO_SPLIT):
                    load(U_F2O + r, i, cols(w_f2o, i * P, k0, k))
            yt = Tally(s_trd)
            yt.add(N_TRD)
            for b in range(TB + 1):
                sp.wait_ge(s_trd, yt.add(2))
                if b < TB:
                    sp.dma_start(y_p[0, b * P:(b + 1) * P], xtok[:, b, :]).then_inc(s_store, 16)
                else:
                    sp.dma_start(y_s[0], xtok[0:NS, TB, :]).then_inc(s_store, 16)
            sp.wait_ge(s_store, 16 * (6 + 1 + TB + 1))

        @block.gpsimd
        def _(pool):
            def low(n, s):
                pool.wait_ge(s_wH, n)
                pool.tensor_tensor(wL[:, s], raw[:, s], wH[:, s].bitcast(F32), ALU.subtract).then_inc(s_wL, 1)

            with pool.Fori(0, U_END // 4) as i:
                for s in range(4):
                    low(4 * i + (s + 1), s)
            for s in range(U_END % 4):
                low(U_END // 4 * 4 + s + 1, s)

        @block.tensor
        def _(pe):
            unit, blocks = Tally(s_unit), Tally(s_slot)
            inp, ss, trd = Tally(s_in), Tally(s_ss), Tally(s_trd)

            def mm(out, lhsT, rhs, start=True, stop=True):
                return pe.matmul(out, lhsT, rhs, start=start, stop=stop, skip_group_check=True)

            def chunk(s, w, b, xH, xL, c, last):
                w = slice(w * P, (w + 1) * P)
                for n, (wt, x) in enumerate(((wH, xH), (wH, xL), (wL, xH))):
                    for h in range(2):
                        m = mm(slot[b][:, h, 0:TH], wt[:, s, w], x[:, c, h * TH:(h + 1) * TH],
                               start=(c == 0 and n == 0), stop=(last and n == 2))
                return m

            def run(s, b, xH, xL, k0=0, k=KD, last=True, wait_in=None):
                pe.wait_ge(s_wL, unit.add())
                for c in range(k0, k0 + k):
                    if wait_in is not None:
                        pe.wait_ge(s_in, wait_in + c + 1)
                    m = chunk(s, c - k0, b, xH, xL, c, last and c == k0 + k - 1)
                m.then_inc(s_unit, 1)

            def slot_free():
                pe.wait_ge(s_slot, blocks.add() - 2)

            def ffn_in(u0, b0, in0):
                for r in range(4):
                    if b0 + u0 + r < 2:
                        blocks.add()
                    else:
                        slot_free()
                    run((u0 + r) % 4, (b0 + r) % 2, hH, hL, wait_in=in0 if r == 0 else None)
                with Loop(pe, KF // 2 - 1, (unit, 4), (blocks, 4)):
                    for r in range(4):
                        slot_free()
                        run((u0 + r) % 4, (b0 + r) % 2, hH, hL)

            def ffn_out(u0, b0, in0):
                pe.wait_ge(s_in, in0 + KF)
                with Loop(pe, KD // 2, (unit, 8), (blocks, 2)):
                    for b in range(2):
                        slot_free()
                        for r, (k0, k) in enumerate(FO_SPLIT):
                            run((u0 + r) % 4, (b0 + b) % 2, hidH, hidL, k0, k, last=(r == 3))

            def norm():
                pe.wait_ge(s_ss, ss.add())
                for h in range(2):
                    m = mm(side[:, h, 0:TH], ones, acc[:, h * TH:(h + 1) * TH])
                m.then_inc(s_ssum, 1)

            pe.wait_ge(s_table, 16)
            pe.wait_ge(s_tokens, 16 * 8)
            pe.transpose(side[:, 2, 0:NG], vrow[:, :], ident[0:NG, 0:NG]).then_inc(s_tr, 1)
            for k in range(KD):
                if k >= 2:
                    pe.wait_ge(s_trd, k)
                for b in range(TB + 1):
                    n = P if b < TB else NS
                    m = pe.transpose(slot_t[k % 2][:, b * P:b * P + n], xtok[0:n, b, k * P:(k + 1) * P],
                                     ident[0:n, 0:n])
                m.then_inc(s_tr, 1)
            norm()
            ffn_in(U_F1I, 0, 0)
            ffn_out(U_F1O, 0, KD)
            norm()

            IN = KD + KF
            for r in range(3):
                slot_free()
                run((U_MIX + r) % 4, r % 2, hH, hL, wait_in=IN if r == 0 else None)
            pe.wait_ge(s_slot, blocks.value())
            for b in range(TB + 1):
                n = P if b < TB else NS
                m = pe.transpose(side[0:n, 2 + b // TB, (b % TB) * P:(b % TB + 1) * P],
                                 vtmp[:, 0, b * P:b * P + n], ident)
            pe.transpose(side[:, 3, P:2 * P], kT[:, NP:NP + P], ident)
            pe.transpose(side[0:NS, 3, 2 * P:3 * P], kT[:, P + NP:P + T], ident).then_inc(s_tr, 1)
            with Loop(pe, 2, (unit, 4), (blocks, 4)):
                for r in range(4):
                    slot_free()
                    run((U_SQ + r) % 4, (3 + r) % 2, hH, hL)

            qk, nm, pr, pts_, ot, oc = (Tally(x) for x in (s_qk, s_nm, s_pr, s_pts, s_ot, s_oc))
            pe.wait_ge(s_trd, KD + 2)

            def swa(n, tiles, fill=lambda point: None):
                keys = sum(m for m, _ in tiles)

                def scores(j):
                    if j >= 2:
                        pe.wait_ge(s_nm, nm.value() + (j - 1))
                    mm(side[0:n, j % 2, :].rearrange("p (g k) -> p g k", g=SKV)[:, :, 0:keys],
                       qst[:, j, 0:n], kst[:, :, 0:keys]).then_inc(s_sc, 1)

                def turn(j):
                    pe.wait_ge(s_pr, pr.add())
                    pe.wait_ge(s_pts, pts_.value() + (1 if j else 0))
                    pe.wait_ge(s_oc, oc.value())
                    for g in range(SKV):
                        k0 = 0
                        for i, (m_, _) in enumerate(tiles):
                            m = pe.transpose(side[0:m_, 2, (2 * g + i) * P:(2 * g + i) * P + n],
                                             probs[0:n, j % 2, g, k0:k0 + m_], ident[0:n, 0:n])
                            k0 += m_
                    m.then_inc(s_pt, 1)

                def values(j):
                    pe.wait_ge(s_pts, pts_.add())
                    if j % 4 == 0:
                        pe.wait_ge(s_ot, ot.value())
                    for g in range(SKV):
                        for i, (m_, v) in enumerate(tiles):
                            c = ((j % 4) * SKV + g) * SHD
                            m = mm(side[0:n, 3, c:c + SHD], pts[0:m_, j % 2, g, i, 0:n],
                                   v[:, g * SHD:(g + 1) * SHD], start=(i == 0), stop=(i == len(tiles) - 1))
                    if j % 4 == 3:
                        m.then_inc(s_av, 1)

                def out(q):
                    pe.wait_ge(s_ot, ot.add())
                    for j in range(4):
                        m = pe.transpose(side[:, 2, j * P:j * P + n],
                                         otok[0:n, 2 * j:2 * j + 2, :].rearrange("p a b -> p (a b)"),
                                         ident[0:n, 0:n])
                    m.then_inc(s_ott, 1)
                    oc.add()

                fill(0)
                pe.wait_ge(s_qk, qk.add())
                scores(0)
                point = 1
                for j in range(SG):
                    if j + 1 < SG:
                        scores(j + 1)
                    fill(point)
                    point += 1
                    if j == 5:
                        out(0)
                        fill(point)
                        point += 1
                    turn(j)
                    if j:
                        values(j - 1)
                fill(point)
                values(SG - 1)
                fill(point + 1)
                out(1)
                fill(point + 2)
                nm.add(SG)

            pe.wait_ge(s_mixin, 32)
            with Loop(pe, TB, (qk, 1), (nm, SG), (pr, SG), (pts_, SG), (ot, 2), (oc, 2), (unit, 4),
                      (blocks, 7)) as i:
                def turned_values(r, wait):
                    b = r
                    pe.wait_ge(s_slot, blocks.value() + wait)
                    for t in range(TB + 1):
                        n = P if t < TB else NS
                        m = pe.transpose(slot[b][0:n, t // TB, (t % TB) * P:(t % TB + 1) * P],
                                         vtmp[:, r, t * P:t * P + n], ident)
                    m.then_inc(s_tr, 1)

                def fill(point):
                    for r, c in SWA_FILL[point]:
                        if c == 0:
                            pe.wait_ge(s_wL, unit.value() + (r + 1))
                            pe.wait_ge(s_slot, blocks.value() + (-1, 1, 2, 4)[r])
                        m = chunk((U_SA + r) % 4, c, (1, 0, 1, 0)[r], hH, hL, c, c == KD - 1)
                        if c == KD - 1:
                            m.then_inc(s_unit, 1)
                    if point == 1:
                        pe.wait_ge(s_slot, blocks.value())
                        for h in range(2):
                            m = mm(slot[0][:, h, 0:TH], gups[:, :],
                                   glr[:, h * TH:(h + 1) * TH])
                        m.then_inc(s_lg, 1)
                    if point == 7:
                        turned_values(0, 3)
                    if point == 10:
                        turned_values(1, 5)

                swa(P, [(P, vtok[:, bass.ds(i, 1), :].rearrange("p a d -> p (a d)")),
                        (P, vtok[:, bass.ds(i + 1, 1), :].rearrange("p a d -> p (a d)"))], fill)
                unit.add(4)
                blocks.add(7)
            pe.wait_ge(s_cache, 32)
            pe.wait_ge(s_oc, oc.value())
            pe.transpose(side[:, 2, 0:P], ckc[:, :], ident).then_inc(s_tr, 1)
            swa(NS, [(P, cvc[:, :]), (NS, vtok[0:NS, TB + 1, :])])
            pe.wait_ge(s_oc, oc.value())

            gx, gA, gn, gf = (Tally(x) for x in (s_gx, s_gA, s_gn, s_gf))

            def gla(n, v, fill, ready=None):
                lv0 = NLV - n.bit_length() + 1
                fill(0)
                if ready is not None:
                    pe.wait_ge(*ready)
                pe.wait_ge(s_gx, gx.add())

                def levels(h):
                    for lv in range(lv0, NLV):
                        f = (P >> lv) // 2
                        mm(side[0:n, 0, lv * 64:lv * 64 + n // 2], lev[:, lv, h, 0:n],
                           lev[:, lv, h, 0:n].rearrange("p (a t f) -> p a t f", t=2, f=f)[:, :, 1, :])
                    mm(side[0:n, 1, 0:n], kg[:, h, 0:n], qg[:, h, 0:n])
                    pe.transpose(side[0:n, 1, P:2 * P], kdec[:, h, 0:n], ident).then_inc(s_ga, 1)

                levels(0)
                for h in range(GH):
                    fill(2 * h + 1)
                    pe.wait_ge(s_gA, gA.add())
                    vh = v[:, h * GDV:(h + 1) * GDV]
                    mm(side[0:n, 2, 0:GDV], A[0:n, 0:n], vh, stop=False)
                    mm(side[0:n, 2, 0:GDV], qeb[:, h, 0:n], state[:, h, :], start=False)
                    mm(side[:, 2, GDV:2 * GDV], kdT[0:n, :], vh).then_inc(s_go, 1)
                    if h + 1 < GH:
                        levels(h + 1)
                    fill(2 * h + 2)
                    pe.wait_ge(s_gn, gn.add())
                    if h:
                        pe.wait_ge(s_gf, gf.add())
                    for e in range(2):
                        m = pe.transpose(side[:, 3, e * P:e * P + n], osb[0:n, e * P:(e + 1) * P],
                                         ident[0:n, 0:n])
                    m.then_inc(s_gt, 1)
                gf.add()

            def beside(u0, table):
                def fill(point):
                    for r, c in table[point]:
                        xH, xL = hH, hL
                        if u0 == U_GA and r >= 2:
                            xH, xL = osH, osL
                            if r == 2 and c == 0:
                                pe.wait_ge(s_in, IN + 2 * KD)
                        if c == 0:
                            pe.wait_ge(s_wL, unit.value() + (r + 1))
                            pe.wait_ge(s_slot, blocks.value() + (r - 1))
                        m = chunk((u0 + r) % 4, c, (1 + r) % 2, xH, xL, c, c == KD - 1)
                        if c == KD - 1:
                            m.then_inc(s_unit, 1)
                return fill

            with Loop(pe, TB, (gx, 1), (gA, GH), (gn, GH), (gf, GH), (unit, 4), (blocks, 4)) as i:
                gla(P, gv[:, bass.ds(i, 1), :].rearrange("p a d -> p (a d)"), beside(U_GA, GLA_FILL))
                unit.add(4)
                blocks.add(4)
            gla(NS, gv[0:NS, TB, :], beside(U_GR, GLA_SAMPLE_FILL), ready=(s_state, 16))
            unit.add(FREED)
            blocks.add(FREED)
            for r in range(FREED, KD):
                slot_free()
                run((U_GR + r) % 4, (1 + r) % 2, hH, hL)

            for u0, xH, xL, ready in ((U_A, hH, hL, None), (U_BR, ogH, ogL, IN + 3 * KD)):
                if ready is not None:
                    pe.wait_ge(s_in, ready)
                with Loop(pe, 2, (unit, 4), (blocks, 4)):
                    for r in range(4):
                        slot_free()
                        run((u0 + r) % 4, (1 + r) % 2, xH, xL)
            pe.wait_ge(s_in, IN + 4 * KD)
            with Loop(pe, 2, (unit, 4), (blocks, 4)):
                for r in range(4):
                    slot_free()
                    run((U_WO + r) % 4, (1 + r) % 2, mH, mL)
            norm()
            ffn_in(U_F2I, 1, IN + 4 * KD)
            ffn_out(U_F2O, 1, IN + 5 * KD)
            norm()
            tr = Tally(s_trd)
            tr.add(N_TRD)
            for b in range(TB + 1):
                n = P if b < TB else NS
                for q in range(2):
                    g = 2 * b + q
                    if g == 0:
                        pe.wait_ge(s_ht, N_HT + KD)
                    if g >= 2:
                        pe.wait_ge(s_trd, tr.value() + g - 1)
                    for k in range(4):
                        m = pe.transpose(side[0:n, g % 2, k * P:(k + 1) * P],
                                         xT[:, 4 * q + k, b * P:b * P + n], ident)
                    m.then_inc(s_tr, 1)

        @block.scalar
        def _(act):
            chain, slots, units = Tally(s_act), Tally(s_slot), Tally(s_unit)

            def link(ins):
                ins.then_inc(s_act, 1)
                act.wait_ge(s_act, chain.add())

            def split(u, i=0):
                if u >= U_END and isinstance(i, int):
                    return
                act.wait_ge(s_raw[u % 4], 32 * i + 32 * (u // 4 + 1))
                if u >= 4:
                    act.wait_ge(s_unit, 4 * i + (u - 3))
                act.activation(wH[:, u % 4], raw[:, u % 4], ACT.Copy).then_inc(s_wH, 1)

            def tanh_of(dst, b, unit_no):
                act.wait_ge(s_unit, unit_no)
                act.activation(two(dst[:, :]), slot_h[b], ACT.Tanh, scale=0.5).then_inc(s_tanh, 1)

            def ffn_in(u0, b0):
                for r in range(4):
                    split(u0 + r + 2)
                    blk = slots.add()
                    if r % 2 == 0:
                        if blk > 2:
                            act.wait_ge(s_slot, blk - 2)
                        tanh_of(ft, (b0 + r) % 2, u0 + r + 1)
                with Loop(act, KF // 2 - 1, (slots, 4)) as i:
                    for r in range(4):
                        split(u0 + 4 + r + 2, i)
                        blk = slots.add()
                        if r % 2 == 0:
                            act.wait_ge(s_slot, blk - 2)
                            tanh_of(ft, (b0 + r) % 2, 4 * i + (u0 + 4 + r + 1))

            def ffn_out(u0, last=False):
                with act.Fori(0, KD - 1) as i:
                    for r in range(4):
                        split(u0 + r + 2, i)
                for r in range(4):
                    split(u0 + 4 * (KD - 1) + r + 2)
                slots.add(KD)

            def norm(n, parts):
                act.wait_ge(s_ssum, n + 1)
                link(act.activation(two(rstd[:, :]), side[:, 0:2, 0:TH], ACT.Ln, scale=1.0 / D, bias=eps))
                act.activation(rstd[:, :], rstd[:, :], ACT.Exp, scale=-0.5).then_inc(s_rstd, 1)
                for k in range(parts):
                    act.wait_ge(s_ht, n * KD + k + 1)
                    act.activation(hH[:, k], ht[:, k % 2], ACT.Copy).then_inc(s_inH, 1)

            act.wait_ge(s_table, 16)
            split(0)
            split(1)
            norm(0, KD)
            ffn_in(U_F1I, 0)
            ffn_out(U_F1O)
            norm(1, KD)
            for r in range(3):
                split(U_MIX + r + 2)
            act.wait_ge(s_ss, 2)
            act.dma_start(xsave, xT[:, :, :].rearrange("p k t -> p (k t)")).then_inc(s_xsave, 16)
            act.preload_act_table_set("natural_log_exp_and_others")
            with act.Fori(0, 2) as i:
                for r in range(4):
                    split(U_SQ + r + 2, i)
            act.wait_ge(s_ktok, 1)
            act.dma_start(ck_p[0, 0].rearrange("t h d -> t (h d)"), ktok[:, 0, :]).then_inc(s_store, 16)
            act.dma_start(cv_p[0, 0].rearrange("t h d -> t (h d)"), vtok[:, TB, :]).then_inc(s_store, 16)
            for new, old, rows in ((ck_s, cache_k, ktok[0:NS, 1, :]), (cv_s, cache_v, vtok[0:NS, TB + 1, :])):
                act.dma_start(new[0, 0, WIN - NS:].rearrange("t h d -> t (h d)"), rows).then_inc(s_store, 16)
                act.dma_start(new[0, 0, 0:WIN - NS], old[0, 0, NS:]).then_inc(s_store, 16)
            act.dma_start(ckc[:, :], cache_k[0, 0].rearrange("t h d -> t (h d)")).then_inc(s_cache, 16)
            act.dma_start(cvc[:, :], cache_v[0, 0].rearrange("t h d -> t (h d)")).then_inc(s_cache, 16)

            nm, pt, esx = Tally(s_nm), Tally(s_pt), Tally(s_esx)
            slots.add(3 + SG)

            def swa(n, keys, beside=lambda j: None):
                for j in range(SG):
                    act.wait_ge(s_nm, nm.add())
                    if j >= 2 or keys != 2 * P:
                        act.wait_ge(s_pt, pt.value() + (j - 1))
                    for g in range(SKV):
                        c = 2 * j + g
                        m = act.activation(probs[0:n, j % 2, g, 0:keys], smax[0:n, j % 2, g, 0:keys], ACT.Exp,
                                           scale=SHD ** -0.5, bias=nmax[0:n, c:c + 1],
                                           accum_out=den[0:n, c:c + 1])
                    m.then_inc(s_pr, 1)
                    if j % 4 == 3:
                        act.wait_ge(s_esx, esx.add())
                        c = 8 * (j // 4)
                        act.activation(esum[0:n, c:c + 8], esum[0:n, c:c + 8], ACT.Exp).then_inc(s_es, 1)
                    beside(j)
                pt.add(SG)

            with Loop(act, TB, (nm, SG), (pt, SG), (esx, 2), (slots, 7), (chain, 2)) as i:
                split(U_SA + 2, i)

                def beside(j):
                    if j in (2, 4, 6):
                        split(U_SA + 2 + j // 2, i)
                    if j == 1:
                        act.wait_ge(s_slot, slots.add())
                        link(act.activation(la1[:, :], la2[:, :], ACT.Abs))
                        link(act.activation(la1[:, :], la1[:, :], ACT.Exp, scale=-1.0))
                        act.activation(la1[:, :], la1[:, :], ACT.Ln, bias=one).then_inc(s_sp, 1)

                swa(P, 2 * P, beside)
                slots.add(6)
            swa(NS, P + NS)

            act.wait_ge(s_oc, 2 * (TB + 1))
            for k in range(KD):
                act.activation(osH[:, k], qs[:, k], ACT.Copy).then_inc(s_inH, 1)

            gd, gs = Tally(s_gd), Tally(s_gs)

            def gla(n, i=None):
                lv0 = NLV - n.bit_length() + 1
                if i is not None:
                    split(U_GA + 2, i)
                else:
                    split(U_GR + 2)
                    split(U_GR + 3)
                for lv in range(lv0, NLV):
                    act.wait_ge(s_gd, gd.add())
                    act.activation(lev[:, lv, :, 0:n], lev[:, lv, :, 0:n], ACT.Exp, scale=1.0 / GTAU
                                   ).then_inc(s_ge, 1)
                act.wait_ge(s_gd, gd.add())
                act.activation(qeb[:, :, 0:n], qeb[:, :, 0:n], ACT.Exp, scale=1.0 / GTAU)
                act.activation(kdec[:, :, 0:n], kdec[:, :, 0:n], ACT.Exp, scale=1.0 / GTAU).then_inc(s_ge, 1)
                for h in range(GH):
                    if i is not None and h == 2:
                        act.wait_ge(s_slot, slots.add(2))
                    act.wait_ge(s_gs, gs.add())
                    link(act.activation(gsq[0:n, :], side[0:n, 2, 0:GDV], ACT.Square, accum_out=ssq[0:n]))
                    link(act.activation(sln[0:n], ssq[0:n], ACT.Ln, scale=1.0 / GDV, bias=eps[0:n]))
                    act.activation(srs[0:n], sln[0:n], ACT.Exp, scale=-0.5).then_inc(s_gr, 1)
                    if i is None:
                        split(U_GR + 4 + h)
                    elif h < 3:
                        split(U_GA + 3 + h, i)
                    if i is not None and h == 2:
                        g = gB[:, bass.ds(2 * i, 2), :]
                        act.activation(g, g, ACT.Tanh, scale=0.5).then_inc(s_gbt, 1)
                        act.preload_act_table_set("natural_log_exp_and_others")

            with Loop(act, TB, (gd, NLV + 1), (gs, GH), (slots, 4), (chain, 2 * GH)) as i:
                gla(P, i)
                slots.add(2)
            act.dma_start(sg_p[0, 0].rearrange("h d e -> d h e"), state[:, :, :]).then_inc(s_stout, 16)
            act.wait_ge(s_stout, 16)
            act.dma_start(state[:, :, :], state_gla[0, 0].rearrange("h d e -> d h e")).then_inc(s_state, 16)
            gla(NS)
            act.dma_start(sg_s[0, 0].rearrange("h d e -> d h e"), state[:, :, :]).then_inc(s_store, 16)

            act.activation(t1[:, :], go[:, 0], ACT.Tanh, scale=0.5).then_inc(s_tanh, 1)
            for k in range(KD):
                act.wait_ge(s_og, k + 1)
                if k + 1 < KD:
                    act.activation(t1[:, :], go[:, k + 1], ACT.Tanh, scale=0.5).then_inc(s_tanh, 1)
                act.activation(ogH[:, k], mts[k % 2][:, :], ACT.Copy).then_inc(s_inH, 1)
                if k in (0, 1, 3, 5, 7):
                    split(U_A + (k + 1) // 2)

            slots.add(KD)
            with Loop(act, 2, (slots, 4)) as i:
                for r in range(4):
                    dst = two(tA[:, bass.ds(act.snap(4 * i + r), 1), :].rearrange("p k t -> p (k t)"))
                    act.wait_ge(s_unit, 4 * i + (U_A + r + 1))
                    act.wait_ge(s_slot, slots.value())
                    act.activation(dst, slot_h[(1 + r) % 2], ACT.Tanh, scale=0.5).then_inc(s_slot, 1)
                    slots.add()
                    split(U_A + 5 + r, i)

            IN = KD + KF
            slots.add(KD)
            merged = Tally(s_in)
            merged.add(IN + 3 * KD)
            with Loop(act, 2, (merged, 4)) as i:
                for r in range(4):
                    split(U_BR + 5 + r, i)
                    dst = xT[:, bass.ds(act.snap(4 * i + r), 1), :].rearrange("p k t -> p (k t)")
                    src = xsave[:, bass.ds(act.snap(i * (4 * T) + r * T), T)]
                    act.wait_ge(s_in, merged.add())
                    act.dma_start(dst, src).then_inc(s_xback, 16)
            for r in range(5):
                split(U_WO + 5 + r)
            slots.add(KD)
            norm(2, KD)
            ffn_in(U_F2I, 1)
            ffn_out(U_F2O)
            norm(3, 0)

        @block.vector
        def _(dve):
            chain, slots, units = Tally(s_dve), Tally(s_slot), Tally(s_unit)
            inp, inH, tanh = Tally(s_in), Tally(s_inH), Tally(s_tanh)
            trd, tr = Tally(s_trd), Tally(s_tr)
            ssn = Tally(s_ss)

            def link(ins):
                ins.then_inc(s_dve, 1)
                dve.wait_ge(s_dve, chain.add())

            def copy(dst, src):
                return dve.tensor_scalar(dst, src, 1.0, None, ALU.mult)

            def free(ins):
                ins.then_inc(s_slot, 1)
                slots.add()

            def squares(x, first=False, last=False):
                if first:
                    link(dve.tensor_tensor(acc[:, :], x, x, ALU.mult))
                    return
                link(dve.tensor_tensor(sq[:, :], x, x, ALU.mult))
                m = dve.tensor_tensor(acc[:, :], acc[:, :], sq[:, :], ALU.add)
                if last:
                    m.then_inc(s_ss, 1)
                    ssn.add()
                else:
                    link(m)

            def norm(n, gain):
                dve.wait_ge(s_rstd, n + 1)

                def low(k):
                    dve.wait_ge(s_inH, inH.add())
                    dve.tensor_tensor(hL[:, k], ht[:, k % 2], hH[:, k].bitcast(F32), ALU.subtract
                                      ).then_inc(s_in, 1)
                    inp.add()

                for k in range(KD):
                    if k >= 2:
                        dve.wait_ge(s_in, inp.value())
                    dve.scalar_tensor_tensor(out=ht[:, k % 2], in0=xT[:, k], scalar=gains[:, gain + k:gain + k + 1],
                                             in1=rstd[:, :], op0=ALU.mult, op1=ALU.mult).then_inc(s_ht, 1)
                    if k:
                        low(k - 1)
                low(KD - 1)

            def ffn_in(u0, b0):
                def pair(b, r, i, j):
                    g, u = slot_h[b], slot_h[1 - b]
                    dve.wait_ge(s_tanh, tanh.add())
                    free(dve.scalar_tensor_tensor(out=two(fs[:, :]), in0=two(ft[:, :]), scalar=1.0, in1=g,
                                                  op0=ALU.add, op1=ALU.mult))
                    dve.wait_ge(s_unit, units.value() + (r + 2))
                    dve.wait_ge(s_slot, slots.value())
                    dve.wait_ge(s_in, inp.value())
                    free(dve.tensor_tensor(two(fp[:, :]), two(fs[:, :]), u, ALU.mult))
                    dve.wait_ge(s_slot, slots.value())
                    hj = hidH[:, bass.ds(j, 1), :].rearrange("p a t -> p (a t)")
                    lj = hidL[:, bass.ds(j, 1), :].rearrange("p a t -> p (a t)")
                    link(copy(hj, fp[:, :]))
                    dve.tensor_tensor(lj, fp[:, :], hj.bitcast(F32), ALU.subtract).then_inc(s_in, 1)
                    inp.add()

                with Loop(dve, KF // 2, (tanh, 2), (slots, 4), (units, 4), (inp, 2), (chain, 2)) as i:
                    for q in range(2):
                        pair(b0, 2 * q, i, 2 * i + q)
                    units.add(4)

            def residual(u_per, b0, scale, nblk):
                assert nblk == KD
                link(dve.memset(acc[:, :], 0.0))
                with Loop(dve, KD // 2, (slots, 2), (units, 2 * u_per), (chain, 4)) as i:
                    for b in range(2):
                        dve.wait_ge(s_unit, units.add(u_per))
                        x = xT[:, bass.ds(2 * i + b, 1), :].rearrange("p a t -> p (a t)")
                        free(dve.scalar_tensor_tensor(out=two(x), in0=slot_h[(b0 + b) % 2], scalar=scale,
                                                      in1=two(x), op0=ALU.mult, op1=ALU.add))
                        dve.wait_ge(s_slot, slots.value())
                        link(dve.tensor_tensor(sq[:, :], x, x, ALU.mult))
                        link(dve.tensor_tensor(acc[:, :], acc[:, :], sq[:, :], ALU.add))
                dve.tensor_scalar(acc[:, :], acc[:, :], 1.0, None, ALU.mult).then_inc(s_ss, 1)
                ssn.add()
                dve.wait_ge(s_ss, ssn.value())

            dve.wait_ge(s_tr, tr.add())
            dve.tensor_copy(gains[:, 0:NG], side[:, 2, 0:NG]).then_inc(s_trd, 1)
            trd.add()
            dve.wait_ge(s_trd, trd.value())
            link(dve.tensor_scalar(sgain, gains[:, G_GLA:G_GLA + 2], 0.5, None, ALU.mult))
            for k in range(KD):
                dve.wait_ge(s_tr, tr.add())
                dve.tensor_copy(xT[:, k], slot_t[k % 2]).then_inc(s_trd, 1)
                dve.wait_ge(s_trd, trd.add())
                squares(xT[:, k], first=(k == 0), last=(k == KD - 1))
            norm(0, G_FFN1)
            ffn_in(U_F1I, 0)
            residual(4, 0, 0.25, KD)
            norm(1, G_MIX)

            def block_done(b, dst, src_rows=P):
                dve.wait_ge(s_unit, units.add())
                free(dve.tensor_scalar(two(dst), slot_h[b][0:src_rows], 1.0, None, ALU.mult))

            block_done(0, kT[:, P:P + T])
            block_done(1, vtmp[:, 0])
            block_done(0, glr[:, :], GRANK)
            dve.wait_ge(s_tr, tr.add())
            dve.memset(vtok[:, 0, :], 0.0)
            dve.memset(kT[:, 0:P], 0.0)
            dve.memset(kst[:, :, :], 0.0)
            for b in range(TB):
                dve.tensor_copy(masks[:, b], band)
            dve.tensor_copy(vtok[:, 1:TB + 1, :], side[:, 2, :].rearrange("p (b d) -> p b d", b=TB))
            dve.tensor_copy(vtok[0:NS, TB + 1, :], side[0:NS, 3, 0:P])
            dve.tensor_copy(ktok[:, 0, :], side[:, 3, P:2 * P])
            dve.tensor_copy(ktok[0:NS, 1, :], side[0:NS, 3, 2 * P:3 * P]).then_inc(s_trd, 1)
            dve.wait_ge(s_trd, trd.add())
            dve.memset(masks[:, 0, 0:P], MASKED)
            dve.wait_ge(s_mixin, 32)
            link(dve.tensor_copy(sink.rearrange("p (j g) -> p g j", g=SKV), rden.rearrange("p (g j) -> p g j", g=SKV)))
            dve.tensor_scalar(negsink, sink, -1.0, None, ALU.mult).then_inc(s_ktok, 1)

            def row(t, j):
                return t[:, bass.ds(j, 1), :].rearrange("p a t -> p (a t)")

            with Loop(dve, 2, (slots, 4), (units, 4)) as i:
                for r in range(4):
                    block_done((3 + r) % 2, row(qs, 4 * i + r))
            sc, pr, pt, av, es, ott, pts_ = (Tally(x) for x in (s_sc, s_pr, s_pt, s_av, s_es, s_ott, s_pts))
            oc, qk, esx, otl = Tally(s_oc), Tally(s_qk), Tally(s_esx), Tally(s_ot)

            def swa(n, tiles, mask, t0, stage, beside=lambda j: None):
                keys = sum(tiles)
                stage()
                dve.wait_ge(s_qk, qk.add())

                def scores(j):
                    dve.wait_ge(s_sc, sc.add())
                    if j >= 2:
                        dve.wait_ge(s_pr, pr.value() + (j - 1))
                    c = slice(2 * j, 2 * j + 2)
                    masked = smax[0:n, j % 2, :, 0:keys]
                    link(dve.tensor_tensor(
                        masked, side[0:n, j % 2, :].rearrange("p (g k) -> p g k", g=SKV)[:, :, 0:keys],
                        mask.unsqueeze(1).broadcast_to([n, SKV, keys]), ALU.add))
                    link(dve.tensor_reduce(mx[0:n, c], masked, AX_X, ALU.max))
                    dve.scalar_tensor_tensor(out=nmax[0:n, c], in0=mx[0:n, c], scalar=-SHD ** -0.5,
                                             in1=negsink[0:n, c], op0=ALU.mult, op1=ALU.min).then_inc(s_nm, 1)
                    if j % 4 == 3:
                        c = slice(8 * (j // 4), 8 * (j // 4) + 8)
                        dve.wait_ge(s_nm, nmt.value() + (j + 1))
                        dve.tensor_tensor(esum[0:n, c], sink[0:n, c], nmax[0:n, c], ALU.add).then_inc(s_esx, 1)
                        esx.add()

                def turned(j):
                    dve.wait_ge(s_pt, pt.add())
                    src = side[:, 2, :].rearrange("p (g i q) -> p g i q", g=SKV, i=2)
                    if tiles == [P, P]:
                        m = dve.tensor_copy(pts[:, j % 2], src)
                    else:
                        for i, k in enumerate(tiles):
                            m = dve.tensor_copy(pts[0:k, j % 2, :, i, 0:n], src[0:k, :, i, 0:n])
                    m.then_inc(s_pts, 1)
                    pts_.add()

                def divide(q):
                    c = slice(8 * q, 8 * q + 8)
                    dve.wait_ge(s_es, es.add())
                    link(dve.tensor_tensor(rden[0:n, c], den[0:n, c], esum[0:n, c], ALU.add))
                    link(dve.reciprocal(rden[0:n, c], rden[0:n, c]))
                    dve.wait_ge(s_av, av.add())
                    dve.tensor_tensor(otok[0:n], side[0:n, 3, :].rearrange("p (a d) -> p a d", d=SHD),
                                      rden[0:n, c].unsqueeze(2).broadcast_to([n, 8, SHD]), ALU.mult
                                      ).then_inc(s_ot, 1)
                    otl.add()

                def output(q):
                    dve.wait_ge(s_ott, ott.add())
                    copy(qs[:, 4 * q:4 * q + 4, bass.ds(t0, n)],
                         side[:, 2, :].rearrange("p (j q) -> p j q", j=4)[:, :, 0:n]).then_inc(s_oc, 1)
                    oc.add()

                scores(0)
                for j in range(SG):
                    if j + 1 < SG:
                        scores(j + 1)
                    if j == 5:
                        output(0)
                    turned(j)
                    if j == 4:
                        divide(0)
                    beside(j)
                divide(1)
                output(1)
                beside(SG)
                pr.add(SG)
                nmt.add(SG)

            nmt = Tally(s_nm)

            def stage(t0, k0, keys):
                link(copy(qst[:, :, :], qs[:, :, bass.ds(t0, P)]))
                for g in range(SKV):
                    rows = slice(g * SHD, (g + 1) * SHD)
                    m = copy(kst[rows, g, 0:keys], kT[rows, bass.ds(k0, keys)])
                m.then_inc(s_qk, 1)

            def stage_block(i):
                dve.tensor_copy(gups[:, :], gup[:, bass.ds(i * GDK, GDK)])
                dve.tensor_copy(bgs[:, :], gains[:, bass.ds(i + G_BG, 1)])
                stage(i * P, i * P, 2 * P)

            dve.wait_ge(s_slot, slots.value())
            dve.wait_ge(s_ktok, 1)
            lg, sp = Tally(s_lg), Tally(s_sp)
            with Loop(dve, TB, (sc, SG), (pr, SG), (pt, SG), (av, 2), (es, 2), (ott, 2), (pts_, SG), (oc, 2),
                      (qk, 1), (esx, 2), (otl, 2), (nmt, SG), (lg, 1), (sp, 1), (tr, 2),
                      (slots, 7), (units, 4), (chain, 2 * SG + 7)) as i:
                def to_rows(r, b):
                    dve.wait_ge(s_tr, tr.add())
                    c = bass.ds(i * (2 * P) + r * P, P)
                    copy(gv[:, 0:TB, c], slot[b][:, 0, :].rearrange("p (b d) -> p b d", b=TB))
                    free(copy(gv[0:NS, TB, c], slot[b][0:NS, 1, 0:P]))

                def beside(j):
                    if j == 0:
                        dve.wait_ge(s_lg, lg.add())
                        free(dve.tensor_scalar(two(la2[:, :]), slot_h[0], bgs[:, :], None, ALU.add))
                    elif j == 1:
                        block_done(1, vtmp[:, 0])
                    elif j == 2:
                        dve.wait_ge(s_sp, sp.add())
                        link(dve.scalar_tensor_tensor(out=la2[:, :], in0=la2[:, :], scalar=0.0, in1=la1[:, :],
                                                      op0=ALU.min, op1=ALU.subtract))
                        link(dve.tensor_tensor_scan(row(gb, i), tab[:, K_RST:K_RST + T], la2[:, :], 0.0,
                                                    ALU.mult, ALU.add))
                    elif j == 4:
                        block_done(0, vtmp[:, 1])
                    elif j == 5:
                        to_rows(0, 0)
                    elif j == 7:
                        dve.wait_ge(s_unit, units.add())
                        free(dve.tensor_scalar(two(row(gqk, i)), slot_h[1], GDK ** -0.5, None, ALU.mult))
                        to_rows(1, 1)
                    elif j == 8:
                        block_done(0, row(gqk, i + GH))

                swa(P, [P, P], row(masks, i), i * P, lambda: stage_block(i), beside)

            def stage_sample():
                dve.wait_ge(s_oc, oc.value())
                link(copy(qst[:, :, 0:NS], qs[:, :, NP:T]))
                dve.wait_ge(s_tr, tr.add())
                for g in range(SKV):
                    rows = slice(g * SHD, (g + 1) * SHD)
                    copy(kst[rows, g, P:P + NS], kT[rows, P + NP:P + T])
                    m = dve.tensor_copy(kst[rows, g, 0:P], side[rows, 2, 0:P])
                m.then_inc(s_qk, 1)

            swa(NS, [P, NS], band[0:NS, 0:P + NS], NP, stage_sample)
            dve.wait_ge(s_oc, oc.value())

            for k in range(KD):
                dve.wait_ge(s_inH, inH.add())
                dve.tensor_tensor(osL[:, k], qs[:, k], osH[:, k].bitcast(F32), ALU.subtract).then_inc(s_in, 1)
                inp.add()
            gbt = Tally(s_gbt)
            dve.wait_ge(s_store, 16 * 6)
            link(dve.memset(state[:, :, :], 0.0))
            ge, ga, go_, gr, gt, gA, gs, gn, gf = (Tally(x) for x in (s_ge, s_ga, s_go, s_gr, s_gt, s_gA, s_gs,
                                                                      s_gn, s_gf))
            gx, gd = Tally(s_gx), Tally(s_gd)

            def gla(n, t0, beside, first=lambda: None):
                lv0 = NLV - n.bit_length() + 1
                tok = bass.ds(t0, n)

                def nodes(x, f, t):
                    return x.rearrange("p h (a t f) -> p h a t f", t=2, f=f)[:, :, :, t, :]

                for lv in range(lv0, NLV):
                    f = (P >> lv) // 2
                    x, b = lev[:, lv, :, 0:n], gb[:, :, tok]
                    ref = nodes(b, f, 0)[:, :, :, f - 1:f].broadcast_to([P, GH, n // (2 * f), f])
                    dve.tensor_tensor(nodes(x, f, 0), ref, nodes(b, f, 0), ALU.subtract)
                    dve.tensor_tensor(nodes(x, f, 1), nodes(b, f, 1), ref, ALU.subtract).then_inc(s_gd, 1)
                copy(qeb[:, :, 0:n], gb[:, :, tok])
                dve.tensor_tensor(kdec[:, :, 0:n],
                                  gb[:, :, bass.ds(t0 + (n - 1), 1)].broadcast_to([P, GH, n]), gb[:, :, tok],
                                  ALU.subtract).then_inc(s_gd, 1)
                copy(qg[:, :, 0:n], gq[:, :, tok])
                link(copy(kg[:, :, 0:n], gk[:, :, tok]))
                for lv in range(lv0, NLV):
                    dve.wait_ge(s_ge, ge.add())
                    f = (P >> lv) // 2
                    x = lev[:, lv, :, 0:n]
                    dve.tensor_tensor(nodes(x, f, 0), nodes(x, f, 0), nodes(kg[:, :, 0:n], f, 0), ALU.mult)
                    dve.tensor_tensor(nodes(x, f, 1), nodes(x, f, 1), nodes(qg[:, :, 0:n], f, 1), ALU.mult)
                dve.wait_ge(s_ge, ge.add())
                link(dve.tensor_copy(eL.unsqueeze(2), qeb[:, :, n - 1:n]))
                dve.tensor_tensor(qeb[:, :, 0:n], qeb[:, :, 0:n], qg[:, :, 0:n], ALU.mult)
                dve.tensor_tensor(kdec[:, :, 0:n], kdec[:, :, 0:n], kg[:, :, 0:n], ALU.mult).then_inc(s_gx, 1)
                first()

                def attention():
                    dve.wait_ge(s_ga, ga.add())
                    link(dve.tensor_tensor(A[0:n, 0:n], side[0:n, 1, 0:n], ident[0:n, 0:n], ALU.mult))
                    dve.tensor_copy(kdT[0:n, :], side[0:n, 1, P:2 * P])
                    link(dve.tensor_tensor(
                        alev[0:n, lv0:NLV, 0:n // 2],
                        side[0:n, 0, 0:NLV * 64].rearrange("p (l c) -> p l c", l=NLV)[:, lv0:NLV, 0:n // 2],
                        tab[0:n, K_LM:K_LM + NLV * 64].rearrange("p (l c) -> p l c", l=NLV)[:, lv0:NLV, 0:n // 2],
                        ALU.mult))
                    for lv in range(lv0, NLV):
                        f = (P >> lv) // 2
                        late = A[0:n, 0:n].rearrange("p (a t f) -> p a t f", t=2, f=f)[:, :, 1, :]
                        m = dve.tensor_tensor(late, late, alev[0:n, lv, 0:n // 2].rearrange("p (a f) -> p a f", f=f),
                                              ALU.add)
                        if lv + 1 < NLV:
                            link(m)
                    m.then_inc(s_gA, 1)
                    gA.add()

                attention()
                for h in range(GH):
                    beside(h)
                    dve.wait_ge(s_go, go_.add())
                    dve.scalar_tensor_tensor(out=state[:, h, :], in0=state[:, h, :], scalar=eL[:, h:h + 1],
                                             in1=side[:, 2, GDV:2 * GDV], op0=ALU.mult, op1=ALU.add
                                             ).then_inc(s_gs, 1)
                    gs.add()
                    if h + 1 < GH:
                        attention()
                    dve.wait_ge(s_gr, gr.add())
                    dve.tensor_scalar(osb[0:n, :], side[0:n, 2, 0:GDV], srs[0:n], None, ALU.mult
                                      ).then_inc(s_gn, 1)
                    dve.wait_ge(s_gt, gt.add())
                    for e in range(2):
                        m = dve.tensor_scalar(gqk[:, 2 * h + e, tok], side[:, 3, e * P:e * P + n],
                                              sgain[:, e:e + 1], None, ALU.mult)
                    m.then_inc(s_gf, 1)
                    gf.add()
                beside(GH)
                dve.wait_ge(s_gs, gs.value())
                dve.wait_ge(s_gf, gf.value())

            dve.wait_ge(s_xsave, 16)
            with Loop(dve, TB, (gbt, 1), (ge, NLV + 1), (ga, GH), (go_, GH), (gr, GH), (gt, GH), (gA, GH), (gs, GH),
                      (gf, GH), (slots, 4), (units, 4), (chain, 2 + GH * (1 + NLV))) as i:
                def branch(b, j):
                    dve.wait_ge(s_unit, units.add())
                    free(dve.scalar_tensor_tensor(out=two(row(gB, j)), in0=two(row(gB, j)), scalar=1.0,
                                                  in1=slot_h[b], op0=ALU.add, op1=ALU.mult))

                def beside(h):
                    if h == 0:
                        block_done(1, row(gB, 2 * i))
                    elif h == 1:
                        block_done(0, row(gB, 2 * i + 1))
                    elif h == 3:
                        dve.wait_ge(s_gbt, gbt.add())
                        branch(1, 2 * i)
                    elif h == GH:
                        branch(0, 2 * i + 1)

                gla(P, i * P, beside)

            def output_gate(k):
                block_done((1 + k) % 2, go[:, k])

            dve.wait_ge(s_state, 16)
            gla(NS, NP, lambda h: output_gate(h + 1), lambda: output_gate(0))

            def low(k):
                dve.wait_ge(s_inH, inH.add())
                dve.tensor_tensor(ogL[:, k], mts[k % 2][:, :], ogH[:, k].bitcast(F32), ALU.subtract
                                  ).then_inc(s_in, 1)
                inp.add()

            for k in range(KD):
                if k in (2, 4):
                    output_gate(FREED + k // 2 - 1)
                dve.wait_ge(s_tanh, tanh.add())
                link(dve.scalar_tensor_tensor(out=t2[:, :], in0=t1[:, :], scalar=1.0, in1=go[:, k],
                                              op0=ALU.add, op1=ALU.mult))
                dve.wait_ge(s_in, inp.value())
                dve.tensor_tensor(mts[k % 2][:, :], t2[:, :], gqk[:, k], ALU.mult).then_inc(s_og, 1)
                if k:
                    low(k - 1)
            low(KD - 1)

            units.add(KD)
            slots.add(KD)
            dve.wait_ge(s_slot, slots.value())
            with Loop(dve, 2, (slots, 4), (units, 4), (chain, 8), (inp, 4)) as i:
                for r in range(4):
                    dve.wait_ge(s_unit, units.add())
                    free(dve.scalar_tensor_tensor(out=two(mA[:, :]), in0=two(row(tA, 4 * i + r)), scalar=1.0,
                                                  in1=slot_h[(1 + r) % 2], op0=ALU.add, op1=ALU.mult))
                    dve.wait_ge(s_slot, slots.value())
                    dve.wait_ge(s_in, inp.value())
                    link(dve.tensor_tensor(mB[:, :], mA[:, :], row(gB, 4 * i + r), ALU.add))
                    link(copy(row(mH, 4 * i + r), mB[:, :]))
                    dve.tensor_tensor(row(mL, 4 * i + r), mB[:, :], row(mH, 4 * i + r).bitcast(F32), ALU.subtract
                                      ).then_inc(s_in, 1)
                    inp.add()
            dve.wait_ge(s_xback, 16 * KD)
            residual(1, 1, 0.5, KD)
            norm(2, G_FFN2)
            ffn_in(U_F2I, 1)
            residual(4, 1, 0.25, KD)

            dve.wait_ge(s_rstd, 4)
            for k in range(KD):
                m = dve.scalar_tensor_tensor(out=xT[:, k], in0=xT[:, k], scalar=gains[:, G_FIN + k:G_FIN + k + 1],
                                             in1=rstd[:, :], op0=ALU.mult, op1=ALU.mult).then_inc(s_ht, 1)
            for b in range(TB + 1):
                n = P if b < TB else NS
                for q in range(2):
                    dve.wait_ge(s_tr, tr.add())
                    dve.tensor_copy(xtok[0:n, b, q * 512:(q + 1) * 512], side[0:n, (2 * b + q) % 2, :]
                                    ).then_inc(s_trd, 1)


_INS = ["x_prompt", "x_sample", "state_gla", "cache_swa_k", "cache_swa_v", "norm_ffn1", "w_ffn1_in", "w_ffn1_out",
        "norm_mix", "w_in", "w_gla_gate_up", "b_gla_gate", "gla_norm", "swa_sinks", "w_branch_gla",
        "w_branch_swa", "w_out", "norm_ffn2", "w_ffn2_in", "w_ffn2_out", "norm_final"]
_OUTS = [(1, NP, D), (1, NS, D), (1, 1, GH, GDK, GDV), (1, 1, WIN, SKV, SHD), (1, 1, WIN, SKV, SHD),
         (1, 1, GH, GDK, GDV), (1, 1, WIN, SKV, SHD), (1, 1, WIN, SKV, SHD)]


def kernel(**inputs):
    import concourse.bacc as bacc
    from concourse.bass_utils import run_bass_kernel_spmd

    nc = bacc.Bacc("TRN2", target_bir_lowering=False, num_devices=1, dynamic_dma_scratch_size=1024)
    arrays, args = {}, []
    for name, a in [(n, inputs[n]) for n in _INS] + [("table", constants())]:
        a = np.ascontiguousarray(a)
        arrays[f"in_{name}"] = a
        args.append(nc.dram_tensor(f"in_{name}", a.shape, mybir.dt.from_np(a.dtype), kind="ExternalInput").ap())
    outs = [nc.dram_tensor(f"out_{i}", shape, F32, kind="ExternalOutput").ap() for i, shape in enumerate(_OUTS)]
    build(nc, args, outs)
    r = run_bass_kernel_spmd(nc, [arrays], core_ids=[0])
    return tuple(r.results[0][f"out_{i}"] for i in range(len(_OUTS)))
```

```python
from contextlib import ExitStack

import concourse.bass as bass
from concourse import mybir
import numpy as np

ALU = mybir.AluOpType
ACT = mybir.ActivationFunctionType
F32 = mybir.dt.float32
F32R = mybir.dt.float32r
U32 = mybir.dt.uint32
AX_X = mybir.AxisListType.X

P = 128
D = 1024
NP, NS = 512, 32
T = NP + NS
TH = T // 2
KD = D // P
DFF = 2816
KF = DFF // P
TB = NP // P
EPS = 1e-6

GH, GDK, GDV, GRANK = 4, 128, 256, 16
GTAU = 16.0
SH, SKV, SHD, WIN, CHUNK = 16, 2, 64, 128, 64
SG = SH // SKV
NLV = 7

C_GQ, C_GK, C_GV, C_GR, C_GLR = 0, 512, 1024, 2048, 3072
C_SQ, C_SK, C_SV, C_GA, C_GB = 3088, 4112, 4240, 4368, 5392

UW = KD * P
FO_SPLIT = ((0, 6), (6, 6), (12, 5), (17, 5))

G_FFN1, G_MIX, G_FFN2, G_FIN, G_BG, G_GLA = 0, 8, 16, 24, 32, 36
NG = 38

K_ID, K_ONE, K_LM = 0, P, 2 * P
K_BAND = K_LM + NLV * 64
K_RST = K_BAND + 2 * P
K_EPS = K_RST + T
NK = K_EPS + 2
MASKED = -1e30
N_TRD = KD + 3


def constants():
    c = np.zeros((P, NK), np.float32)
    s = np.arange(P)[:, None]
    c[:, K_ID:K_ID + P] = np.eye(P)
    c[:, K_ONE:K_ONE + P] = 1.0
    for lv in range(NLV):
        span = P >> lv
        half = span // 2
        col = np.arange(64)[None, :]
        c[:, K_LM + 64 * lv:K_LM + 64 * lv + 64] = (s // span == col // half) & (s % span < half)
    key = np.arange(2 * P)[None, :]
    chunk = s // CHUNK
    seen = (key // CHUNK >= chunk) & (key // CHUNK <= chunk + WIN // CHUNK)
    c[:, K_BAND:K_BAND + 2 * P] = np.where(seen, 0.0, MASKED)
    c[:, K_RST:K_RST + T] = (np.arange(T) % P != 0)[None, :]
    c[:, K_EPS] = EPS
    c[:, K_EPS + 1] = 1.0
    return c


class Tally:

    def __init__(self, sem):
        self.sem, self.base, self.local, self.turn, self.per = sem, 0, 0, None, 0

    def add(self, n=1):
        self.local += n
        return self.value()

    def value(self):
        v = self.base + self.local
        return v if self.turn is None else self.turn * self.per + v


class Loop:

    def __init__(self, eng, count, *counted):
        self.eng, self.count, self.counted = eng, count, counted

    def __enter__(self):
        self.fori = self.eng.Fori(0, self.count)
        i = self.fori.__enter__()
        for tally, per in self.counted:
            tally.base += tally.local
            tally.local, tally.turn, tally.per = 0, i, per
        return i

    def __exit__(self, kind, *exc):
        self.fori.__exit__(kind, *exc)
        if kind is None:
            for tally, per in self.counted:
                assert tally.local == per, (tally.sem, tally.local, per)
                tally.base += self.count * per
                tally.local, tally.turn = 0, None


def build(nc, a, outs):
    (x_prompt, x_sample, state_gla, cache_k, cache_v, norm_ffn1, w_f1i, w_f1o, norm_mix, w_in, w_gup, b_gate,
     gla_norm, sinks, w_bgla, w_bswa, w_out, norm_ffn2, w_f2i, w_f2o, norm_final, table) = a
    y_p, y_s, sg_p, ck_p, cv_p, sg_s, ck_s, cv_s = outs

    with ExitStack() as ctx:
        at = [(nc.sbuf_base + 63) // 64 * 64]

        def place(name, shape, dt=F32, offset=None):
            size = (int(np.prod(shape[1:])) * 4 + 31) // 32 * 32
            if offset is None:
                offset = at[0]
                at[0] += size
            return nc.alloc_sbuf_tensor_at(name, shape, dt, offset=offset)

        def sem(name):
            return ctx.enter_context(nc.semaphore(name))

        ROW = T * 4
        X = at[0]
        xT = place("xT", [P, KD, T])
        hH = place("hH", [P, KD, T], F32R)
        hL = place("hL", [P, KD, T], F32R)
        R = at[0]
        at[0] += 48 * ROW
        raw = place("raw", [P, 4, UW])
        wH = place("wH", [P, 4, UW], F32R)
        wL = place("wL", [P, 4, UW], F32R)
        N = at[0]
        sq = place("sq", [P, T])
        acc = place("acc", [P, T])
        rstd = place("rstd", [P, T])
        tab = place("tab", [P, NK])
        gains = place("gains", [P, 40])
        small = place("small", [P, 128])
        S0 = at[0]
        state = place("state", [P, GH, GDV])
        assert at[0] <= nc.sbuf_usable_end, (at[0], nc.sbuf_usable_end)

        hidH = place("hidH", [P, KF, T], F32R, R)
        hidL = place("hidL", [P, KF, T], F32R, R + KF * ROW)
        ft = place("ft", [P, T], F32, R + 44 * ROW)
        fs = place("fs", [P, T], F32, R + 45 * ROW)
        fp = place("fp", [P, T], F32, R + 46 * ROW)
        fg = place("fg", [P, T], F32, R + 47 * ROW)
        xtok = place("xtok", [P, TB + 1, D], F32, R)
        vrow = place("vrow", [NG, P], F32, R + 20 * ROW)
        qs = place("qs", [P, SG, T], F32, R)
        gqk = place("gqk", [P, 2 * GH, T], F32, R + 8 * ROW)
        gq, gk = gqk[:, 0:GH], gqk[:, GH:2 * GH]
        go = place("go", [P, KD, T], F32, R + 16 * ROW)
        gb = place("gb", [P, GH, T], F32, R + 24 * ROW)
        gv = place("gv", [P, TB + 1, GH * GDV], F32, R + 28 * ROW)
        gB = place("gB", [P, KD, T], F32, X)
        vtmp = place("vtmp", [P, 2, T], F32, R + 16 * ROW)
        la1 = place("la1", [P, T], F32, R + 18 * ROW)
        la2 = place("la2", [P, T], F32, R + 19 * ROW)
        glr = place("glr", [GRANK, T], F32, R + 20 * ROW)
        gup = place("gup", [GRANK, GH * GDK], F32, R + 21 * ROW)
        ktok = place("ktok", [P, 2, P])
        gups = place("gups", [GRANK, GDK])
        bgs = place("bgs", [P, 1])
        M0 = R + 38 * ROW
        kT = place("kT", [P, P + T], F32, M0)
        vtok = place("vtok", [P, TB + 2, P], F32, M0 + (P + T) * 4)
        M1 = M0 + (P + T) * 4 + (TB + 2) * P * 4
        qst = place("qst", [P, SG, P], F32, M1)
        M2 = M1 + SG * P * 4
        kst = place("kst", [P, SKV, 2 * P], F32, M2)
        pts = place("pts", [P, 2, 2, 2, P], F32, M2 + 2048)
        probs = place("probs", [P, 2, 2, 2 * P], F32, M2 + 6144)
        assert M2 + 6144 + 4096 <= M0 + 10 * ROW
        otok = place("otok", [P, SG, P // 2])
        masks = place("masks", [P, TB, 2 * P], F32, S0)
        smax = place("smax", [P, 2, 2, 2 * P], F32, N)
        ckc = place("ckc", [P, P])
        cvc = place("cvc", [P, P])
        M3 = M0
        lev = place("lev", [P, NLV, GH, P], F32, M3)
        M4 = M3 + NLV * GH * P * 4
        qeb = place("qeb", [P, GH, P], F32, M4)
        kdec = place("kdec", [P, GH, P], F32, M4 + 2048)
        kdT = place("kdT", [P, GH, P], F32, M4 + 2048)
        osb = place("osb", [P, GDV], F32, M4 + 5120)
        gsq = place("gsq", [P, GDV], F32, M4 + 6144)
        assert M4 + 7168 <= M0 + 10 * ROW
        qg = place("qg", [P, GH, P], F32, N)
        kg = place("kg", [P, GH, P], F32, N + 2048)
        A = place("A", [P, GH, P], F32, N + 2048)
        osH = place("osH", [P, KD, T], F32R, R + 16 * ROW)
        osL = place("osL", [P, KD, T], F32R, R)
        ogH = place("ogH", [P, KD, T], F32R, R + 8 * ROW)
        ogL = place("ogL", [P, KD, T], F32R, R + 16 * ROW)
        tA = place("tA", [P, KD, T], F32, R)
        mH = place("mH", [P, KD, T], F32R, R + 24 * ROW)
        mL = place("mL", [P, KD, T], F32R, R + 32 * ROW)
        t1 = sq
        t2 = acc
        mA = place("mA", [P, T], F32, R + 40 * ROW)
        mB = place("mB", [P, T], F32, (at[0] - P * SG // 2 * 4) // 32 * 32)
        alev = place("alev", [P, NLV, 64], F32, (at[0] - P * SG // 2 * 4) // 32 * 32)
        at[0] += ROW - P * SG // 2 * 4
        mts = (mA, mB)
        assert at[0] <= nc.sbuf_usable_end, (at[0], nc.sbuf_usable_end)

        ident = tab[:, K_ID:K_ID + P]
        ones = tab[:, K_ONE:K_ONE + P]
        band = tab[:, K_BAND:K_BAND + 2 * P]
        eps = tab[:, K_EPS:K_EPS + 1]
        one = tab[:, K_EPS + 1:K_EPS + 2]
        negsink, sink = small[:, 0:16], small[:, 16:32]
        mx, nmax, den, esum = small[:, 32:48], small[:, 48:64], small[:, 64:80], small[:, 80:96]
        rden = small[:, 96:112]
        ssq, sln, srs = small[:, 112:113], small[:, 113:114], small[:, 114:115]
        sgain = small[:, 116:118]
        eL = small[:, 120:124]

        slot = [ctx.enter_context(nc.psum_tensor(f"slot{i}", [P, 2, 512], F32)) for i in range(2)]
        side = ctx.enter_context(nc.psum_tensor("side", [P, 4, 512], F32))
        slot_t = [p[:, :, :].rearrange("p a b -> p (a b)")[:, 0:T] for p in slot]
        slot_h = [p[:, :, 0:TH] for p in slot]

        def two(ap):
            return ap.rearrange("p (a b) -> p a b", a=2)

        s_table = sem("s_table")
        s_tokens = sem("s_tokens")
        s_mixin = sem("s_mixin")
        s_raw = [sem(f"s_raw{i}") for i in range(4)]
        s_wH = sem("s_wH")
        s_wL = sem("s_wL")
        s_unit = sem("s_unit")
        s_slot = sem("s_slot")
        s_tanh = sem("s_tanh")
        s_in = sem("s_in")
        s_ss = sem("s_ss")
        s_ssum = sem("s_ssum")
        s_rstd = sem("s_rstd")
        s_sq = sem("s_sq")
        s_squ = sem("s_squ")
        s_ht = sem("s_ht")
        s_inH = sem("s_inH")
        s_tr = sem("s_tr")
        s_trd = sem("s_trd")
        s_lg = sem("s_lg")
        s_sp = sem("s_sp")
        s_dve = sem("s_dve")
        s_act = sem("s_act")
        s_store = sem("s_store")
        s_ktok = sem("s_ktok")
        s_qk = sem("s_qk")
        s_sc = sem("s_sc")
        s_nm = sem("s_nm")
        s_pr = sem("s_pr")
        s_pt = sem("s_pt")
        s_pts = sem("s_pts")
        s_esx = sem("s_esx")
        s_es = sem("s_es")
        s_av = sem("s_av")
        s_ot = sem("s_ot")
        s_ott = sem("s_ott")
        s_oc = sem("s_oc")
        s_cache = sem("s_cache")
        s_gq = sem("s_gq")
        s_gd = sem("s_gd")
        s_ge = sem("s_ge")
        s_gx = sem("s_gx")
        s_g4 = sem("s_g4")
        s_gdi = sem("s_gdi")
        s_gkd = sem("s_gkd")
        s_ga = sem("s_ga")
        s_gA = sem("s_gA")
        s_go = sem("s_go")
        s_gs = sem("s_gs")
        s_gr = sem("s_gr")
        s_gn = sem("s_gn")
        s_gt = sem("s_gt")
        s_gf = sem("s_gf")
        s_state = sem("s_state")
        s_stout = sem("s_stout")
        s_xsave = sem("s_xsave")
        s_xback = sem("s_xback")
        s_gbt = sem("s_gbt")
        s_og = sem("s_og")

        U_F1I = 0
        U_F1O = U_F1I + 2 * KF
        U_MIX = U_F1O + 4 * KD
        U_SQ = U_MIX + 3
        U_SA = U_SQ + SG
        U_GA = U_SA + 4 * TB
        U_GR = U_GA + 4 * TB
        U_A = U_GR + KD
        U_BR = U_A + KD
        U_WO = U_BR + KD
        U_F2I = U_WO + KD
        U_F2O = U_F2I + 2 * KF
        U_END = U_F2O + 4 * KD

        xsave = nc.dram_tensor("xsave", (P, KD * T), F32).ap()

        def cut(counts):
            ends = [sum(counts[:n + 1]) for n in range(len(counts))]
            assert ends[-1] % KD == 0
            return [[(c // KD, c % KD) for c in range(e - n, e)] for n, e in zip(counts, ends)]

        SWA_FILL = cut([2, 3, 3, 3, 3, 3, 1, 2, 3, 3, 3, 1, 2])
        GLA_FILL = cut([20] + [0, 3] * GH)
        GLA_SAMPLE_FILL = cut([20] + [2, 5] * GH)
        FREED = 6

        block = ctx.enter_context(nc.Block())

        @block.sync
        def _(sp):
            sp.dma_start(tab[:, :], table).then_inc(s_table, 16)
            sp.dma_start(xtok[:, 0:TB, :], x_prompt[0].rearrange("(b p) d -> p b d", p=P)).then_inc(s_tokens, 16)
            sp.dma_start(xtok[0:NS, TB, :], x_sample[0]).then_inc(s_tokens, 16)
            for c0, v, n in ((G_FFN1, norm_ffn1[0], 8), (G_MIX, norm_mix[0], 8), (G_FFN2, norm_ffn2[0], 8),
                             (G_FIN, norm_final, 8), (G_BG, b_gate[0], 4), (G_GLA, gla_norm[0], 2)):
                sp.dma_start(vrow[c0:c0 + n, :], v.rearrange("(k p) -> k p", p=P)).then_inc(s_tokens, 16)

            def buffer(u, i=0):
                if u >= 4:
                    sp.wait_ge(s_wL, 4 * i + (u - 3))
                return raw[:, u % 4]

            def load(u, i, src, waits=True):
                k = src.shape[1]
                dst = buffer(u, i) if waits else raw[:, u % 4]
                sp.dma_start(dst[:, 0:k * P].rearrange("p (k n) -> p k n", k=k), src
                             ).then_inc(s_raw[u % 4], 32)

            def cols(w, c0, k0=0, k=KD):
                c0 = c0 if isinstance(c0, int) else sp.snap(c0)
                return w[0].rearrange("(k p) n -> p k n", p=P)[:, k0:k0 + k, bass.ds(c0, P)]

            for r in range(4):
                load(r, 0, cols(w_f1i, (r // 2) * P + (r % 2) * DFF))
            with sp.Fori(1, KF // 2) as i:
                for r in range(4):
                    src = cols(w_f1i, i * (2 * P) + (r // 2) * P + (r % 2) * DFF)
                    sp.wait_ge(s_wL, 4 * i + (r - 3))
                    sp.dma_start(raw[:, r].rearrange("p (k n) -> p k n", k=KD), src).then_inc(s_raw[r], 32)
            with sp.Fori(0, KD) as i:
                for r, (k0, k) in enumerate(FO_SPLIT):
                    load(U_F1O + r, i, cols(w_f1o, i * P, k0, k))
            for r, c0 in enumerate((C_SK, C_SV, C_GLR)):
                load(U_MIX + r, 0, cols(w_in, c0))
            sp.wait_ge(s_unit, U_F1O + 4 * KD)
            sp.dma_start(gup[:, :], w_gup[0]).then_inc(s_mixin, 16)
            sp.dma_start(rden, sinks.broadcast_to([P, SH])).then_inc(s_mixin, 16)
            with sp.Fori(0, 2) as i:
                for r in range(4):
                    srcs = [w_in[0].rearrange("(k p) n -> p k n", p=P)[:, :, bass.ds(sp.snap(
                        i * (4 * SHD) + (C_SQ + g * SG * SHD + r * SHD)), SHD)] for g in range(SKV)]
                    dst = buffer(U_SQ + r, i).rearrange("p (k g n) -> p k g n", k=KD, g=SKV)
                    for g in range(SKV):
                        sp.dma_start(dst[:, :, g], srcs[g]).then_inc(s_raw[(U_SQ + r) % 4], 16)
            with sp.Fori(0, TB) as i:
                load(U_SA, i, cols(w_in, i * (2 * P) + C_GV))
                load(U_SA + 1, i, cols(w_in, i * (2 * P) + (C_GV + P)))
                load(U_SA + 2, i, cols(w_in, i * P + C_GQ))
                load(U_SA + 3, i, cols(w_in, i * P + C_GK))
            def branch_swa(u, i, c0):
                c0 = sp.snap(c0)
                dst = buffer(u, i).rearrange("p (k n) -> p k n", k=KD)
                src = w_bswa[0].rearrange("(g j n) c -> g n j c", g=SKV, n=SHD)
                for g in (1, 0):
                    sp.dma_start(dst[g * SHD:(g + 1) * SHD], src[g][:, :, bass.ds(c0, P)]
                                 ).then_inc(s_raw[u % 4], 16)

            with sp.Fori(0, TB) as i:
                load(U_GA, i, cols(w_in, i * (2 * P) + C_GB))
                load(U_GA + 1, i, cols(w_in, i * (2 * P) + (C_GB + P)))
                branch_swa(U_GA + 2, i, i * (2 * P))
                branch_swa(U_GA + 3, i, i * (2 * P) + P)
            for u0, w, c0 in ((U_GR, w_in, C_GR), (U_A, w_in, C_GA), (U_BR, w_bgla, 0)):
                with sp.Fori(0, 2) as i:
                    for r in range(4):
                        load(u0 + r, i, cols(w, i * (4 * P) + (c0 + r * P)))
            with sp.Fori(0, 2) as i:
                for r in range(4):
                    load(U_WO + r, i, cols(w_out, i * (4 * P) + r * P))
            with sp.Fori(0, KF // 2) as i:
                for r in range(4):
                    load(U_F2I + r, i, cols(w_f2i, i * (2 * P) + (r // 2) * P + (r % 2) * DFF))
            with sp.Fori(0, KD) as i:
                for r, (k0, k) in enumerate(FO_SPLIT):
                    load(U_F2O + r, i, cols(w_f2o, i * P, k0, k))
            yt = Tally(s_trd)
            yt.add(N_TRD)
            for b in range(TB + 1):
                sp.wait_ge(s_trd, yt.add(2))
                if b < TB:
                    sp.dma_start(y_p[0, b * P:(b + 1) * P], xtok[:, b, :]).then_inc(s_store, 16)
                else:
                    sp.dma_start(y_s[0], xtok[0:NS, TB, :]).then_inc(s_store, 16)
            sp.wait_ge(s_store, 16 * (6 + 1 + TB + 1))

        @block.gpsimd
        def _(pool):
            def low(n, s):
                pool.wait_ge(s_wH, n)
                pool.tensor_tensor(wL[:, s], raw[:, s], wH[:, s].bitcast(F32), ALU.subtract).then_inc(s_wL, 1)

            with pool.Fori(0, U_END // 4) as i:
                for s in range(4):
                    low(4 * i + (s + 1), s)
            for s in range(U_END % 4):
                low(U_END // 4 * 4 + s + 1, s)

        @block.tensor
        def _(pe):
            unit, blocks = Tally(s_unit), Tally(s_slot)
            inp, ss, trd = Tally(s_in), Tally(s_ss), Tally(s_trd)

            def mm(out, lhsT, rhs, start=True, stop=True):
                return pe.matmul(out, lhsT, rhs, start=start, stop=stop, skip_group_check=True)

            def chunk(s, w, b, xH, xL, c, last):
                w = slice(w * P, (w + 1) * P)
                for n, (wt, x) in enumerate(((wH, xH), (wH, xL), (wL, xH))):
                    for h in range(2):
                        m = mm(slot[b][:, h, 0:TH], wt[:, s, w], x[:, c, h * TH:(h + 1) * TH],
                               start=(c == 0 and n == 0), stop=(last and n == 2))
                return m

            def run(s, b, xH, xL, k0=0, k=KD, last=True, wait_in=None):
                pe.wait_ge(s_wL, unit.add())
                for c in range(k0, k0 + k):
                    if wait_in is not None:
                        pe.wait_ge(s_in, wait_in + c + 1)
                    m = chunk(s, c - k0, b, xH, xL, c, last and c == k0 + k - 1)
                m.then_inc(s_unit, 1)

            def slot_free():
                pe.wait_ge(s_slot, blocks.add() - 2)

            def ffn_in(u0, b0, in0):
                for r in range(4):
                    if u0 + r < 2:
                        continue
                    slot_free()
                    run((u0 + r) % 4, (b0 + r) % 2, hH, hL, wait_in=in0 if r == 0 else None)
                    if r == 0:
                        norm()
                with Loop(pe, KF // 2 - 1, (unit, 4), (blocks, 4)):
                    for r in range(4):
                        slot_free()
                        run((u0 + r) % 4, (b0 + r) % 2, hH, hL)

            def ffn_out(u0, b0, in0):
                with Loop(pe, KD // 2, (unit, 8), (blocks, 2)):
                    for b in range(2):
                        slot_free()
                        for r, (k0, k) in enumerate(FO_SPLIT):
                            if b == 0:
                                pe.wait_ge(s_in, in0 + k0 + k)
                            run((u0 + r) % 4, (b0 + b) % 2, hidH, hidL, k0, k, last=(r == 3))

            def norm():
                pe.wait_ge(s_ss, ss.add())
                for h in range(2):
                    m = mm(side[:, h, 0:TH], ones, acc[:, h * TH:(h + 1) * TH])
                m.then_inc(s_ssum, 1)

            pe.wait_ge(s_table, 16)
            pe.wait_ge(s_tokens, 16 * 8)
            pe.transpose(side[:, 2, 0:NG], vrow[:, :], ident[0:NG, 0:NG]).then_inc(s_tr, 1)
            for k in range(KD):
                m = pe.transpose(side[:, 0, k * NS:(k + 1) * NS], xtok[0:NS, TB, k * P:(k + 1) * P],
                                 ident[0:NS, 0:NS])
            m.then_inc(s_tr, 1)

            def turn_tokens(k):
                pe.wait_ge(s_trd, k + 1)
                for b in range(TB):
                    m = pe.transpose(side[:, 2 + k % 2, b * P:(b + 1) * P], xtok[:, b, k * P:(k + 1) * P], ident)
                m.then_inc(s_tr, 1)

            turn_tokens(0)
            for k in range(KD):
                if k + 1 < KD:
                    turn_tokens(k + 1)
                pe.wait_ge(s_in, k + 1)
                for u in range(2):
                    if k == 0:
                        pe.wait_ge(s_wL, unit.add())
                        blocks.add()
                    m = chunk(u, k, u, hH, hL, k, k == KD - 1)
                    if k == KD - 1:
                        m.then_inc(s_unit, 1)
                pe.wait_ge(s_trd, 2)
                pe.wait_ge(s_sq, k + 1)
                for h in range(2):
                    m = mm(side[:, h, 0:TH], ones, (sq, acc)[k % 2][:, h * TH:(h + 1) * TH], start=(k == 0),
                           stop=(k == KD - 1))
                m.then_inc(s_ssum if k == KD - 1 else s_squ, 1)
            ffn_in(U_F1I, 0, 0)
            ffn_out(U_F1O, 0, KD)

            IN = KD + KF
            for r in range(3):
                slot_free()
                run((U_MIX + r) % 4, r % 2, hH, hL, wait_in=IN if r == 0 else None)
                if r == 0:
                    norm()
            pe.wait_ge(s_slot, blocks.value())
            for b in range(TB + 1):
                n = P if b < TB else NS
                m = pe.transpose(side[0:n, 2 + b // TB, (b % TB) * P:(b % TB + 1) * P],
                                 vtmp[:, 0, b * P:b * P + n], ident)
            pe.transpose(side[:, 3, P:2 * P], kT[:, NP:NP + P], ident)
            pe.transpose(side[0:NS, 3, 2 * P:3 * P], kT[:, P + NP:P + T], ident).then_inc(s_tr, 1)
            with Loop(pe, 2, (unit, 4), (blocks, 4)):
                for r in range(4):
                    slot_free()
                    run((U_SQ + r) % 4, (3 + r) % 2, hH, hL)

            qk, nm, pr, pts_, ot, oc = (Tally(x) for x in (s_qk, s_nm, s_pr, s_pts, s_ot, s_oc))
            pe.wait_ge(s_trd, KD + 3)

            def swa(n, tiles, fill=lambda point: None):
                keys = sum(m for m, _ in tiles)

                def scores(j):
                    if j >= 2:
                        pe.wait_ge(s_nm, nm.value() + (j - 1))
                    mm(side[0:n, j % 2, :].rearrange("p (g k) -> p g k", g=SKV)[:, :, 0:keys],
                       qst[:, j, 0:n], kst[:, :, 0:keys]).then_inc(s_sc, 1)

                def turn(j):
                    pe.wait_ge(s_pr, pr.add())
                    pe.wait_ge(s_pts, pts_.value() + (1 if j else 0))
                    pe.wait_ge(s_oc, oc.value())
                    for g in range(SKV):
                        k0 = 0
                        for i, (m_, _) in enumerate(tiles):
                            m = pe.transpose(side[0:m_, 2, (2 * g + i) * P:(2 * g + i) * P + n],
                                             probs[0:n, j % 2, g, k0:k0 + m_], ident[0:n, 0:n])
                            k0 += m_
                    m.then_inc(s_pt, 1)

                def values(j):
                    pe.wait_ge(s_pts, pts_.add())
                    if j % 4 == 0:
                        pe.wait_ge(s_ot, ot.value())
                    for g in range(SKV):
                        for i, (m_, v) in enumerate(tiles):
                            c = ((j % 4) * SKV + g) * SHD
                            m = mm(side[0:n, 3, c:c + SHD], pts[0:m_, j % 2, g, i, 0:n],
                                   v[:, g * SHD:(g + 1) * SHD], start=(i == 0), stop=(i == len(tiles) - 1))
                    if j % 4 == 3:
                        m.then_inc(s_av, 1)

                def out(q):
                    pe.wait_ge(s_ot, ot.add())
                    for j in range(4):
                        m = pe.transpose(side[:, 2, j * P:j * P + n],
                                         otok[0:n, 2 * j:2 * j + 2, :].rearrange("p a b -> p (a b)"),
                                         ident[0:n, 0:n])
                    m.then_inc(s_ott, 1)
                    oc.add()

                fill(0)
                pe.wait_ge(s_qk, qk.add())
                scores(0)
                point = 1
                for j in range(SG):
                    if j + 1 < SG:
                        scores(j + 1)
                    fill(point)
                    point += 1
                    if j == 5:
                        out(0)
                        fill(point)
                        point += 1
                    turn(j)
                    if j:
                        values(j - 1)
                fill(point)
                values(SG - 1)
                fill(point + 1)
                out(1)
                fill(point + 2)
                nm.add(SG)

            pe.wait_ge(s_mixin, 32)
            with Loop(pe, TB, (qk, 1), (nm, SG), (pr, SG), (pts_, SG), (ot, 2), (oc, 2), (unit, 4),
                      (blocks, 7)) as i:
                def turned_values(r, wait):
                    b = r
                    pe.wait_ge(s_slot, blocks.value() + wait)
                    for t in range(TB + 1):
                        n = P if t < TB else NS
                        m = pe.transpose(slot[b][0:n, t // TB, (t % TB) * P:(t % TB + 1) * P],
                                         vtmp[:, r, t * P:t * P + n], ident)
                    m.then_inc(s_tr, 1)

                def fill(point):
                    for r, c in SWA_FILL[point]:
                        if c == 0:
                            pe.wait_ge(s_wL, unit.value() + (r + 1))
                            pe.wait_ge(s_slot, blocks.value() + (-1, 1, 2, 4)[r])
                        m = chunk((U_SA + r) % 4, c, (1, 0, 1, 0)[r], hH, hL, c, c == KD - 1)
                        if c == KD - 1:
                            m.then_inc(s_unit, 1)
                    if point == 1:
                        pe.wait_ge(s_slot, blocks.value())
                        for h in range(2):
                            m = mm(slot[0][:, h, 0:TH], gups[:, :],
                                   glr[:, h * TH:(h + 1) * TH])
                        m.then_inc(s_lg, 1)
                    if point == 7:
                        turned_values(0, 3)
                    if point == 10:
                        turned_values(1, 5)

                swa(P, [(P, vtok[:, bass.ds(i, 1), :].rearrange("p a d -> p (a d)")),
                        (P, vtok[:, bass.ds(i + 1, 1), :].rearrange("p a d -> p (a d)"))], fill)
                unit.add(4)
                blocks.add(7)
            pe.wait_ge(s_cache, 32)
            pe.wait_ge(s_oc, oc.value())
            pe.transpose(side[:, 2, 0:P], ckc[:, :], ident).then_inc(s_tr, 1)
            swa(NS, [(P, cvc[:, :]), (NS, vtok[0:NS, TB + 1, :])])
            pe.wait_ge(s_oc, oc.value())

            gdi, gkd = Tally(s_gdi), Tally(s_gkd)
            gx, gA, gn, gf = (Tally(x) for x in (s_gx, s_gA, s_gn, s_gf))

            def gla(n, v, fill, ready=None):
                lv0 = NLV - n.bit_length() + 1
                fill(0)
                if ready is not None:
                    pe.wait_ge(*ready)
                pe.wait_ge(s_gx, gx.add())

                for h in range(GH):
                    mm(side[0:n, 0, h * P:h * P + n], kg[:, h, 0:n], qg[:, h, 0:n])
                for h in range(GH):
                    m = pe.transpose(side[0:n, 1, h * P:(h + 1) * P], kdec[:, h, 0:n], ident)
                m.then_inc(s_g4, 1)

                def levels(h):
                    if h == 0:
                        pe.wait_ge(s_gdi, gdi.add())
                    if h == 1:
                        pe.wait_ge(s_gkd, gkd.add())
                    for lv in range(lv0, NLV):
                        f = (P >> lv) // 2
                        m = mm(side[0:n, h % 2, lv * 64:lv * 64 + n // 2], lev[:, lv, h, 0:n],
                               lev[:, lv, h, 0:n].rearrange("p (a t f) -> p a t f", t=2, f=f)[:, :, 1, :])
                    m.then_inc(s_ga, 1)

                levels(0)
                levels(1)
                for h in range(GH):
                    fill(2 * h + 1)
                    pe.wait_ge(s_gA, gA.add())
                    vh = v[:, h * GDV:(h + 1) * GDV]
                    mm(side[0:n, 2, 0:GDV], A[0:n, h, 0:n], vh, stop=False)
                    mm(side[0:n, 2, 0:GDV], qeb[:, h, 0:n], state[:, h, :], start=False)
                    mm(side[:, 2, GDV:2 * GDV], kdT[0:n, h, :], vh).then_inc(s_go, 1)
                    if h + 2 < GH:
                        levels(h + 2)
                    fill(2 * h + 2)
                    pe.wait_ge(s_gn, gn.add())
                    if h:
                        pe.wait_ge(s_gf, gf.add())
                    for e in range(2):
                        m = pe.transpose(side[:, 3, e * P:e * P + n], osb[0:n, e * P:(e + 1) * P],
                                         ident[0:n, 0:n])
                    m.then_inc(s_gt, 1)
                gf.add()

            def beside(u0, table):
                def fill(point):
                    for r, c in table[point]:
                        xH, xL = hH, hL
                        if u0 == U_GA and r >= 2:
                            xH, xL = osH, osL
                            if r == 2 and c == 0:
                                pe.wait_ge(s_in, IN + 2 * KD)
                        if c == 0:
                            pe.wait_ge(s_wL, unit.value() + (r + 1))
                            pe.wait_ge(s_slot, blocks.value() + (r - 1))
                        m = chunk((u0 + r) % 4, c, (1 + r) % 2, xH, xL, c, c == KD - 1)
                        if c == KD - 1:
                            m.then_inc(s_unit, 1)
                return fill

            with Loop(pe, TB, (gx, 1), (gdi, 1), (gkd, 1), (gA, GH), (gn, GH), (gf, GH), (unit, 4), (blocks, 4)) as i:
                gla(P, gv[:, bass.ds(i, 1), :].rearrange("p a d -> p (a d)"), beside(U_GA, GLA_FILL))
                unit.add(4)
                blocks.add(4)
            gla(NS, gv[0:NS, TB, :], beside(U_GR, GLA_SAMPLE_FILL), ready=(s_state, 16))
            unit.add(FREED)
            blocks.add(FREED)
            for r in range(FREED, KD):
                slot_free()
                run((U_GR + r) % 4, (1 + r) % 2, hH, hL)

            for u0, xH, xL, ready in ((U_A, hH, hL, None), (U_BR, ogH, ogL, IN + 3 * KD)):
                if ready is not None:
                    pe.wait_ge(s_in, ready)
                with Loop(pe, 2, (unit, 4), (blocks, 4)):
                    for r in range(4):
                        slot_free()
                        run((u0 + r) % 4, (1 + r) % 2, xH, xL)
            pe.wait_ge(s_in, IN + 4 * KD)
            with Loop(pe, 2, (unit, 4), (blocks, 4)):
                for r in range(4):
                    slot_free()
                    run((U_WO + r) % 4, (1 + r) % 2, mH, mL)
            ffn_in(U_F2I, 1, IN + 4 * KD)
            ffn_out(U_F2O, 1, IN + 5 * KD)
            norm()
            tr = Tally(s_trd)
            tr.add(N_TRD)
            for b in range(TB + 1):
                n = P if b < TB else NS
                for q in range(2):
                    g = 2 * b + q
                    if g == 0:
                        pe.wait_ge(s_ht, KD)
                    if g >= 2:
                        pe.wait_ge(s_trd, tr.value() + g - 1)
                    for k in range(4):
                        m = pe.transpose(side[0:n, g % 2, k * P:(k + 1) * P],
                                         xT[:, 4 * q + k, b * P:b * P + n], ident)
                    m.then_inc(s_tr, 1)

        @block.scalar
        def _(act):
            chain, slots, units = Tally(s_act), Tally(s_slot), Tally(s_unit)

            def link(ins):
                ins.then_inc(s_act, 1)
                act.wait_ge(s_act, chain.add())

            def split(u, i=0):
                if u >= U_END and isinstance(i, int):
                    return
                act.wait_ge(s_raw[u % 4], 32 * i + 32 * (u // 4 + 1))
                if u >= 4:
                    act.wait_ge(s_unit, 4 * i + (u - 3))
                act.activation(wH[:, u % 4], raw[:, u % 4], ACT.Copy).then_inc(s_wH, 1)

            def ffn_in(u0, n):
                def tanh_of_gate():
                    act.wait_ge(s_slot, slots.add())
                    act.activation(ft[:, :], fg[:, :], ACT.Tanh, scale=0.5).then_inc(s_tanh, 1)
                    slots.add()

                for r in range(4):
                    split(u0 + r + 2)
                    if r == 0:
                        norm(n)
                    if r % 2 == 0:
                        tanh_of_gate()
                with Loop(act, KF // 2 - 1, (slots, 4)) as i:
                    for r in range(4):
                        split(u0 + 4 + r + 2, i)
                        if r % 2 == 0:
                            tanh_of_gate()

            def ffn_out(u0, last=False):
                with act.Fori(0, KD - 1) as i:
                    for r in range(4):
                        split(u0 + r + 2, i)
                for r in range(4):
                    split(u0 + 4 * (KD - 1) + r + 2)
                slots.add(KD)

            def norm(n):
                act.preload_act_table_set("natural_log_exp_and_others")
                act.wait_ge(s_ssum, n + 1)
                link(act.activation(two(rstd[:, :]), side[:, 0:2, 0:TH], ACT.Ln, scale=1.0 / D, bias=eps))
                act.activation(rstd[:, :], rstd[:, :], ACT.Exp, scale=-0.5).then_inc(s_rstd, 1)

            act.wait_ge(s_table, 16)
            split(0)
            split(1)
            for k in range(KD):
                act.wait_ge(s_trd, k + 3)
                if k >= 2:
                    act.wait_ge(s_squ, k - 1)
                act.activation((sq, acc)[k % 2][:, :], xT[:, k], ACT.Square).then_inc(s_sq, 1)
            ffn_in(U_F1I, 0)
            ffn_out(U_F1O)
            for r in range(3):
                split(U_MIX + r + 2)
                if r == 0:
                    norm(1)
            act.wait_ge(s_ss, 1)
            act.dma_start(xsave, xT[:, :, :].rearrange("p k t -> p (k t)")).then_inc(s_xsave, 16)
            with act.Fori(0, 2) as i:
                for r in range(4):
                    split(U_SQ + r + 2, i)
            act.wait_ge(s_ktok, 1)
            act.dma_start(ck_p[0, 0].rearrange("t h d -> t (h d)"), ktok[:, 0, :]).then_inc(s_store, 16)
            act.dma_start(cv_p[0, 0].rearrange("t h d -> t (h d)"), vtok[:, TB, :]).then_inc(s_store, 16)
            for new, old, rows in ((ck_s, cache_k, ktok[0:NS, 1, :]), (cv_s, cache_v, vtok[0:NS, TB + 1, :])):
                act.dma_start(new[0, 0, WIN - NS:].rearrange("t h d -> t (h d)"), rows).then_inc(s_store, 16)
                act.dma_start(new[0, 0, 0:WIN - NS], old[0, 0, NS:]).then_inc(s_store, 16)
            act.dma_start(ckc[:, :], cache_k[0, 0].rearrange("t h d -> t (h d)")).then_inc(s_cache, 16)
            act.dma_start(cvc[:, :], cache_v[0, 0].rearrange("t h d -> t (h d)")).then_inc(s_cache, 16)

            nm, pt, esx = Tally(s_nm), Tally(s_pt), Tally(s_esx)
            slots.add(3 + SG)

            def swa(n, keys, beside=lambda j: None):
                for j in range(SG):
                    act.wait_ge(s_nm, nm.add())
                    if j >= 2 or keys != 2 * P:
                        act.wait_ge(s_pt, pt.value() + (j - 1))
                    for g in range(SKV):
                        c = 2 * j + g
                        m = act.activation(probs[0:n, j % 2, g, 0:keys], smax[0:n, j % 2, g, 0:keys], ACT.Exp,
                                           scale=SHD ** -0.5, bias=nmax[0:n, c:c + 1],
                                           accum_out=den[0:n, c:c + 1])
                    m.then_inc(s_pr, 1)
                    if j % 4 == 3:
                        act.wait_ge(s_esx, esx.add())
                        c = 8 * (j // 4)
                        act.activation(esum[0:n, c:c + 8], esum[0:n, c:c + 8], ACT.Exp).then_inc(s_es, 1)
                    beside(j)
                pt.add(SG)

            with Loop(act, TB, (nm, SG), (pt, SG), (esx, 2), (slots, 7), (chain, 2)) as i:
                split(U_SA + 2, i)

                def beside(j):
                    if j in (2, 4, 6):
                        split(U_SA + 2 + j // 2, i)
                    if j == 1:
                        act.wait_ge(s_slot, slots.add())
                        link(act.activation(la1[:, :], la2[:, :], ACT.Abs))
                        link(act.activation(la1[:, :], la1[:, :], ACT.Exp, scale=-1.0))
                        act.activation(la1[:, :], la1[:, :], ACT.Ln, bias=one).then_inc(s_sp, 1)

                swa(P, 2 * P, beside)
                slots.add(6)
            swa(NS, P + NS)

            act.wait_ge(s_oc, 2 * (TB + 1))
            for k in range(KD):
                act.activation(osH[:, k], qs[:, k], ACT.Copy).then_inc(s_inH, 1)

            gd, gs, g4 = Tally(s_gd), Tally(s_gs), Tally(s_g4)

            def gla(n, i=None):
                lv0 = NLV - n.bit_length() + 1
                if i is not None:
                    split(U_GA + 2, i)
                else:
                    split(U_GR + 2)
                    split(U_GR + 3)
                tok = bass.ds(i * P, P) if i is not None else slice(NP, T)
                act.activation(qg[:, :, 0:n], gq[:, :, tok], ACT.Copy)
                act.activation(kg[:, :, 0:n], gk[:, :, tok], ACT.Copy)
                act.activation(qeb[:, :, 0:n], gb[:, :, tok], ACT.Exp, scale=1.0 / GTAU).then_inc(s_gq, 1)
                for lv in range(lv0, NLV):
                    act.wait_ge(s_gd, gd.add())
                    act.activation(lev[:, lv, :, 0:n], lev[:, lv, :, 0:n], ACT.Exp, scale=1.0 / GTAU
                                   ).then_inc(s_ge, 1)
                act.wait_ge(s_gd, gd.add())
                act.activation(kdec[:, :, 0:n], kdec[:, :, 0:n], ACT.Exp, scale=1.0 / GTAU).then_inc(s_ge, 1)
                act.wait_ge(s_g4, g4.add())
                act.activation(kdT[0:n], side[0:n, 1, :].rearrange("p (h d) -> p h d", h=GH), ACT.Copy
                               ).then_inc(s_gkd, 1)
                for h in range(GH):
                    if i is not None and h == 0:
                        act.wait_ge(s_slot, slots.add(2))
                    act.wait_ge(s_gs, gs.add())
                    link(act.activation(gsq[0:n, :], side[0:n, 2, 0:GDV], ACT.Square, accum_out=ssq[0:n]))
                    link(act.activation(sln[0:n], ssq[0:n], ACT.Ln, scale=1.0 / GDV, bias=eps[0:n]))
                    act.activation(srs[0:n], sln[0:n], ACT.Exp, scale=-0.5).then_inc(s_gr, 1)
                    if i is None:
                        split(U_GR + 4 + h)
                    elif h < 3:
                        split(U_GA + 3 + h, i)
                    if i is not None and h == 0:
                        g = gB[:, bass.ds(2 * i, 2), :]
                        act.activation(g, g, ACT.Tanh, scale=0.5).then_inc(s_gbt, 1)
                        act.preload_act_table_set("natural_log_exp_and_others")

            with Loop(act, TB, (g4, 1), (gd, NLV + 1), (gs, GH), (slots, 4), (chain, 2 * GH)) as i:
                gla(P, i)
                slots.add(2)
            act.dma_start(sg_p[0, 0].rearrange("h d e -> d h e"), state[:, :, :]).then_inc(s_stout, 16)
            act.wait_ge(s_stout, 16)
            act.dma_start(state[:, :, :], state_gla[0, 0].rearrange("h d e -> d h e")).then_inc(s_state, 16)
            gla(NS)
            act.dma_start(sg_s[0, 0].rearrange("h d e -> d h e"), state[:, :, :]).then_inc(s_store, 16)

            slots.add(FREED)
            act.activation(t1[:, :], go[:, 0], ACT.Tanh, scale=0.5).then_inc(s_tanh, 1)
            for k in range(KD):
                act.wait_ge(s_og, k + 1)
                if k + 1 < KD:
                    act.activation(t1[:, :], go[:, k + 1], ACT.Tanh, scale=0.5).then_inc(s_tanh, 1)
                act.activation(ogH[:, k], mts[k % 2][:, :], ACT.Copy).then_inc(s_inH, 1)
                if k in (0, 1, 3, 5, 7):
                    split(U_A + (k + 1) // 2)

            slots.add(KD - FREED)
            for q in range(2):
                for r in range(4):
                    split(U_A + 5 + 4 * q + r)
                act.wait_ge(s_slot, slots.add(4))
                act.activation(tA[:, 4 * q:4 * q + 4], tA[:, 4 * q:4 * q + 4], ACT.Tanh, scale=0.5
                               ).then_inc(s_tanh, 1)

            IN = KD + KF
            slots.add(KD)
            merged = Tally(s_in)
            merged.add(IN + 3 * KD)
            with Loop(act, 2, (merged, 4)) as i:
                for r in range(4):
                    split(U_BR + 5 + r, i)
                    dst = xT[:, bass.ds(act.snap(4 * i + r), 1), :].rearrange("p k t -> p (k t)")
                    src = xsave[:, bass.ds(act.snap(i * (4 * T) + r * T), T)]
                    act.wait_ge(s_in, merged.add())
                    act.dma_start(dst, src).then_inc(s_xback, 16)
            for r in range(5):
                split(U_WO + 5 + r)
            slots.add(KD)
            ffn_in(U_F2I, 2)
            ffn_out(U_F2O)
            norm(3)

        @block.vector
        def _(dve):
            chain, slots, units = Tally(s_dve), Tally(s_slot), Tally(s_unit)
            inp, inH, tanh = Tally(s_in), Tally(s_inH), Tally(s_tanh)
            trd, tr = Tally(s_trd), Tally(s_tr)
            ssn = Tally(s_ss)

            def link(ins):
                ins.then_inc(s_dve, 1)
                dve.wait_ge(s_dve, chain.add())

            def row(t, j):
                return t[:, bass.ds(j, 1), :].rearrange("p a t -> p (a t)")

            def copy(dst, src):
                return dve.tensor_scalar(dst, src, 1.0, None, ALU.mult)

            def free(ins):
                ins.then_inc(s_slot, 1)
                slots.add()

            def split_in(x, k, gain):
                g = gains[:, bass.ds(k + gain, 1)]
                link(dve.tensor_scalar(row(hH, k), x, g, None, ALU.mult))
                dve.scalar_tensor_tensor(out=row(hL, k), in0=x, scalar=g, in1=row(hH, k).bitcast(F32), op0=ALU.mult,
                                         op1=ALU.subtract).then_inc(s_in, 1)
                inp.add()

            def ffn_in(b0, n):
                def pair(b, r, i, j):
                    g, u = slot_h[b], slot_h[1 - b]
                    dve.wait_ge(s_unit, units.value() + (r + 1))
                    free(dve.tensor_tensor(two(fg[:, :]), g, two(rstd[:, :]), ALU.mult))
                    dve.wait_ge(s_unit, units.value() + (r + 2))
                    dve.wait_ge(s_in, inp.value())
                    free(dve.tensor_tensor(two(fp[:, :]), u, two(rstd[:, :]), ALU.mult))
                    dve.wait_ge(s_tanh, tanh.add())
                    link(dve.scalar_tensor_tensor(out=fs[:, :], in0=ft[:, :], scalar=1.0, in1=fg[:, :],
                                                  op0=ALU.add, op1=ALU.mult))
                    dve.wait_ge(s_slot, slots.value())
                    link(dve.tensor_tensor(fp[:, :], fs[:, :], fp[:, :], ALU.mult))
                    hj = hidH[:, bass.ds(j, 1), :].rearrange("p a t -> p (a t)")
                    lj = hidL[:, bass.ds(j, 1), :].rearrange("p a t -> p (a t)")
                    link(copy(hj, fp[:, :]))
                    dve.tensor_tensor(lj, fp[:, :], hj.bitcast(F32), ALU.subtract).then_inc(s_in, 1)
                    inp.add()

                dve.wait_ge(s_rstd, n + 1)
                with Loop(dve, KF // 2, (tanh, 2), (slots, 4), (units, 4), (inp, 2), (chain, 6)) as i:
                    for q in range(2):
                        pair(b0, 2 * q, i, 2 * i + q)
                    units.add(4)

            def residual(u_per, b0, scale, gain=None):
                more = gain is not None
                link(dve.memset(acc[:, :], 0.0))
                with Loop(dve, KD // 2, (slots, 2), (units, 2 * u_per), (inp, 2 * more),
                          (chain, 4 + 2 * more)) as i:
                    for b in range(2):
                        dve.wait_ge(s_unit, units.add(u_per))
                        x = xT[:, bass.ds(2 * i + b, 1), :].rearrange("p a t -> p (a t)")
                        free(dve.scalar_tensor_tensor(out=two(x), in0=slot_h[(b0 + b) % 2], scalar=scale,
                                                      in1=two(x), op0=ALU.mult, op1=ALU.add))
                        dve.wait_ge(s_slot, slots.value())
                        if more:
                            split_in(x, 2 * i + b, gain)
                        link(dve.tensor_tensor(sq[:, :], x, x, ALU.mult))
                        link(dve.tensor_tensor(acc[:, :], acc[:, :], sq[:, :], ALU.add))
                dve.tensor_scalar(acc[:, :], acc[:, :], 1.0, None, ALU.mult).then_inc(s_ss, 1)
                ssn.add()
                dve.wait_ge(s_ss, ssn.value())

            dve.wait_ge(s_tr, tr.add())
            dve.tensor_copy(gains[:, 0:NG], side[:, 2, 0:NG]).then_inc(s_trd, 1)
            trd.add()
            dve.wait_ge(s_trd, trd.value())
            link(dve.tensor_scalar(sgain, gains[:, G_GLA:G_GLA + 2], 0.5, None, ALU.mult))
            dve.wait_ge(s_tr, tr.add())
            dve.tensor_copy(xT[:, :, NP:T], side[:, 0, 0:KD * NS].rearrange("p (k t) -> p k t", k=KD)
                            ).then_inc(s_trd, 1)
            trd.add()
            for k in range(KD):
                dve.wait_ge(s_tr, tr.add())
                dve.tensor_copy(xT[:, k, 0:NP], side[:, 2 + k % 2, :]).then_inc(s_trd, 1)
                dve.wait_ge(s_trd, trd.add())
                split_in(xT[:, k], k, G_FFN1)
            ffn_in(0, 0)
            residual(4, 0, 0.25, G_MIX)
            dve.wait_ge(s_rstd, 2)

            def block_done(b, dst, src_rows=P):
                dve.wait_ge(s_unit, units.add())
                free(dve.tensor_tensor(two(dst), slot_h[b][0:src_rows], two(rstd[0:src_rows, :]), ALU.mult))

            block_done(0, kT[:, P:P + T])
            block_done(1, vtmp[:, 0])
            block_done(0, glr[:, :], GRANK)
            dve.wait_ge(s_tr, tr.add())
            dve.memset(vtok[:, 0, :], 0.0)
            dve.memset(kT[:, 0:P], 0.0)
            dve.memset(kst[:, :, :], 0.0)
            for b in range(TB):
                dve.tensor_copy(masks[:, b], band)
            dve.tensor_copy(vtok[:, 1:TB + 1, :], side[:, 2, :].rearrange("p (b d) -> p b d", b=TB))
            dve.tensor_copy(vtok[0:NS, TB + 1, :], side[0:NS, 3, 0:P])
            dve.tensor_copy(ktok[:, 0, :], side[:, 3, P:2 * P])
            dve.tensor_copy(ktok[0:NS, 1, :], side[0:NS, 3, 2 * P:3 * P]).then_inc(s_trd, 1)
            dve.wait_ge(s_trd, trd.add())
            dve.memset(masks[:, 0, 0:P], MASKED)
            dve.wait_ge(s_mixin, 32)
            link(dve.tensor_copy(sink.rearrange("p (j g) -> p g j", g=SKV), rden.rearrange("p (g j) -> p g j", g=SKV)))
            dve.tensor_scalar(negsink, sink, -1.0, None, ALU.mult).then_inc(s_ktok, 1)

            with Loop(dve, 2, (slots, 4), (units, 4)) as i:
                for r in range(4):
                    block_done((3 + r) % 2, row(qs, 4 * i + r))
            sc, pr, pt, av, es, ott, pts_ = (Tally(x) for x in (s_sc, s_pr, s_pt, s_av, s_es, s_ott, s_pts))
            oc, qk, esx, otl = Tally(s_oc), Tally(s_qk), Tally(s_esx), Tally(s_ot)

            def swa(n, tiles, mask, t0, stage, beside=lambda j: None):
                keys = sum(tiles)
                stage()
                dve.wait_ge(s_qk, qk.add())

                def scores(j):
                    dve.wait_ge(s_sc, sc.add())
                    if j >= 2:
                        dve.wait_ge(s_pr, pr.value() + (j - 1))
                    c = slice(2 * j, 2 * j + 2)
                    masked = smax[0:n, j % 2, :, 0:keys]
                    link(dve.tensor_tensor(
                        masked, side[0:n, j % 2, :].rearrange("p (g k) -> p g k", g=SKV)[:, :, 0:keys],
                        mask.unsqueeze(1).broadcast_to([n, SKV, keys]), ALU.add))
                    link(dve.tensor_reduce(mx[0:n, c], masked, AX_X, ALU.max))
                    dve.scalar_tensor_tensor(out=nmax[0:n, c], in0=mx[0:n, c], scalar=-SHD ** -0.5,
                                             in1=negsink[0:n, c], op0=ALU.mult, op1=ALU.min).then_inc(s_nm, 1)
                    if j % 4 == 3:
                        c = slice(8 * (j // 4), 8 * (j // 4) + 8)
                        dve.wait_ge(s_nm, nmt.value() + (j + 1))
                        dve.tensor_tensor(esum[0:n, c], sink[0:n, c], nmax[0:n, c], ALU.add).then_inc(s_esx, 1)
                        esx.add()

                def turned(j):
                    dve.wait_ge(s_pt, pt.add())
                    src = side[:, 2, :].rearrange("p (g i q) -> p g i q", g=SKV, i=2)
                    if tiles == [P, P]:
                        m = dve.tensor_copy(pts[:, j % 2], src)
                    else:
                        for i, k in enumerate(tiles):
                            m = dve.tensor_copy(pts[0:k, j % 2, :, i, 0:n], src[0:k, :, i, 0:n])
                    m.then_inc(s_pts, 1)
                    pts_.add()

                def divide(q):
                    c = slice(8 * q, 8 * q + 8)
                    dve.wait_ge(s_es, es.add())
                    link(dve.tensor_tensor(rden[0:n, c], den[0:n, c], esum[0:n, c], ALU.add))
                    link(dve.reciprocal(rden[0:n, c], rden[0:n, c]))
                    dve.wait_ge(s_av, av.add())
                    dve.tensor_tensor(otok[0:n], side[0:n, 3, :].rearrange("p (a d) -> p a d", d=SHD),
                                      rden[0:n, c].unsqueeze(2).broadcast_to([n, 8, SHD]), ALU.mult
                                      ).then_inc(s_ot, 1)
                    otl.add()

                def output(q):
                    dve.wait_ge(s_ott, ott.add())
                    copy(qs[:, 4 * q:4 * q + 4, bass.ds(t0, n)],
                         side[:, 2, :].rearrange("p (j q) -> p j q", j=4)[:, :, 0:n]).then_inc(s_oc, 1)
                    oc.add()

                scores(0)
                for j in range(SG):
                    if j + 1 < SG:
                        scores(j + 1)
                    if j == 5:
                        output(0)
                    turned(j)
                    if j == 4:
                        divide(0)
                    beside(j)
                divide(1)
                output(1)
                beside(SG)
                pr.add(SG)
                nmt.add(SG)

            nmt = Tally(s_nm)

            def stage(t0, k0, keys):
                link(copy(qst[:, :, :], qs[:, :, bass.ds(t0, P)]))
                for g in range(SKV):
                    rows = slice(g * SHD, (g + 1) * SHD)
                    m = copy(kst[rows, g, 0:keys], kT[rows, bass.ds(k0, keys)])
                m.then_inc(s_qk, 1)

            def stage_block(i):
                dve.tensor_copy(gups[:, :], gup[:, bass.ds(i * GDK, GDK)])
                dve.tensor_copy(bgs[:, :], gains[:, bass.ds(i + G_BG, 1)])
                stage(i * P, i * P, 2 * P)

            dve.wait_ge(s_slot, slots.value())
            dve.wait_ge(s_ktok, 1)
            lg, sp = Tally(s_lg), Tally(s_sp)
            with Loop(dve, TB, (sc, SG), (pr, SG), (pt, SG), (av, 2), (es, 2), (ott, 2), (pts_, SG), (oc, 2),
                      (qk, 1), (esx, 2), (otl, 2), (nmt, SG), (lg, 1), (sp, 1), (tr, 2),
                      (slots, 7), (units, 4), (chain, 2 * SG + 7)) as i:
                def to_rows(r, b):
                    dve.wait_ge(s_tr, tr.add())
                    c = bass.ds(i * (2 * P) + r * P, P)
                    copy(gv[:, 0:TB, c], slot[b][:, 0, :].rearrange("p (b d) -> p b d", b=TB))
                    free(copy(gv[0:NS, TB, c], slot[b][0:NS, 1, 0:P]))

                def beside(j):
                    if j == 0:
                        dve.wait_ge(s_lg, lg.add())
                        free(dve.tensor_scalar(two(la2[:, :]), slot_h[0], bgs[:, :], None, ALU.add))
                    elif j == 1:
                        block_done(1, vtmp[:, 0])
                    elif j == 2:
                        dve.wait_ge(s_sp, sp.add())
                        link(dve.scalar_tensor_tensor(out=la2[:, :], in0=la2[:, :], scalar=0.0, in1=la1[:, :],
                                                      op0=ALU.min, op1=ALU.subtract))
                        link(dve.tensor_tensor_scan(row(gb, i), tab[:, K_RST:K_RST + T], la2[:, :], 0.0,
                                                    ALU.mult, ALU.add))
                    elif j == 4:
                        block_done(0, vtmp[:, 1])
                    elif j == 5:
                        to_rows(0, 0)
                    elif j == 7:
                        dve.wait_ge(s_unit, units.add())
                        free(dve.scalar_tensor_tensor(out=two(row(gqk, i)), in0=slot_h[1], scalar=GDK ** -0.5,
                                                      in1=two(rstd[:, :]), op0=ALU.mult, op1=ALU.mult))
                        to_rows(1, 1)
                    elif j == 8:
                        block_done(0, row(gqk, i + GH))

                swa(P, [P, P], row(masks, i), i * P, lambda: stage_block(i), beside)

            def stage_sample():
                dve.wait_ge(s_oc, oc.value())
                link(copy(qst[:, :, 0:NS], qs[:, :, NP:T]))
                dve.wait_ge(s_tr, tr.add())
                for g in range(SKV):
                    rows = slice(g * SHD, (g + 1) * SHD)
                    copy(kst[rows, g, P:P + NS], kT[rows, P + NP:P + T])
                    m = dve.tensor_copy(kst[rows, g, 0:P], side[rows, 2, 0:P])
                m.then_inc(s_qk, 1)

            swa(NS, [P, NS], band[0:NS, 0:P + NS], NP, stage_sample)
            dve.wait_ge(s_oc, oc.value())

            for k in range(KD):
                dve.wait_ge(s_inH, inH.add())
                dve.tensor_tensor(osL[:, k], qs[:, k], osH[:, k].bitcast(F32), ALU.subtract).then_inc(s_in, 1)
                inp.add()
            gbt = Tally(s_gbt)
            dve.wait_ge(s_store, 16 * 6)
            link(dve.memset(state[:, :, :], 0.0))
            ge, ga, go_, gr, gt, gA, gs, gn, gf = (Tally(x) for x in (s_ge, s_ga, s_go, s_gr, s_gt, s_gA, s_gs,
                                                                      s_gn, s_gf))
            gqt, g4 = Tally(s_gq), Tally(s_g4)

            def gla(n, t0, early, first, beside):
                lv0 = NLV - n.bit_length() + 1
                tok = bass.ds(t0, n)

                def nodes(x, f, t):
                    return x.rearrange("p h (a t f) -> p h a t f", t=2, f=f)[:, :, :, t, :]

                for lv in range(lv0, NLV):
                    f = (P >> lv) // 2
                    x, b = lev[:, lv, :, 0:n], gb[:, :, tok]
                    ref = nodes(b, f, 0)[:, :, :, f - 1:f].broadcast_to([P, GH, n // (2 * f), f])
                    dve.tensor_tensor(nodes(x, f, 0), ref, nodes(b, f, 0), ALU.subtract)
                    dve.tensor_tensor(nodes(x, f, 1), nodes(b, f, 1), ref, ALU.subtract).then_inc(s_gd, 1)
                dve.tensor_tensor(kdec[:, :, 0:n],
                                  gb[:, :, bass.ds(t0 + (n - 1), 1)].broadcast_to([P, GH, n]), gb[:, :, tok],
                                  ALU.subtract).then_inc(s_gd, 1)
                early()
                dve.wait_ge(s_gq, gqt.add())
                for lv in range(lv0, NLV):
                    dve.wait_ge(s_ge, ge.add())
                    f = (P >> lv) // 2
                    x = lev[:, lv, :, 0:n]
                    dve.tensor_tensor(nodes(x, f, 0), nodes(x, f, 0), nodes(kg[:, :, 0:n], f, 0), ALU.mult)
                    dve.tensor_tensor(nodes(x, f, 1), nodes(x, f, 1), nodes(qg[:, :, 0:n], f, 1), ALU.mult)
                dve.wait_ge(s_ge, ge.add())
                link(dve.tensor_copy(eL.unsqueeze(2), qeb[:, :, n - 1:n]))
                dve.tensor_tensor(qeb[:, :, 0:n], qeb[:, :, 0:n], qg[:, :, 0:n], ALU.mult)
                dve.tensor_tensor(kdec[:, :, 0:n], kdec[:, :, 0:n], kg[:, :, 0:n], ALU.mult).then_inc(s_gx, 1)
                first()

                dve.wait_ge(s_g4, g4.add())
                dve.tensor_tensor(A[0:n, :, 0:n], side[0:n, 0, :].rearrange("p (h c) -> p h c", h=GH)[:, :, 0:n],
                                  ident[0:n, 0:n].unsqueeze(1).broadcast_to([n, GH, n]), ALU.mult
                                  ).then_inc(s_gdi, 1)

                def attention(h):
                    dve.wait_ge(s_ga, ga.add())
                    link(dve.tensor_tensor(
                        alev[0:n, lv0:NLV, 0:n // 2],
                        side[0:n, h % 2, 0:NLV * 64].rearrange("p (l c) -> p l c", l=NLV)[:, lv0:NLV, 0:n // 2],
                        tab[0:n, K_LM:K_LM + NLV * 64].rearrange("p (l c) -> p l c", l=NLV)[:, lv0:NLV, 0:n // 2],
                        ALU.mult))
                    for lv in range(lv0, NLV):
                        f = (P >> lv) // 2
                        late = A[0:n, h, 0:n].rearrange("p (a t f) -> p a t f", t=2, f=f)[:, :, 1, :]
                        m = dve.tensor_tensor(late, late, alev[0:n, lv, 0:n // 2].rearrange("p (a f) -> p a f", f=f),
                                              ALU.add)
                        if lv + 1 < NLV:
                            link(m)
                    m.then_inc(s_gA, 1)
                    gA.add()

                attention(0)
                for h in range(GH):
                    beside(h)
                    dve.wait_ge(s_go, go_.add())
                    dve.scalar_tensor_tensor(out=state[:, h, :], in0=state[:, h, :], scalar=eL[:, h:h + 1],
                                             in1=side[:, 2, GDV:2 * GDV], op0=ALU.mult, op1=ALU.add
                                             ).then_inc(s_gs, 1)
                    gs.add()
                    if h + 1 < GH:
                        attention(h + 1)
                    dve.wait_ge(s_gr, gr.add())
                    dve.tensor_scalar(osb[0:n, :], side[0:n, 2, 0:GDV], srs[0:n], None, ALU.mult
                                      ).then_inc(s_gn, 1)
                    dve.wait_ge(s_gt, gt.add())
                    for e in range(2):
                        m = dve.tensor_scalar(gqk[:, 2 * h + e, tok], side[:, 3, e * P:e * P + n],
                                              sgain[:, e:e + 1], None, ALU.mult)
                    m.then_inc(s_gf, 1)
                    gf.add()
                beside(GH)
                dve.wait_ge(s_gs, gs.value())
                dve.wait_ge(s_gf, gf.value())

            dve.wait_ge(s_xsave, 16)
            with Loop(dve, TB, (gbt, 1), (ge, NLV + 1), (ga, GH), (go_, GH), (gr, GH), (gt, GH), (gA, GH), (gs, GH),
                      (gf, GH), (slots, 4), (units, 4), (gqt, 1), (g4, 1), (chain, 1 + GH * NLV)) as i:
                def branch(b, j):
                    dve.wait_ge(s_unit, units.add())
                    free(dve.scalar_tensor_tensor(out=two(row(gB, j)), in0=two(row(gB, j)), scalar=1.0,
                                                  in1=slot_h[b], op0=ALU.add, op1=ALU.mult))

                def beside(h):
                    if h == 3:
                        dve.wait_ge(s_gbt, gbt.add())
                        branch(1, 2 * i)
                    elif h == GH:
                        branch(0, 2 * i + 1)

                gla(P, i * P, lambda: block_done(1, row(gB, 2 * i)), lambda: block_done(0, row(gB, 2 * i + 1)),
                    beside)

            def output_gate(k):
                block_done((1 + k) % 2, go[:, k])

            dve.wait_ge(s_state, 16)
            gla(NS, NP, lambda: output_gate(0), lambda: output_gate(1), lambda h: output_gate(h + 1) if h else None)

            def low(k):
                dve.wait_ge(s_inH, inH.add())
                dve.tensor_tensor(ogL[:, k], mts[k % 2][:, :], ogH[:, k].bitcast(F32), ALU.subtract
                                  ).then_inc(s_in, 1)
                inp.add()

            for k in range(KD):
                if k in (2, 4):
                    output_gate(FREED + k // 2 - 1)
                dve.wait_ge(s_tanh, tanh.add())
                link(dve.scalar_tensor_tensor(out=t2[:, :], in0=t1[:, :], scalar=1.0, in1=go[:, k],
                                              op0=ALU.add, op1=ALU.mult))
                dve.wait_ge(s_in, inp.value())
                dve.tensor_tensor(mts[k % 2][:, :], t2[:, :], gqk[:, k], ALU.mult).then_inc(s_og, 1)
                if k:
                    low(k - 1)
            low(KD - 1)

            with Loop(dve, 2, (slots, 4), (units, 4)) as i:
                for r in range(4):
                    block_done((1 + r) % 2, row(tA, 4 * i + r))
            with Loop(dve, 2, (tanh, 1), (slots, 4), (units, 4), (chain, 8), (inp, 4)) as i:
                dve.wait_ge(s_tanh, tanh.add())
                for r in range(4):
                    dve.wait_ge(s_unit, units.add())
                    free(dve.scalar_tensor_tensor(out=two(mA[:, :]), in0=two(row(tA, 4 * i + r)), scalar=1.0,
                                                  in1=slot_h[(1 + r) % 2], op0=ALU.add, op1=ALU.mult))
                    dve.wait_ge(s_slot, slots.value())
                    dve.wait_ge(s_in, inp.value())
                    link(dve.tensor_tensor(mB[:, :], mA[:, :], row(gB, 4 * i + r), ALU.add))
                    link(copy(row(mH, 4 * i + r), mB[:, :]))
                    dve.tensor_tensor(row(mL, 4 * i + r), mB[:, :], row(mH, 4 * i + r).bitcast(F32), ALU.subtract
                                      ).then_inc(s_in, 1)
                    inp.add()
            dve.wait_ge(s_xback, 16 * KD)
            residual(1, 1, 0.5, G_FFN2)
            ffn_in(1, 2)
            residual(4, 1, 0.25)

            dve.wait_ge(s_rstd, 4)
            for k in range(KD):
                m = dve.scalar_tensor_tensor(out=xT[:, k], in0=xT[:, k], scalar=gains[:, G_FIN + k:G_FIN + k + 1],
                                             in1=rstd[:, :], op0=ALU.mult, op1=ALU.mult).then_inc(s_ht, 1)
            for b in range(TB + 1):
                n = P if b < TB else NS
                for q in range(2):
                    dve.wait_ge(s_tr, tr.add())
                    dve.tensor_copy(xtok[0:n, b, q * 512:(q + 1) * 512], side[0:n, (2 * b + q) % 2, :]
                                    ).then_inc(s_trd, 1)


_INS = ["x_prompt", "x_sample", "state_gla", "cache_swa_k", "cache_swa_v", "norm_ffn1", "w_ffn1_in", "w_ffn1_out",
        "norm_mix", "w_in", "w_gla_gate_up", "b_gla_gate", "gla_norm", "swa_sinks", "w_branch_gla",
        "w_branch_swa", "w_out", "norm_ffn2", "w_ffn2_in", "w_ffn2_out", "norm_final"]
_OUTS = [(1, NP, D), (1, NS, D), (1, 1, GH, GDK, GDV), (1, 1, WIN, SKV, SHD), (1, 1, WIN, SKV, SHD),
         (1, 1, GH, GDK, GDV), (1, 1, WIN, SKV, SHD), (1, 1, WIN, SKV, SHD)]


def kernel(**inputs):
    import concourse.bacc as bacc
    from concourse.bass_utils import run_bass_kernel_spmd

    nc = bacc.Bacc("TRN2", target_bir_lowering=False, num_devices=1, dynamic_dma_scratch_size=1024)
    arrays, args = {}, []
    for name, a in [(n, inputs[n]) for n in _INS] + [("table", constants())]:
        a = np.ascontiguousarray(a)
        arrays[f"in_{name}"] = a
        args.append(nc.dram_tensor(f"in_{name}", a.shape, mybir.dt.from_np(a.dtype), kind="ExternalInput").ap())
    outs = [nc.dram_tensor(f"out_{i}", shape, F32, kind="ExternalOutput").ap() for i, shape in enumerate(_OUTS)]
    build(nc, args, outs)
    r = run_bass_kernel_spmd(nc, [arrays], core_ids=[0])
    return tuple(r.results[0][f"out_{i}"] for i in range(len(_OUTS)))
```
